# Optimizing a Trainium2 kernel written in Bass

```python
import math
import jax, jax.numpy as jnp
from jax import lax
import numpy as np

D_MODEL = 2048
BATCH = 1
SEQ = 256
DEPTH = 1

M_HEADS = 4
M_HEAD_DIM = 256
M_WIDTH = M_HEADS * M_HEAD_DIM
M_CHUNK = 64
M_CONV = 4
A_HEADS = 8
A_HEAD_DIM = 128
A_WIDTH = A_HEADS * A_HEAD_DIM
MOBA_BLOCK = 256
MOBA_TOPK = 3
Q_CHUNK = 16
REL_BUCKETS = 32
REL_MAX_DIST = 128
N_GROUPS = 4
EXP_PER_GROUP = 8
N_EXPERTS = N_GROUPS * EXP_PER_GROUP
TOP_K_IN_GROUP = 2
D_FF_EXPERT = 256
N_BRANCH = 2
RMS_EPS = 1e-6
LN_EPS = 1e-5
IN_COLS = 4 * M_WIDTH + 2 * M_HEADS + 3 * A_WIDTH + N_BRANCH * D_MODEL

kernel_name = 'hybrid_mlstm_moba_hmoe'

def _split_cols(z):
    sizes = (M_WIDTH,) * 4 + (M_HEADS,) * 2 + (A_WIDTH,) * 3 + (D_MODEL,) * N_BRANCH
    idx, acc = [], 0
    for s in sizes[:-1]:
        acc += s
        idx.append(acc)
    return jnp.split(z, idx, axis=-1)

def rms_norm(x, g):
    xf = x.astype(jnp.float32)
    y = xf * lax.rsqrt(jnp.mean(xf * xf, axis=-1, keepdims=True) + RMS_EPS)
    return (y * g.astype(jnp.float32)).astype(x.dtype)

def causal_dwconv(x, w):
    c = x.shape[-1]
    return lax.conv_general_dilated(x, w[:, None, :], window_strides=(1,),
                                    padding=[(M_CONV - 1, 0)],
                                    dimension_numbers=('NWC', 'WIO', 'NWC'),
                                    feature_group_count=c)

def rel_bucket(n):
    n = jnp.maximum(n, 0)
    max_exact = REL_BUCKETS // 2
    nf = jnp.maximum(n, 1).astype(jnp.float32)
    large = max_exact + (jnp.log(nf / max_exact) / math.log(REL_MAX_DIST / max_exact)
                         * (REL_BUCKETS - max_exact)).astype(jnp.int32)
    large = jnp.minimum(large, REL_BUCKETS - 1)
    return jnp.where(n < max_exact, n, large)

def mlstm_chunkwise(q, k, v, ig, fg):
    B, S, H, dh = q.shape
    nc = S // M_CHUNK
    L = M_CHUNK

    def to_chunks(t):
        t = t.astype(jnp.float32).reshape((B, nc, L) + t.shape[2:])
        return jnp.moveaxis(jnp.moveaxis(t, 3, 2), 1, 0)

    qs = to_chunks(q)
    ks = to_chunks(k * (dh ** -0.5))
    vs = to_chunks(v)
    is_ = to_chunks(ig)
    fs = to_chunks(jax.nn.log_sigmoid(fg.astype(jnp.float32)))
    causal = jnp.tril(jnp.ones((L, L), dtype=bool))

    def step(carry, xs):
        C, n, m = carry
        qc, kc, vc, ic, fc = xs
        b = jnp.cumsum(fc, axis=-1)
        dlog = b[..., :, None] - b[..., None, :] + ic[..., None, :]
        dlog = jnp.where(causal, dlog, -jnp.inf)
        inter = b + m[..., None]
        mt = jnp.maximum(inter, jnp.max(dlog, axis=-1))
        dmat = jnp.exp(dlog - mt[..., None])
        wi = jnp.exp(inter - mt)
        s = jnp.einsum('bhtd,bhsd->bhts', qc, kc) * dmat
        num = (jnp.einsum('bhts,bhse->bhte', s, vc)
               + wi[..., None] * jnp.einsum('bhtd,bhde->bhte', qc, C))
        den = jnp.sum(s, axis=-1) + wi * jnp.einsum('bhtd,bhd->bht', qc, n)
        h = num / jnp.maximum(jnp.abs(den), jnp.exp(-mt))[..., None]
        bl = b[..., -1]
        endlog = bl[..., None] - b + ic
        m_new = jnp.maximum(bl + m, jnp.max(endlog, axis=-1))
        ws = jnp.exp(endlog - m_new[..., None])
        decay = jnp.exp(bl + m - m_new)
        wk = ws[..., None] * kc
        C = decay[..., None, None] * C + jnp.einsum('bhsd,bhse->bhde', wk, vc)
        n = decay[..., None] * n + jnp.sum(wk, axis=2)
        return (C, n, m_new), h

    init = (jnp.zeros((B, H, dh, dh), jnp.float32),
            jnp.zeros((B, H, dh), jnp.float32),
            jnp.zeros((B, H), jnp.float32))
    _, hs = lax.scan(step, init, (qs, ks, vs, is_, fs))
    h = jnp.moveaxis(jnp.moveaxis(hs, 0, 1), 2, 3)
    return h.reshape(B, S, H, dh)

def head_layernorm(h, g):
    mu = jnp.mean(h, axis=-1, keepdims=True)
    var = jnp.mean(jnp.square(h - mu), axis=-1, keepdims=True)
    y = (h - mu) * lax.rsqrt(var + LN_EPS)
    B, S, H, dh = h.shape
    return y.reshape(B, S, H * dh) * g.astype(jnp.float32)

def moba_attention(q, k, v, rel_bias):
    B, S, H, dh = q.shape
    f32 = jnp.float32
    nb = -(-S // MOBA_BLOCK)
    s_pad = nb * MOBA_BLOCK
    topk = min(MOBA_TOPK, nb)
    q = jnp.transpose(q, (0, 2, 1, 3)) * (dh ** -0.5)
    pad = ((0, 0), (0, 0), (0, s_pad - S), (0, 0))
    k = jnp.pad(jnp.transpose(k, (0, 2, 1, 3)), pad)
    v = jnp.pad(jnp.transpose(v, (0, 2, 1, 3)), pad)
    kblk = k.reshape(B, H, nb, MOBA_BLOCK, dh)
    vblk = v.reshape(B, H, nb, MOBA_BLOCK, dh)
    kmean = jnp.mean(kblk.astype(f32), axis=3)
    bidx = jnp.arange(B)[:, None, None, None]
    hidx = jnp.arange(H)[None, :, None, None]
    blk_off = jnp.arange(MOBA_BLOCK)
    nsel = topk * MOBA_BLOCK

    def chunk(ci):
        q0 = ci * Q_CHUNK
        qc = lax.dynamic_slice_in_dim(q, q0, Q_CHUNK, axis=2).astype(f32)
        qpos = q0 + jnp.arange(Q_CHUNK)
        own = q0 // MOBA_BLOCK
        gate = jnp.einsum('bhqd,bhnd->bhqn', qc, kmean)
        gate = jnp.where(jnp.arange(nb) < own, gate, -jnp.inf)
        _, idx = lax.top_k(gate, topk)
        valid = jnp.arange(topk) < own
        ksel = kblk[bidx, hidx, idx]
        vsel = vblk[bidx, hidx, idx]
        kpos = idx[..., None] * MOBA_BLOCK + blk_off
        bias_sel = rel_bias[rel_bucket(qpos[:, None, None] - kpos), hidx[..., None]]
        ls = jnp.einsum('bhqd,bhqkjd->bhqkj', qc, ksel.astype(f32)) + bias_sel
        ls = jnp.where(valid[:, None], ls, -jnp.inf)
        kown = lax.dynamic_slice_in_dim(k, own * MOBA_BLOCK, MOBA_BLOCK, axis=2)
        vown = lax.dynamic_slice_in_dim(v, own * MOBA_BLOCK, MOBA_BLOCK, axis=2)
        rel_own = qpos[:, None] - (own * MOBA_BLOCK + blk_off)[None, :]
        bias_own = jnp.transpose(rel_bias[rel_bucket(rel_own)], (2, 0, 1))
        lo = jnp.einsum('bhqd,bhjd->bhqj', qc, kown.astype(f32)) + bias_own
        lo = jnp.where(rel_own >= 0, lo, -jnp.inf)
        logits = jnp.concatenate([ls.reshape(B, H, Q_CHUNK, nsel), lo], axis=-1)
        p = jax.nn.softmax(logits.astype(f32), axis=-1)
        ps = p[..., :nsel].reshape(B, H, Q_CHUNK, topk, MOBA_BLOCK)
        po = p[..., nsel:]
        out = (jnp.einsum('bhqkj,bhqkjd->bhqd', ps, vsel.astype(f32))
               + jnp.einsum('bhqj,bhjd->bhqd', po, vown.astype(f32)))
        return out.astype(q.dtype)

    outs = lax.map(chunk, jnp.arange(S // Q_CHUNK))
    out = jnp.transpose(outs, (1, 2, 0, 3, 4)).reshape(B, H, S, dh)
    return jnp.transpose(out, (0, 2, 1, 3)).reshape(B, S, H * dh)

def hier_moe(h, w_grp, b_grp, w_exp, b_exp, w1, w3, w2):
    B, S, D = h.shape
    f32 = jnp.float32
    t = h.reshape(-1, D)
    pg = jax.nn.softmax((t @ w_grp).astype(f32) + b_grp.astype(f32), axis=-1)
    pg_top, g_sel = lax.top_k(pg, 1)
    el = ((t @ w_exp).astype(f32) + b_exp.astype(f32)).reshape(-1, N_GROUPS, EXP_PER_GROUP)
    el = jnp.take_along_axis(el, g_sel[:, :, None], axis=1)[:, 0]
    pe_top, e_sel = lax.top_k(jax.nn.softmax(el, axis=-1), TOP_K_IN_GROUP)
    w = pg_top * pe_top / jnp.sum(pe_top, axis=-1, keepdims=True)
    eid = g_sel * EXP_PER_GROUP + e_sel
    combine = jnp.sum(jax.nn.one_hot(eid, N_EXPERTS, dtype=f32) * w[..., None], axis=1)
    hid = jax.nn.silu(jnp.einsum('td,edf->tef', t, w1)) * jnp.einsum('td,edf->tef', t, w3)
    hid = hid * combine[..., None].astype(hid.dtype)
    out = jnp.einsum('tef,efd->td', hid, w2)
    return out.reshape(B, S, D).astype(h.dtype)

def hybrid_layer(x, norm1_g, w_in, conv_w, if_bias, mnorm_g, w_branch_m, w_branch_a,
                 w_out, rel_bias, norm2_g, w_grp, b_grp, w_exp, b_exp, w1, w3, w2):
    B, S, _ = x.shape
    h = rms_norm(x, norm1_g)
    z = h @ w_in
    qm, km, vm, om, im, fm, qa, ka, va, gm, ga = _split_cols(z)
    qk = jax.nn.silu(causal_dwconv(jnp.concatenate([qm, km], axis=-1), conv_w))
    qm, km = qk[..., :M_WIDTH], qk[..., M_WIDTH:]
    heads_m = lambda t: t.reshape(B, S, M_HEADS, M_HEAD_DIM)
    ig = im + if_bias[:M_HEADS]
    fg = fm + if_bias[M_HEADS:]
    hm = mlstm_chunkwise(heads_m(qm), heads_m(km), heads_m(vm), ig, fg)
    hm = (jax.nn.sigmoid(om.astype(jnp.float32)) * head_layernorm(hm, mnorm_g)).astype(x.dtype)
    heads_a = lambda t: t.reshape(B, S, A_HEADS, A_HEAD_DIM)
    ha = moba_attention(heads_a(qa), heads_a(ka), heads_a(va), rel_bias)
    y = jax.nn.sigmoid(gm) * (hm @ w_branch_m) + jax.nn.sigmoid(ga) * (ha @ w_branch_a)
    x = x + y @ w_out
    x = x + hier_moe(rms_norm(x, norm2_g), w_grp, b_grp, w_exp, b_exp, w1, w3, w2)
    return x

def setup_inputs(seed: int = 0) -> dict:
    key = jax.random.key(seed)
    ks = jax.random.split(key, 20)
    f32 = jnp.float32

    def nrm(k, shape, scale):
        return jax.random.normal(k, shape, f32) * scale

    i_bias = nrm(ks[4], (DEPTH, M_HEADS), 0.1)
    f_bias = jnp.linspace(3.0, 6.0, M_HEADS, dtype=f32)[None, :] + nrm(ks[5], (DEPTH, M_HEADS), 0.1)
    return {
        'x': nrm(ks[0], (BATCH, SEQ, D_MODEL), 1.0),
        'norm1_g': 1.0 + nrm(ks[1], (DEPTH, D_MODEL), 0.02),
        'w_in': nrm(ks[2], (DEPTH, D_MODEL, IN_COLS), D_MODEL ** -0.5),
        'conv_w': nrm(ks[3], (DEPTH, M_CONV, 2 * M_WIDTH), M_CONV ** -0.5),
        'if_bias': jnp.concatenate([i_bias, f_bias], axis=-1),
        'mnorm_g': 1.0 + nrm(ks[6], (DEPTH, M_WIDTH), 0.02),
        'w_branch_m': nrm(ks[7], (DEPTH, M_WIDTH, D_MODEL), M_WIDTH ** -0.5),
        'w_branch_a': nrm(ks[8], (DEPTH, A_WIDTH, D_MODEL), A_WIDTH ** -0.5),
        'w_out': nrm(ks[9], (DEPTH, D_MODEL, D_MODEL), D_MODEL ** -0.5),
        'rel_bias': nrm(ks[10], (REL_BUCKETS, A_HEADS), 0.5),
        'norm2_g': 1.0 + nrm(ks[11], (DEPTH, D_MODEL), 0.02),
        'w_grp': nrm(ks[12], (DEPTH, D_MODEL, N_GROUPS), D_MODEL ** -0.5),
        'b_grp': nrm(ks[13], (DEPTH, N_GROUPS), 0.01),
        'w_exp': nrm(ks[14], (DEPTH, D_MODEL, N_EXPERTS), D_MODEL ** -0.5),
        'b_exp': nrm(ks[15], (DEPTH, N_EXPERTS), 0.01),
        'w1': nrm(ks[16], (DEPTH, N_EXPERTS, D_MODEL, D_FF_EXPERT), D_MODEL ** -0.5),
        'w3': nrm(ks[17], (DEPTH, N_EXPERTS, D_MODEL, D_FF_EXPERT), D_MODEL ** -0.5),
        'w2': nrm(ks[18], (DEPTH, N_EXPERTS, D_FF_EXPERT, D_MODEL), D_FF_EXPERT ** -0.5),
        'final_g': 1.0 + nrm(ks[19], (D_MODEL,), 0.02),
    }

def reference(x, norm1_g, w_in, conv_w, if_bias, mnorm_g, w_branch_m, w_branch_a, w_out,
              rel_bias, norm2_g, w_grp, b_grp, w_exp, b_exp, w1, w3, w2, final_g):
    for l in range(DEPTH):
        x = hybrid_layer(x, norm1_g[l], w_in[l], conv_w[l], if_bias[l], mnorm_g[l],
                         w_branch_m[l], w_branch_a[l], w_out[l], rel_bias, norm2_g[l],
                         w_grp[l], b_grp[l], w_exp[l], b_exp[l], w1[l], w3[l], w2[l])
    return rms_norm(x, final_g)


_drawn_inputs = setup_inputs


def setup_inputs(seed=0):
    import zlib

    import numpy as np

    out = dict(_drawn_inputs(seed))
    spreads = {}
    factors = {'mnorm_g': 3.285, 'b_grp': 4.928, 'b_exp': 11.581, 'final_g': 8.509, 'norm2_g': 2.76}
    for name, (base, spread) in spreads.items():
        noise = np.random.default_rng([zlib.crc32(name.encode()), seed]).standard_normal(out[name].shape)
        drawn = base * np.exp(spread * noise) if base else spread * noise
        out[name] = __import__('jax').numpy.asarray(drawn.astype(out[name].dtype))
    for name, factor in factors.items():
        out[name] = (out[name] * factor).astype(out[name].dtype)
    return out
```

```python
from contextlib import ExitStack, contextmanager

import numpy as np

import concourse.bass as bass
from concourse import mybir

F32 = mybir.dt.float32
F32R = mybir.dt.float32r
I32 = mybir.dt.int32
ALU = mybir.AluOpType
ACT = mybir.ActivationFunctionType
AX = mybir.AxisListType
ds = bass.ds

P = 128
T = 256
TT = T // P
D = 2048
DC = D // P
M_HEADS, M_DIM = 4, 256
M_WIDTH = M_HEADS * M_DIM
A_HEADS, A_DIM = 8, 128
A_WIDTH = A_HEADS * A_DIM
CONV = 4
BUCKETS, MAX_DIST = 32, 128
GROUPS, PER_GROUP = 4, 8
EXPERTS = GROUPS * PER_GROUP
FF = 256
FC = FF // P
RMS_EPS, LN_EPS = 1e-6, 1e-5
MASKED = -1e30

COL_QK, COL_V, COL_O = 0, 2 * M_WIDTH, 3 * M_WIDTH
COL_IF = 4 * M_WIDTH
COL_QA = COL_IF + 2 * M_HEADS
COL_KA, COL_VA = COL_QA + A_WIDTH, COL_QA + 2 * A_WIDTH
COL_GATES = COL_VA + A_WIDTH

UNIT = 256
HALF_K = DC // 2
RAW = 4
PAIR_HALVES = 4

UNITS_QK = 2 * M_WIDTH // UNIT
UNITS_QKA = 2 * A_WIDTH // UNIT
UNITS_VO = 2 * M_WIDTH // UNIT
UNITS_VA = A_WIDTH // UNIT
UNITS_GATES = 2 * D // UNIT
UNITS_BRANCH = D // UNIT
UNITS_OUT = D // UNIT
UNIT_QKA = UNITS_QK
UNIT_VO = UNIT_QKA + UNITS_QKA
UNIT_VA = UNIT_VO + UNITS_VO
UNIT_GATES = UNIT_VA + UNITS_VA
UNIT_BRANCH = UNIT_GATES + UNITS_GATES
UNIT_OUT = UNIT_BRANCH + UNITS_BRANCH
UNITS = UNIT_OUT + UNITS_OUT
HALVES = 2 * UNITS

SLOTS = 64
PAIRS = 2 * T
CHUNKS = T // SLOTS
GROUPS_OUT = TT * D // 512
REV = 384

G1_ROW, CONV_ROW, MN_ROW = 0, DC, DC + CONV * DC
PARAM_ROWS = MN_ROW + M_WIDTH // P


def bucket_onehot():
    n = np.arange(T)
    half = BUCKETS // 2
    large = half + (np.log(np.maximum(n, 1).astype(np.float32) / half)
                    / np.log(MAX_DIST / half) * (BUCKETS - half)).astype(np.int32)
    bucket = np.where(n < half, n, np.minimum(large, BUCKETS - 1))[::-1]
    return (np.arange(BUCKETS)[:, None] == bucket[None, :]).astype(np.float32)


class Steps:

    def __init__(self, eng, sem):
        self.eng, self.sem, self.n, self.loops = eng, sem, 0, []

    def done(self, ins):
        ins.then_inc(self.sem, 1)
        self.n += 1
        value = self.n
        for i, per in self.loops:
            value = i * per + value
        self.eng.wait_ge(self.sem, value)

    @contextmanager
    def loop(self, start, end, per):
        entered = self.n
        with self.eng.Fori(start, end) as i:
            self.n -= start * per
            self.loops.append((i, per))
            yield i
            self.loops.pop()
            assert self.n == entered - start * per + per, (self.n - entered + start * per, per)
        self.n = entered + (end - start) * per


def layer(nc, x, norm1_g, w_in, conv_w, if_bias, mnorm_g, w_branch_m, w_branch_a, w_out, rel_bias,
          norm2_g, w_grp, b_grp, w_exp, b_exp, w1, w3, w2, final_g, onehot, out):
    ctx = ExitStack()
    with ctx:
        place = {"at": 2048, "end": 229 * 1000}

        def sb(name, shape, dt=F32, at=None):
            size = int(np.prod(shape[1:])) * 4
            where = place["at"] if at is None else at
            if at is None:
                place["at"] += (size + 31) // 32 * 32
            assert where + size <= place["end"], (name, where + size)
            return nc.alloc_sbuf_tensor_at(name, shape, dt, offset=where)

        def sem(name):
            return ctx.enter_context(nc.semaphore(name))

        KB = 1024
        AT_TOK = place["at"]
        AT_ACT = AT_TOK + 24 * KB
        AT_WRAW = AT_ACT + 32 * KB
        AT_WSPLIT = AT_WRAW + 32 * KB
        AT_GATES = AT_WSPLIT + 32 * KB
        AT_QK = AT_GATES + 32 * KB
        AT_SMALL = AT_QK + 32 * KB
        place["at"] = AT_SMALL
        tok = sb("tok", [P, 3, TT, M_WIDTH], at=AT_TOK)
        act_split = sb("act_split", [P, DC, 2, T], F32R, at=AT_ACT)
        wraw = sb("wraw", [P, RAW, HALF_K, UNIT], at=AT_WRAW)
        wsplit = sb("wsplit", [P, 2, HALF_K, 2, UNIT], F32R, at=AT_WSPLIT)
        gates = sb("gates", [P, 2 * DC, T], at=AT_GATES)
        xin = sb("xin", [P, TT, D], at=AT_GATES)
        qk = sb("qk", [P, 32, T], at=AT_QK)
        br_split = sb("br_split", [P, DC, 2, T], F32R, at=AT_QK)
        x2 = sb("x2", [P, TT, D], at=AT_TOK)
        xg = sb("xg", [P, DC, PAIRS + SLOTS], at=AT_TOK + 16 * KB)
        w13 = [sb("w13_a", [P, 2, DC, FF], at=AT_GATES), sb("w13_b", [P, 2, DC, FF], at=AT_WRAW)]
        w2s = [sb("w2_a", [P, FC, D], at=AT_GATES + 32 * KB), sb("w2_b", [P, FC, D], at=AT_WRAW + 32 * KB)]
        h2T = sb("h2T", [P, DC, T], at=AT_WRAW + 48 * KB)
        h2n = sb("h2n", [P, TT, D], at=AT_QK + 16 * KB)
        fin_g = sb("fin_g", [P, D], at=AT_QK + 16 * KB)
        fin = sb("fin", [P, TT, D], at=AT_TOK + 16 * KB)

        ident = sb("ident", [P, P])
        flip = sb("flip", [P, P])
        ones = sb("ones", [P, P])
        upto = sb("upto", [P, P])
        before = sb("before", [P, P])
        mask_ts = sb("mask_ts", [P, P])
        mask_st = sb("mask_st", [P, P])
        params = sb("params", [P, PARAM_ROWS])
        g2T = sb("g2T", [P, DC])
        stat = sb("stat", [P, 64])
        power = sb("power", [P, TT])
        AT_PHASE = place["at"]

        pick = sb("pick", [M_HEADS, M_HEADS, P])
        ifb = sb("ifb", [P, 2 * M_HEADS])
        relb = sb("relb", [BUCKETS, A_HEADS])
        ifg = sb("ifg", [P, TT, 2 * M_HEADS])
        lsg = sb("lsg", [P, TT, M_HEADS])
        lst = sb("lst", [P, TT, M_HEADS])
        cum = sb("cum", [P, TT, M_HEADS])
        aa = sb("aa", [P, TT, M_HEADS])
        aaT = negMT = sb("row_by_head", [M_HEADS, T])
        negM = sb("negM", [P, TT, M_HEADS])
        pick_now = sb("pick_now", [M_HEADS, P])
        bn = sb("bn", [P, TT, 6])
        mean_var = sb("mean_var", [P, TT, 2])
        expm = sb("expm", [P, TT, M_HEADS])
        AT_CONV = place["at"]
        bias_flipped = sb("bias_flipped", [P, A_HEADS, T])
        qk_now = sb("qk_now", [P, 8, T])
        v_now = sb("v_now", [P, 2, TT, M_DIM])
        decay = scored = sb("decay", [P, REV])
        prob = probT = sb("prob", [P, 2, REV])
        hm = sb("hm", [P, TT, M_DIM])
        AT_EARLY = AT_CONV + 20 * KB
        param_rows = sb("param_rows", [PARAM_ROWS, P], at=AT_EARLY)
        wif_raw = sb("wif_raw", [P, DC, 2 * M_HEADS], at=AT_EARLY + 512)
        wif = sb("wif", [P, DC, 2, 2 * M_HEADS], F32R, at=AT_EARLY + 1024)
        onehot_s = sb("onehot_s", [BUCKETS, T], at=AT_EARLY + 2048)
        rev = sb("rev", [A_HEADS, REV], at=AT_EARLY + 3072)
        pre = sb("pre", [P, 2, T + CONV - 1], at=AT_CONV + 8 * KB)
        conv = sb("conv", [P, 2, T], at=AT_CONV + 12 * KB)
        csig = sb("csig", [P, 2, T], at=AT_CONV + 16 * KB)
        sgm = sb("sgm", [P, 2, 2, T], at=AT_CONV)
        bsum = sb("bsum", [P, 2, 2, T], at=AT_CONV + 4 * KB)
        osum = sb("osum", [P, TT, UNIT], at=AT_CONV + 8 * KB)
        xsq = sb("xsq", [P, D], at=AT_CONV)

        place["at"] = AT_PHASE
        wrt = sb("wrt", [P, DC, GROUPS + EXPERTS])
        brt = sb("brt", [P, GROUPS + EXPERTS])
        lr = sb("lr", [P, TT, GROUPS + EXPERTS])
        iota_e = sb("iota_e", [P, EXPERTS])
        iota_s = sb("iota_s", [P, PAIRS])
        iota_c = sb("iota_c", [P, CHUNKS, SLOTS])
        rt = sb("rt", [P, 8, EXPERTS])
        oh = sb("oh", [P, TT, 2, EXPERTS])
        mk = sb("mk", [P, TT, EXPERTS])
        wt = sb("wt", [P, TT, EXPERTS])
        rank = sb("rank", [P, TT, EXPERTS])
        pos = sb("pos", [P, TT, EXPERTS])
        starts = sb("starts", [P, EXPERTS, CHUNKS])
        starts_i = sb("starts_i", [1, EXPERTS, CHUNKS], I32)
        most_i = sb("most_i", [1, 1], I32)
        AT_SEL = place["at"]
        sel = sb("sel", [P, TT, PAIRS])
        xsq2 = sb("xsq2", [P, D])
        phase_a = place["at"]
        place["at"] = AT_SEL
        xe = sb("xe", [P, 2, DC, SLOTS])
        mix = sb("mix", [P, TT, P])
        mixT = sb("mixT", [P, T])
        sg = sb("sg", [P, P])
        hid = sb("hid", [P, P])
        hidT = sb("hidT", [P, 2, P])
        ys = sb("ys", [P, D])

        ps = ctx.enter_context(nc.psum_tensor("ps", [P, 8, 512], F32))
        rev_dram = nc.dram_tensor("rev_dram", (A_HEADS, REV), F32, kind="Internal").ap()

        x_loaded, par_loaded, consts = sem("x_loaded"), sem("par_loaded"), sem("consts_ready")
        raw_loaded = [sem(f"raw_loaded{i}") for i in range(RAW)]
        rounded, split, used, acc_free = sem("rounded"), sem("split"), sem("used"), sem("acc_free")
        dve_s, act_s, pool_s = sem("dve_step"), sem("act_step"), sem("pool_step")
        squares, normed, turned, hi_ready, bank_free = (sem(n) for n in (
            "squares", "normed", "turned", "hi_ready", "bank_free"))
        param_turned, param_ready, wif_hi, wif_ready = (sem(n) for n in (
            "param_turned", "param_ready", "wif_hi", "wif_ready"))
        rev_summed, rev_ready, rev_stored, flip_loaded = (sem(n) for n in (
            "rev_summed", "rev_ready", "rev_stored", "bias_flipped_loaded"))
        conv_ready, conv_sig = sem("conv_ready"), sem("conv_sigmoid")
        if_summed, absf_ready, expf_ready, onef_ready, lnf_ready, ls_ready, cum_summed, aa_ready = (
            sem(n) for n in ("if_summed", "absf_ready", "expf_ready", "onef_ready", "lnf_ready",
                             "ls_ready", "cum_summed", "aa_ready"))
        aa_turned, aaT_ready, aa_spread, negM_ready, negM_turned, negMT_ready, mt_ready, expm_ready = (
            sem(n) for n in ("aa_turned", "aaT_ready", "aa_spread", "negM_ready", "negM_turned",
                             "negMT_ready", "mt_ready", "expm_ready"))
        o_ready, staged = sem("o_sigmoid_ready"), sem("staged")
        logits, scores, decay_arg, decay_exp = (sem(n) for n in (
            "logits_summed", "scores_summed", "decay_arg", "decay_exp"))
        negmax, prob_exp, prob_ready, scored_ready = (sem(n) for n in (
            "negmax_ready", "prob_exp", "prob_ready", "scored_ready"))
        prob_turned, num_summed, probT_ready, hm_ready, ha_summed, hm_turned, br_hi, br_lo = (
            sem(n) for n in ("prob_turned", "num_summed", "probT_ready", "hm_ready", "ha_summed",
                             "hm_turned", "branch_hi", "branch_lo"))
        root_go, root_done, gate_sig, y_sum, y_hi, y_ready = (sem(n) for n in (
            "root_go", "root_done", "gate_sigmoid", "y_sum", "y_hi", "y_ready"))
        x2_loaded, x2_ready, moe_par, iotas = (sem(n) for n in (
            "x2_loaded", "x2_ready", "expert_params_loaded", "iotas_ready"))
        squares2, h2n_ready, h2_turned, h2T_ready, routed = (sem(n) for n in (
            "squares2", "h2n_ready", "h2_turned", "h2T_ready", "router_summed"))
        gexp_go, gexp_done, mk_ready, rank_summed, sel_ready, xg_summed, xg_act, xg_dve, tab_ready = (
            sem(n) for n in ("group_exp_go", "group_exp_done", "chosen_ready", "rank_summed",
                             "selection_ready", "gathered", "gathered_even", "gathered_odd",
                             "table_ready"))
        w13_loaded = [sem("w13a_loaded"), sem("w13b_loaded")]
        w2_loaded = [sem("w2a_loaded"), sem("w2b_loaded")]
        xe_ready, h_summed, sg_ready, hid_ready, hid_turned, hidT_ready, y_summed, ys_ready = (
            sem(n) for n in ("xe_ready", "hidden_summed", "hidden_sigmoid", "hid_ready", "hid_turned",
                             "hidT_ready", "ye_summed", "ye_ready"))
        mix_ready, mix_turned, mixT_ready, scattered, added = (sem(n) for n in (
            "mix_ready", "mix_turned", "mixT_ready", "scattered", "added"))
        fing_loaded, squares3, out_ready, out_stored = (sem(n) for n in (
            "final_g_loaded", "squares3", "out_ready", "out_stored"))
        dve_x = sem("dve_expert_step")

        win_v = w_in.rearrange("(h k p) n -> p h k n", h=2, p=P)
        wout_v = w_out.rearrange("(h k p) n -> p h k n", h=2, p=P)
        wbm_v = w_branch_m.rearrange("(k p) n -> p k n", p=P)
        wba_v = w_branch_a.rearrange("(k p) n -> p k n", p=P)
        x_v = x.rearrange("(t p) d -> p t d", p=P)
        out_v = out.rearrange("(t p) d -> p t d", p=P)
        w1_v = w1.rearrange("e (p c) f -> p e c f", c=DC)
        w3_v = w3.rearrange("e (p c) f -> p e c f", c=DC)
        w2_v = w2.rearrange("e (j p) n -> p e j n", p=P)

        def halves_sum(bank):
            return bank.rearrange("p (a n) -> p n a", a=2)

        def by_most(eng, experts):
            eng.wait_ge(tab_ready, 1)
            most = eng.value_load(most_i[0:1, 0:1], min_val=0, max_val=T)
            with eng.If(most < SLOTS + 1):
                experts(1)
            with eng.Else():
                experts(CHUNKS)
            eng.end_ifs()

        @contextmanager
        def passes(eng, chunks, steps=None, per=0):
            if chunks == 1:
                yield 0
            elif steps is None:
                with eng.Fori(0, chunks) as c:
                    yield c
            else:
                with steps.loop(0, chunks, per) as c:
                    yield c

        block = ctx.enter_context(nc.Block())

        @block.sync
        def _(sp):
            sp.dma_start(xin[:], x_v).then_inc(x_loaded, 16)

            def load(slot, src, half):
                if half is not None:
                    sp.wait_ge(split, half + (1 - RAW))
                sp.dma_start(wraw[:, slot], src).then_inc(raw_loaded[slot], 16)

            def pair(col, half):
                for q in range(PAIR_HALVES):
                    load(q, win_v[:, q % 2, :, ds(col + (q // 2) * UNIT, UNIT)],
                         None if half is None else half + q)

            def pairs(start, units, col, unit):
                with sp.Fori(start, units // 2) as i:
                    pair(i * (2 * UNIT) + col, i * PAIR_HALVES + 2 * unit)

            pair(COL_QK, None)
            pairs(1, UNITS_QK, COL_QK, 0)
            pairs(0, UNITS_QKA, COL_QA, UNIT_QKA)
            pairs(0, UNITS_VO, COL_V, UNIT_VO)
            pairs(0, UNITS_VA, COL_VA, UNIT_VA)
            pairs(0, UNITS_GATES, COL_GATES, UNIT_GATES)
            with sp.Fori(0, UNITS_BRANCH // 2) as i:
                for q in range(PAIR_HALVES):
                    load(q, (wbm_v, wba_v)[q % 2][:, :, ds(i * (2 * UNIT) + (q // 2) * UNIT, UNIT)],
                         i * PAIR_HALVES + 2 * UNIT_BRANCH + q)
            sp.wait_ge(br_lo, M_HEADS + 1)
            sp.dma_start(x2[:], x_v).then_inc(x2_loaded, 16)
            with sp.Fori(0, UNITS_OUT // 2) as i:
                for q in range(PAIR_HALVES):
                    load(q, wout_v[:, q % 2, :, ds(i * (2 * UNIT) + (q // 2) * UNIT, UNIT)],
                         i * PAIR_HALVES + 2 * UNIT_OUT + q)

            def load_hidden(b, e):
                sp.dma_start(w13[b][:, 0], w1_v[:, e]).then_inc(w13_loaded[b], 16)
                sp.dma_start(w13[b][:, 1], w3_v[:, e]).then_inc(w13_loaded[b], 16)

            def load_rows(b, e):
                sp.dma_start(w2s[b][:], w2_v[:, e]).then_inc(w2_loaded[b], 16)

            sp.wait_ge(y_ready, UNITS_BRANCH + 1)
            load_hidden(0, 0)
            load_rows(0, 0)
            sp.wait_ge(used, HALVES)
            load_hidden(1, 1)
            load_rows(1, 1)

            def experts(chunks):
                with sp.Fori(0, EXPERTS // 2 - 1) as i:
                    for b in range(2):
                        sp.wait_ge(h_summed, i * (2 * chunks) + (2 * chunks + b))
                        load_hidden(b, ds(i * 2 + (b + 2), 1))
                    sp.wait_ge(y_summed, i * chunks + (chunks + 1))
                    for b in range(2):
                        load_rows(b, ds(i * 2 + (b + 2), 1))

            by_most(sp, experts)
            for t in range(TT):
                sp.wait_ge(out_ready, t + 1)
                sp.dma_start(out_v[:, t], fin[:, t]).then_inc(out_stored, 16)
            sp.wait_ge(out_stored, 16 * TT)

        @block.gpsimd
        def _(pool):
            steps = Steps(pool, pool_s)
            for primed in (hm_turned, ha_summed, br_lo, y_sum, y_ready, x2_ready, h_summed, mix_turned, hid_turned,
                           hid_ready, hidT_ready, mixT_ready, y_summed, ys_ready, scattered, added):
                pool.sem_inc(primed, 1)
            for m in (ident, flip, before, mask_ts, mask_st, pick):
                last = pool.memset(m[:], 0.0)
            pool.memset(upto[:], 1.0)
            pool.memset(power[:], -0.5)
            steps.done(pool.memset(ones[:], 1.0))

            def choose(m, keep, fill, base, pattern, mult):
                return pool.affine_select(out=m[:], in_=m[:], compare_op=keep, fill=fill, base=base,
                                          pattern=pattern, channel_multiplier=mult)

            choose(ident, ALU.not_equal, 1.0, 0, [[-1, P]], 1)
            choose(flip, ALU.not_equal, 1.0, -(P - 1), [[1, P]], 1)
            choose(upto, ALU.is_ge, 0.0, 0, [[1, P]], -1)
            choose(before, ALU.is_ge, 1.0, 0, [[-1, P]], 1)
            choose(mask_ts, ALU.is_ge, MASKED, 0, [[-1, P]], 1)
            choose(mask_st, ALU.is_ge, MASKED, 0, [[1, P]], -1)
            choose(pick, ALU.not_equal, 1.0, 0, [[-1, M_HEADS], [0, P]], 1).then_inc(consts, 1)

            def root(col, n, turn):
                pool.wait_ge(root_go, turn)
                pool.tensor_tensor(stat[:, col:col + n], stat[:, col:col + n], power[:, 0:n], ALU.pow).then_inc(root_done, 1)

            root(2, TT, 1)
            pool.wait_ge(acc_free, UNIT_GATES)
            with steps.loop(0, M_HEADS, 1) as i:
                pool.wait_ge(hm_turned, i + 1)
                pool.wait_ge(ha_summed, i * 2 + 1)
                pool.tensor_copy(pick_now[:], pick[:, ds(i, 1)])
                pool.tensor_copy(qk_now[:, 0:4], qk[:, ds(i * 4, 4)])
                steps.done(pool.tensor_copy(qk_now[:, 4:8], qk[:, ds(i * 4 + 16, 4)]))
                q_now = qk_now[:, 4:8].rearrange("p (a k) t -> p a k t", k=2)[:, :, 0]
                pool.tensor_copy(v_now[:, 0], tok[:, 0, :, ds(i * M_DIM, M_DIM)])
                pool.tensor_scalar(q_now, q_now, float(A_DIM) ** -0.5, None, ALU.mult)
                pool.tensor_copy(v_now[:, 1], tok[:, 2, :, ds(i * M_DIM, M_DIM)]).then_inc(staged, 1)
                root(36, 2, i + 2)

            pool.wait_ge(x2_ready, UNITS_OUT + 1)
            pool.iota(iota_e[:], pattern=[[1, EXPERTS]], base=-SLOTS, channel_multiplier=0,
                      allow_small_or_imprecise_dtypes=True)
            pool.iota(iota_s[:], pattern=[[1, PAIRS]], base=0, channel_multiplier=0,
                      allow_small_or_imprecise_dtypes=True)
            pool.iota(iota_c[:], pattern=[[SLOTS, CHUNKS], [1, SLOTS]], base=0,
                      channel_multiplier=0, allow_small_or_imprecise_dtypes=True).then_inc(iotas, 1)
            root(22, TT, M_HEADS + 2)
            root(42, TT, M_HEADS + 3)

        @block.scalar
        def _(act):
            steps = Steps(act, act_s)
            act.dma_start(param_rows[G1_ROW:CONV_ROW], norm1_g.rearrange("(r c) -> r c", c=P)).then_inc(par_loaded, 16)
            act.dma_start(param_rows[CONV_ROW:MN_ROW], conv_w.rearrange("j (r c) -> (j r) c", c=P)).then_inc(par_loaded, 16)
            act.dma_start(param_rows[MN_ROW:PARAM_ROWS], mnorm_g.rearrange("(r c) -> r c", c=P)).then_inc(par_loaded, 16)
            act.dma_start(wif_raw[:], w_in[:, COL_IF:COL_QA].rearrange("(k p) n -> p k n", p=P)).then_inc(par_loaded, 16)
            act.dma_start(ifb[:], if_bias.partition_broadcast(P)).then_inc(par_loaded, 16)
            act.dma_start(relb[:], rel_bias).then_inc(par_loaded, 16)
            act.dma_start(onehot_s[:], onehot).then_inc(par_loaded, 16)
            act.dma_start(g2T[:], norm2_g.rearrange("(p c) -> p c", c=DC)).then_inc(par_loaded, 16)

            act.wait_ge(x_loaded, 16)
            for t in range(TT):
                act.wait_ge(squares, t)
                act.activation(xsq[:], xin[:, t], ACT.Square, accum_out=stat[:, t:t + 1]).then_inc(squares, 1)
            act.wait_ge(par_loaded, 16 * 8)
            act.activation(wif[:, :, 0], wif_raw[:], ACT.Copy).then_inc(wif_hi, 1)

            def round_half(q, turn, half):
                act.wait_ge(raw_loaded[q % RAW], turn)
                if half is not None:
                    act.wait_ge(used, half - 1)
                act.activation(wsplit[:, q % 2, :, 0], wraw[:, q % RAW], ACT.Copy).then_inc(rounded, 1)

            def round_ahead(u, unit, i, last=False):
                for q in (2 * u + 2, 2 * u + 3):
                    round_half(q, i * 16 + (16 * (unit // 2 + q // RAW) + 16),
                               i * PAIR_HALVES + (2 * unit + q))

            for q in range(2):
                round_half(q, 16, None)
            act.wait_ge(param_ready, 1)
            for g in range(DC // 2):
                act.wait_ge(turned, g + 1)
                for c in range(2):
                    act.activation(act_split[:, 2 * g + c, 0], ps[:, g, c * T:(c + 1) * T], ACT.Copy,
                                   scale=params[:, G1_ROW + 2 * g + c:G1_ROW + 2 * g + c + 1]).then_inc(hi_ready, 1)
            act.wait_ge(rev_ready, 1)
            act.dma_start(rev_dram, rev[:]).then_inc(rev_stored, 16)
            act.wait_ge(rev_stored, 16)
            for h in range(A_HEADS):
                act.dma_start(bias_flipped[:, h], bass.AP(tensor=rev_dram.tensor, offset=h * REV, ap=[[1, P], [1, T]])).then_inc(flip_loaded, 16)

            with act.Fori(0, UNITS_QK // 2) as i:
                for u in range(2):
                    round_ahead(u, 0, i)
                    act.wait_ge(conv_ready, i * 2 + (u + 1))
                    act.activation(csig[:], conv[:], ACT.Sigmoid).then_inc(conv_sig, 1)
            act.wait_ge(absf_ready, 1)
            act.activation(lsg[:], lsg[:], ACT.Exp, scale=-1.0).then_inc(expf_ready, 1)
            act.wait_ge(onef_ready, 1)
            act.activation(lsg[:], lsg[:], ACT.Ln).then_inc(lnf_ready, 1)
            for unit, units in ((UNIT_QKA, UNITS_QKA), (UNIT_VO, UNITS_VO)):
                with act.Fori(0, units // 2) as i:
                    for u in range(2):
                        round_ahead(u, unit, i)
            act.wait_ge(acc_free, UNIT_VA)
            act.activation(tok[:, 1], tok[:, 1], ACT.Sigmoid).then_inc(o_ready, 1)
            with act.Fori(0, UNITS_VA // 2) as i:
                for u in range(2):
                    round_ahead(u, UNIT_VA, i)
            act.wait_ge(mt_ready, 1)
            act.activation(expm[:], expm[:], ACT.Exp, scale=-1.0).then_inc(expm_ready, 1)

            with act.Fori(0, M_HEADS) as i:
                def ahead(q):
                    round_half(q, i * 32 + (16 * (UNIT_GATES // 2 + q // RAW) + 16),
                               i * 8 + (2 * UNIT_GATES + q))

                ahead(2)
                act.wait_ge(decay_arg, i + 1)
                act.activation(decay[:], decay[:], ACT.Exp).then_inc(decay_exp, 1)
                for a in range(2):
                    act.wait_ge(negmax, i * 2 + (a + 1))
                    act.activation(prob[:, a, 0:P], ps[:, 4 + a, 0:P], ACT.Exp,
                                   bias=stat[:, 8 + 2 * a:9 + 2 * a], accum_out=stat[:, 12 + 2 * a:13 + 2 * a])
                    act.activation(prob[:, a, P:REV], ps[:, 4 + a, P:REV], ACT.Exp,
                                   bias=stat[:, 9 + 2 * a:10 + 2 * a],
                                   accum_out=stat[:, 13 + 2 * a:14 + 2 * a]).then_inc(prob_exp, 1)
                for q in range(3, 8):
                    ahead(q)
                for a in range(2):
                    act.wait_ge(ha_summed, i * 2 + (a + 2))
                    act.activation(br_split[:, ds(i * 2 + (8 + a), 1), 0], ps[:, 4 + a, 0:T], ACT.Copy).then_inc(br_hi, 1)
                act.wait_ge(hm_turned, i + 2)
                for c in range(2):
                    act.activation(br_split[:, ds(i * 2 + c, 1), 0], ps[:, 6, c * T:(c + 1) * T], ACT.Copy,
                                   scale=params[:, ds(i * 2 + (MN_ROW + c), 1)]).then_inc(br_hi, 1)
                ahead(8)
                ahead(9)

            with act.Fori(0, UNITS_BRANCH // 2) as i:
                for u in range(2):
                    round_ahead(u, UNIT_BRANCH, i)
                    act.wait_ge(y_sum, i * 2 + (u + 1))
                    for g in range(2):
                        last = act.activation(sgm[:, g], gates[:, ds(i * 4 + (2 * u + g * DC), 2)], ACT.Sigmoid)
                    last.then_inc(gate_sig, 1)
                    act.wait_ge(y_sum, i * 2 + (u + 2))
                    act.activation(act_split[:, ds(i * 4 + 2 * u, 2), 0], bsum[:, 0], ACT.Copy).then_inc(y_hi, 1)
            act.dma_start(wrt[:, :, 0:GROUPS], w_grp.rearrange("(p c) n -> p c n", c=DC)).then_inc(moe_par, 16)
            act.dma_start(wrt[:, :, GROUPS:], w_exp.rearrange("(p c) n -> p c n", c=DC)).then_inc(moe_par, 16)
            act.dma_start(brt[:, 0:GROUPS], b_grp.partition_broadcast(P)).then_inc(moe_par, 16)
            act.dma_start(brt[:, GROUPS:], b_exp.partition_broadcast(P)).then_inc(moe_par, 16)
            with act.Fori(0, UNITS_OUT // 2 - 1) as i:
                for u in range(2):
                    round_ahead(u, UNIT_OUT, i)
            round_half(2, 16 * (HALVES // RAW), HALVES - 2)
            round_half(3, 16 * (HALVES // RAW), HALVES - 1)

            act.wait_ge(x2_ready, UNITS_OUT + 1)
            for t in range(TT):
                act.wait_ge(squares2, t)
                act.activation(xsq2[:], x2[:, t], ACT.Square, accum_out=stat[:, 20 + t:21 + t]).then_inc(squares2, 1)
            act.wait_ge(h2n_ready, TT)
            for g in range(0, DC // 2, 2):
                act.wait_ge(h2_turned, g + 1)
                for c in range(2):
                    act.activation(h2T[:, 2 * g + c], ps[:, g, c * T:(c + 1) * T], ACT.Copy,
                                   scale=g2T[:, 2 * g + c:2 * g + c + 1]).then_inc(h2T_ready, 1)
            for t in range(TT):
                act.wait_ge(gexp_go, 2 * t + 1)
                act.activation(rt[:, 0, 0:GROUPS], lr[:, t, 0:GROUPS], ACT.Exp, bias=stat[:, 24:25],
                               accum_out=stat[:, 25:26]).then_inc(gexp_done, 1)
                act.wait_ge(gexp_go, 2 * t + 2)
                act.activation(stat[:, 28:29], stat[:, 27:28], ACT.Exp).then_inc(gexp_done, 1)
            for c in range(DC):
                if c % 2 == 0:
                    act.wait_ge(xg_summed, c + 1)
                    act.activation(xg[:, c, 0:PAIRS], ps[:, c % 8], ACT.Copy, scale=g2T[:, c:c + 1]).then_inc(xg_act, 1)
            act.wait_ge(xg_summed, DC)
            act.dma_start(fin_g[:], final_g.partition_broadcast(P)).then_inc(fing_loaded, 16)

            def experts(chunks):
                with act.Fori(0, EXPERTS // 2) as i:
                    with passes(act, chunks) as c:
                        s = i * chunks + c
                        for b in range(2):
                            n = s * 2 + b
                            act.wait_ge(h_summed, n + 2)
                            act.wait_ge(hid_ready, n + 1)
                            act.activation(sg[:], ps[:, 0, 0:P], ACT.Sigmoid).then_inc(sg_ready, 1)
                            act.wait_ge(hid_turned, n + 2)
                            act.wait_ge(y_summed, s + 1)
                            act.activation(hidT[:, b], ps[:, 1, 0:P], ACT.Copy).then_inc(hidT_ready, 1)
                        act.wait_ge(mix_turned, s + 2)
                        act.wait_ge(scattered, s * GROUPS_OUT + 1)
                        act.activation(mixT[:], ps[:, 1, P:3 * P], ACT.Copy).then_inc(mixT_ready, 1)
                        act.wait_ge(y_summed, s + 2)
                        act.activation(ys[:], ps[:, 2:6].rearrange("p a n -> p (a n)"), ACT.Copy).then_inc(ys_ready, 1)
                act.wait_ge(added, EXPERTS // 2 * chunks * GROUPS_OUT + 1)

            by_most(act, experts)
            for t in range(TT):
                act.activation(fin[:, t], x2[:, t], ACT.Square, accum_out=stat[:, 40 + t:41 + t]).then_inc(squares3, 1)

        @block.tensor
        def _(pe):
            pe.wait_ge(consts, 1)
            pe.wait_ge(par_loaded, 16 * 8)
            pe.transpose(ps[:, 7, 0:PARAM_ROWS], param_rows[:], ident[0:PARAM_ROWS, 0:PARAM_ROWS]).then_inc(param_turned, 1)
            pe.matmul(ps[0:A_HEADS, 6, 0:T], relb[:], onehot_s[:], start=True, stop=True).then_inc(rev_summed, 1)
            pe.wait_ge(param_ready, 1)
            pe.wait_ge(rev_ready, 1)
            for t in range(TT):
                pe.wait_ge(normed, t + 1)
            for g in range(DC // 2):
                for c in range(2):
                    for t in range(TT):
                        last = pe.transpose(ps[:, g, c * T + t * P:c * T + (t + 1) * P],
                                            xin[:, t, (2 * g + c) * P:(2 * g + c + 1) * P], ident[:])
                last.then_inc(turned, 1)

            def channel_half(banks, q, first, last_half):
                w = wsplit[:, q % 2]
                for b in range(2):
                    for k in range(HALF_K):
                        a = act_of(q, k)
                        pe.matmul(banks[b], w[:, k, 0, b * P:(b + 1) * P], a, start=first and k == 0,
                                  stop=False)
                        last = pe.matmul(banks[b][:, 0:T], w[:, k, 1, b * P:(b + 1) * P], a[:, 0],
                                         start=False, stop=last_half and k == HALF_K - 1)
                last.then_inc(used, 1)

            def act_of(q, k):
                return act_split[:, (q % 2) * HALF_K + k]

            def token_half(banks, q, first, last_half):
                w = wsplit[:, q % 2]
                for t in range(TT):
                    for k in range(HALF_K):
                        a = act_of(q, k)
                        pe.matmul(banks[t], a[:, 0, t * P:(t + 1) * P], w[:, k], start=first and k == 0,
                                  stop=False)
                        last = pe.matmul(banks[t][:, 0:UNIT], a[:, 1, t * P:(t + 1) * P], w[:, k, 0],
                                         start=False, stop=last_half and k == HALF_K - 1)
                last.then_inc(used, 1)

            def half(kind, q, half_no, unit_no):
                pe.wait_ge(split, half_no + 1)
                if q % 2 == 0 and unit_no is not None:
                    pe.wait_ge(acc_free, unit_no - 1)
                u = (q // 2) % 2
                kind([ps[:, 2 * u], ps[:, 2 * u + 1]], q, q % 2 == 0, q % 2 == 1)

            def stage(kind, unit, start, units):
                with pe.Fori(start, units // 2) as i:
                    for q in range(PAIR_HALVES):
                        half(kind, q, i * PAIR_HALVES + (2 * unit + q), i * 2 + (unit + q // 2))

            pe.wait_ge(bank_free, DC)
            for q in range(PAIR_HALVES):
                half(channel_half, q, q, None)
            stage(channel_half, 0, 1, UNITS_QK)

            pe.wait_ge(wif_ready, 1)
            for t in range(TT):
                out_if = ps[:, 4, t * 16:(t + 1) * 16]
                for k in range(DC):
                    pe.matmul(out_if, act_split[:, k, 0, t * P:(t + 1) * P], wif[:, k], start=k == 0, stop=False)
                    last = pe.matmul(out_if[:, 0:8], act_split[:, k, 1, t * P:(t + 1) * P], wif[:, k, 0],
                                     start=False, stop=k == DC - 1)
            last.then_inc(if_summed, 1)
            stage(channel_half, UNIT_QKA, 0, UNITS_QKA)

            pe.wait_ge(ls_ready, 1)
            pe.matmul(ps[:, 5, 0:4], upto[:], lst[:, 0], start=True, stop=True)
            pe.matmul(ps[:, 5, 4:8], ones[:], lst[:, 0], start=True, stop=False)
            pe.matmul(ps[:, 5, 4:8], upto[:], lst[:, 1], start=False, stop=True).then_inc(cum_summed, 1)
            stage(token_half, UNIT_VO, 0, UNITS_VO)
            pe.wait_ge(aa_ready, 1)
            for t in range(TT):
                last = pe.transpose(ps[0:M_HEADS, 6, t * P:(t + 1) * P], aa[:, t], ident[:])
            last.then_inc(aa_turned, 1)
            stage(token_half, UNIT_VA, 0, UNITS_VA)
            pe.wait_ge(aaT_ready, 1)
            for h in range(M_HEADS):
                last = pe.matmul(ps[:, 4 + h // 2, (h % 2) * T:(h % 2 + 1) * T], pick[:, h], aaT[:], start=True, stop=True)
            last.then_inc(aa_spread, 1)
            pe.wait_ge(negM_ready, 1)
            for t in range(TT):
                last = pe.transpose(ps[0:M_HEADS, 6, t * P:(t + 1) * P], negM[:, t], ident[:])
            last.then_inc(negM_turned, 1)
            pe.wait_ge(negMT_ready, 1)
            pe.wait_ge(flip_loaded, 16 * A_HEADS)

            with pe.Fori(0, M_HEADS) as i:
                def gate_half(q):
                    half(channel_half, q, i * 8 + (2 * UNIT_GATES + q), i * 4 + (UNIT_GATES + q // 2))

                gate_half(0)
                pe.wait_ge(staged, i + 1)
                pe.wait_ge(br_lo, i + 1)
                for a in range(2):
                    q_h, k_h, bias = qk_now[:, 4 + 2 * a], qk_now[:, 5 + 2 * a], bias_flipped[:, ds(i * 2 + a, 1)]
                    bank = ps[:, 4 + a]
                    pe.matmul(bank[:, 0:P], q_h[:, 0:P], k_h[:, 0:P], start=True, stop=False)
                    pe.matmul(bank[:, 0:P], flip[:], bias[:, 0, P:T], start=False, stop=True)
                    pe.matmul(bank[:, P:REV], q_h[:, P:T], k_h[:], start=True, stop=False)
                    pe.matmul(bank[:, P:REV], flip[:], bias[:, 0], start=False, stop=True).then_inc(logits, 1)
                for k in range(2):
                    pe.matmul(ps[:, 6, 0:T], qk_now[:, 2 + k, 0:P], qk_now[:, k], start=k == 0, stop=k == 1)
                for k in range(2):
                    pe.matmul(ps[:, 6, T:REV], qk_now[:, 2 + k, P:T], qk_now[:, k, P:T], start=k == 0, stop=k == 1)
                pe.matmul(ps[:, 7, 0:T], pick_now[:], negMT[:], start=True, stop=True).then_inc(scores, 1)
                for q in (1, 2, 3):
                    gate_half(q)
                for a in range(2):
                    pe.wait_ge(prob_ready, i * 2 + (a + 1))
                    for c in range(3):
                        last = pe.transpose(ps[:, 4 + a, c * P:(c + 1) * P], prob[:, a, c * P:(c + 1) * P], ident[:])
                    last.then_inc(prob_turned, 1)
                pe.wait_ge(scored_ready, i + 1)
                for t, parts in enumerate(([(0, 0)], [(1, 0), (2, 1)])):
                    for n, (c, s) in enumerate(parts):
                        s_t = scored[:, c * P:(c + 1) * P]
                        first, end = n == 0, n == len(parts) - 1
                        pe.matmul(ps[:, 6 + t, 0:M_DIM], s_t, v_now[:, 0, s], start=first, stop=end)
                    for n, (c, s) in enumerate(parts):
                        s_t = scored[:, c * P:(c + 1) * P]
                        first, end = n == 0, n == len(parts) - 1
                        last = pe.matmul(ps[:, 6 + t, M_DIM:M_DIM + 1], s_t, ones[:, 0:1], start=first, stop=end)
                last.then_inc(num_summed, 1)
                gate_half(4)
                gate_half(5)
                for a in range(2):
                    pe.wait_ge(probT_ready, i * 2 + (a + 1))
                    v_h = v_now[:, 1, :, a * P:(a + 1) * P]
                    pe.matmul(ps[:, 4 + a, 0:T], v_h[:, 0], probT[:, a, 0:T], start=True, stop=False)
                    pe.matmul(ps[:, 4 + a, P:T], v_h[:, 1], probT[:, a, T:REV], start=False, stop=True).then_inc(ha_summed, 1)
                pe.wait_ge(hm_ready, i + 1)
                for c in range(2):
                    for t in range(TT):
                        last = pe.transpose(ps[:, 6, c * T + t * P:c * T + (t + 1) * P], hm[:, t, c * P:(c + 1) * P], ident[:])
                last.then_inc(hm_turned, 1)
                gate_half(6)
                gate_half(7)

            pe.wait_ge(br_lo, M_HEADS + 1)
            with pe.Fori(0, UNITS_BRANCH // 2) as i:
                for q in range(PAIR_HALVES):
                    pe.wait_ge(split, i * PAIR_HALVES + (2 * UNIT_BRANCH + q + 1))
                    if q % 2 == 0:
                        pe.wait_ge(acc_free, i * 2 + (UNIT_BRANCH + q // 2 - 1))
                    w = wsplit[:, q % 2]
                    for b in range(2):
                        bank = ps[:, 4 * (1 - q // 2) + 2 * (q % 2) + b]
                        for k in range(HALF_K):
                            a = br_split[:, (q % 2) * HALF_K + k]
                            pe.matmul(bank, w[:, k, 0, b * P:(b + 1) * P], a, start=k == 0, stop=False)
                            last = pe.matmul(bank[:, 0:T], w[:, k, 1, b * P:(b + 1) * P], a[:, 0],
                                             start=False, stop=k == HALF_K - 1)
                    last.then_inc(used, 1)
            pe.wait_ge(y_ready, UNITS_BRANCH + 1)
            stage(token_half, UNIT_OUT, 0, UNITS_OUT)

            pe.wait_ge(h2n_ready, TT)
            h2n_v = h2n[:].rearrange("p t (q c) -> p t c q", c=DC)
            for g in range(DC // 2):
                for c in range(2):
                    for t in range(TT):
                        last = pe.transpose(ps[:, g, c * T + t * P:c * T + (t + 1) * P], h2n_v[:, t, 2 * g + c], ident[:])
                last.then_inc(h2_turned, 1)
            pe.wait_ge(h2T_ready, DC)
            pe.wait_ge(moe_par, 16 * 4)
            n_r = GROUPS + EXPERTS
            for t in range(TT):
                for c in range(DC):
                    last = pe.matmul(ps[:, 0, t * n_r:(t + 1) * n_r], h2T[:, c, t * P:(t + 1) * P], wrt[:, c],
                                     start=c == 0, stop=c == DC - 1)
            last.then_inc(routed, 1)
            pe.wait_ge(mk_ready, 1)
            pe.matmul(ps[:, 1, 0:32], before[:], mk[:, 0], start=True, stop=True)
            pe.matmul(ps[:, 1, 32:64], ones[:], mk[:, 0], start=True, stop=False)
            pe.matmul(ps[:, 1, 32:64], before[:], mk[:, 1], start=False, stop=True)
            pe.matmul(ps[:, 1, 64:96], ones[:], mk[:, 0], start=True, stop=False)
            pe.matmul(ps[:, 1, 64:96], ones[:], mk[:, 1], start=False, stop=True).then_inc(rank_summed, 1)
            pe.wait_ge(sel_ready, 1)
            for c in range(DC):
                if c >= 8:
                    pe.wait_ge((xg_act, xg_dve)[c % 2], (c - 8) // 2 + 1)
                for t in range(TT):
                    last = pe.matmul(ps[:, c % 8], h2n_v[:, t, c], sel[:, t], start=t == 0, stop=t == TT - 1)
                last.then_inc(xg_summed, 1)

            def hidden(i, s, b):
                pe.wait_ge(xe_ready, s * 2 + (b + 1))
                pe.wait_ge(w13_loaded[b], i * 32 + 32)
                pe.wait_ge(hid_ready, s * 2 + (b + 1))
                for k in range(DC):
                    for f in range(FC):
                        last = pe.matmul(
                            ps[f * SLOTS:(f + 1) * SLOTS, 0, 0:2 * P].rearrange("p (w f) -> p w f", w=2),
                            xe[:, b, k], w13[b][:, :, k, f * P:(f + 1) * P], start=k == 0, stop=k == DC - 1)
                last.then_inc(h_summed, 1)

            def turn(s, b):
                pe.wait_ge(hidT_ready, s * 2 + (b + 1))
                if b == 0:
                    pe.wait_ge(mixT_ready, s + 1)
                if b == 1:
                    pe.wait_ge(mix_ready, s + 1)
                    for t in range(TT):
                        last = pe.transpose(ps[:, 1, P + t * P:P + (t + 1) * P], mix[:, t], ident[:])
                    last.then_inc(mix_turned, 1)
                pe.wait_ge(hid_ready, s * 2 + (b + 2))
                pe.transpose(ps[:, 1, 0:P], hid[:], ident[:]).then_inc(hid_turned, 1)

            def rows(i, s):
                pe.wait_ge(hidT_ready, s * 2 + 3)
                for b in range(2):
                    pe.wait_ge(w2_loaded[b], i * 16 + 16)
                pe.wait_ge(ys_ready, s + 1)
                for n in range(4):
                    for f in range(FC):
                        for b in range(2):
                            last = pe.matmul(ps[b * SLOTS:(b + 1) * SLOTS, 2 + n],
                                             hidT[:, b, f * SLOTS:(f + 1) * SLOTS],
                                             w2s[b][:, f, n * 512:(n + 1) * 512], start=f == 0, stop=f == FC - 1)
                last.then_inc(y_summed, 1)

            def scatter(s, groups):
                for g in groups:
                    if g == 0:
                        pe.wait_ge(ys_ready, s + 2)
                        pe.wait_ge(mixT_ready, s + 2)
                    pe.wait_ge(added, s * GROUPS_OUT + max(1, g))
                    pe.matmul(ps[:, 6 + g % 2], mixT[:, g // 4 * P:(g // 4 + 1) * P],
                              ys[:, g % 4 * 512:(g % 4 + 1) * 512], start=True, stop=True).then_inc(scattered, 1)

            def experts(chunks):
                if chunks > 1:
                    with pe.Fori(0, EXPERTS // 2) as i:
                        with pe.Fori(0, chunks) as c:
                            s = i * chunks + c
                            for b in range(2):
                                hidden(i, s, b)
                                turn(s, b)
                            rows(i, s)
                            scatter(s, range(GROUPS_OUT))
                    return
                for b in range(2):
                    hidden(0, 0, b)
                    turn(0, b)
                rows(0, 0)
                with pe.Fori(1, EXPERTS // 2) as i:
                    hidden(i, i, 0)
                    scatter(i - 1, (0, 1, 2))
                    turn(i, 0)
                    hidden(i, i, 1)
                    scatter(i - 1, (3, 4, 5))
                    turn(i, 1)
                    scatter(i - 1, (6, 7))
                    rows(i, i)
                scatter(EXPERTS // 2 - 1, range(GROUPS_OUT))

            by_most(pe, experts)

        @block.vector
        def _(dve):
            steps = Steps(dve, dve_s)

            def split_half(q, half_no):
                dve.wait_ge(rounded, half_no + 1)
                dve.tensor_tensor(wsplit[:, q % 2, :, 1], wraw[:, q % RAW], wsplit[:, q % 2, :, 0].bitcast(F32),
                                  ALU.subtract).then_inc(split, 1)

            def split_ahead(u, unit, i):
                for q in (2 * u + 2, 2 * u + 3):
                    split_half(q, i * PAIR_HALVES + (2 * unit + q))

            def sum_halves(outs, banks):
                for o, bank in zip(outs, banks):
                    last = dve.tensor_reduce(o, halves_sum(bank), AX.X, ALU.add)
                last.then_inc(acc_free, 1)

            def rms(col, out_col, n, turn):
                dve.tensor_scalar(stat[:, out_col:out_col + n], stat[:, col:col + n], 1.0 / D, RMS_EPS,
                                  ALU.mult, ALU.add).then_inc(root_go, 1)
                dve.wait_ge(root_done, turn)

            dve.memset(rev[:, T:REV], MASKED)
            dve.memset(pre[:, :, 0:CONV - 1], 0.0)
            dve.wait_ge(squares, TT)
            rms(0, 2, TT, 1)
            for t in range(TT):
                dve.tensor_scalar(xin[:, t], xin[:, t], stat[:, 2 + t:3 + t], None, ALU.mult).then_inc(normed, 1)
            dve.wait_ge(param_turned, 1)
            dve.tensor_copy(params[:], ps[:, 7, 0:PARAM_ROWS]).then_inc(param_ready, 1)
            dve.wait_ge(rev_summed, 1)
            dve.tensor_copy(rev[:, 0:T], ps[0:A_HEADS, 6, 0:T]).then_inc(rev_ready, 1)
            dve.wait_ge(wif_hi, 1)
            dve.tensor_tensor(wif[:, :, 1], wif_raw[:], wif[:, :, 0].bitcast(F32), ALU.subtract).then_inc(wif_ready, 1)
            for q in range(2):
                split_half(q, q)
            dve.wait_ge(param_ready, 1)
            for c in range(DC):
                dve.wait_ge(hi_ready, c // 2 * 2 + 2)
                dve.scalar_tensor_tensor(act_split[:, c, 1], ps[:, c // 2, (c % 2) * T:(c % 2 + 1) * T],
                                         params[:, G1_ROW + c:G1_ROW + c + 1], act_split[:, c, 0].bitcast(F32),
                                         ALU.mult, ALU.subtract).then_inc(bank_free, 1)

            with steps.loop(0, UNITS_QK // 2, 2 * (CONV - 1)) as i:
                for u in range(2):
                    split_ahead(u, 0, i)
                    dve.wait_ge(used, i * PAIR_HALVES + (2 * u + 2))
                    sum_halves([pre[:, b, CONV - 1:] for b in range(2)], [ps[:, 2 * u + b] for b in range(2)])
                    dve.wait_ge(acc_free, i * 2 + (u + 1))
                    for j in range(CONV):
                        for b in range(2):
                            tap = params[:, ds(i * 4 + (CONV_ROW + j * DC + 2 * u + b), 1)]
                            moved = pre[:, b, j:j + T]
                            if j == 0:
                                last = dve.tensor_scalar(conv[:, b], moved, tap, None, ALU.mult)
                            else:
                                last = dve.scalar_tensor_tensor(conv[:, b], moved, tap, conv[:, b], ALU.mult, ALU.add)
                        if j < CONV - 1:
                            steps.done(last)
                    last.then_inc(conv_ready, 1)
                    dve.wait_ge(conv_sig, i * 2 + (u + 1))
                    dve.wait_ge(conv_ready, i * 2 + (u + 1))
                    to = (i % 2) * 8 + (i // 2) * 2 + 4 * u
                    dve.tensor_tensor(qk[:, ds(to, 2)], conv[:], csig[:], ALU.mult)

            dve.wait_ge(if_summed, 1)
            steps.done(dve.tensor_reduce(ifg[:], ps[:, 4, 0:32].rearrange("p (t a n) -> p t n a", t=TT, a=2), AX.X, ALU.add))
            steps.done(dve.tensor_tensor(ifg[:], ifg[:], ifb[:].unsqueeze(1).to_broadcast([P, TT, 2 * M_HEADS]), ALU.add))
            dve.scalar_tensor_tensor(lsg[:], ifg[:, :, M_HEADS:], -1.0, ifg[:, :, M_HEADS:], ALU.mult,
                                     ALU.max).then_inc(absf_ready, 1)
            dve.tensor_scalar(lst[:], ifg[:, :, M_HEADS:], 0.0, None, ALU.min)
            dve.wait_ge(expf_ready, 1)
            dve.tensor_scalar(lsg[:], lsg[:], 1.0, None, ALU.add).then_inc(onef_ready, 1)
            dve.wait_ge(lnf_ready, 1)
            dve.tensor_tensor(lst[:], lst[:], lsg[:], ALU.subtract).then_inc(ls_ready, 1)

            with dve.Fori(0, UNITS_QKA // 2) as i:
                for u in range(2):
                    split_ahead(u, UNIT_QKA, i)
                    dve.wait_ge(used, i * PAIR_HALVES + (2 * UNIT_QKA + 2 * u + 2))
                    sum_halves([qk[:, ds((i % 2) * 8 + i // 2 + (16 + 4 * u + 2 * b), 1)].rearrange("p a t -> p (a t)")
                                for b in range(2)],
                               [ps[:, 2 * u + b] for b in range(2)])

            dve.wait_ge(cum_summed, 1)
            steps.done(dve.tensor_copy(cum[:], ps[:, 5, 0:8].rearrange("p (t h) -> p t h", t=TT)))
            dve.tensor_tensor(aa[:], ifg[:, :, 0:M_HEADS], cum[:], ALU.subtract).then_inc(aa_ready, 1)

            tok_f = tok[:].rearrange("p k t n -> p (k t n)")

            def token_stage(unit, units, start_of):
                with dve.Fori(0, units // 2) as i:
                    for u in range(2):
                        split_ahead(u, unit, i)
                        dve.wait_ge(used, i * PAIR_HALVES + (2 * unit + 2 * u + 2))
                        sum_halves([tok_f[:, ds(start_of(i) + (t * M_WIDTH + u * UNIT), UNIT)] for t in range(TT)],
                                   [ps[:, 2 * u + t] for t in range(TT)])

            token_stage(UNIT_VO, UNITS_VO, lambda i: (i // 2) * (TT * M_WIDTH) + (i % 2) * (2 * UNIT))
            dve.wait_ge(aa_turned, 1)
            dve.tensor_copy(aaT[:], ps[0:M_HEADS, 6, 0:T]).then_inc(aaT_ready, 1)
            token_stage(UNIT_VA, UNITS_VA, lambda i: i * (2 * UNIT) + 2 * TT * M_WIDTH)

            dve.wait_ge(aa_spread, 1)
            mask_2 = mask_ts[:].unsqueeze(1).to_broadcast([P, 2, P])
            for n in range(2):
                rows = ps[:, 4 + n].rearrange("p (h s) -> p h s", h=2)
                dve.tensor_tensor(prob[:, :, 0:P], rows[:, :, 0:P], mask_2, ALU.add)
                steps.done(dve.tensor_tensor(prob[:, :, P:T], rows[:, :, P:T], mask_2, ALU.add))
                dve.tensor_reduce(negM[:, 0, 2 * n:2 * n + 2], prob[:, :, 0:P], AX.X, ALU.max)
                dve.tensor_reduce(negM[:, 1, 2 * n:2 * n + 2], prob[:, :, P:T], AX.X, ALU.max)
                steps.done(dve.tensor_reduce(stat[:, 50:52], rows[:, :, 0:P], AX.X, ALU.max))
                steps.done(dve.tensor_tensor(negM[:, 1, 2 * n:2 * n + 2], negM[:, 1, 2 * n:2 * n + 2], stat[:, 50:52], ALU.max))
            dve.tensor_scalar(negM[:], negM[:], 0.0, -1.0, ALU.max, ALU.mult).then_inc(negM_ready, 1)
            dve.wait_ge(negM_ready, 1)
            dve.tensor_tensor(expm[:], cum[:], negM[:], ALU.subtract).then_inc(mt_ready, 1)
            dve.wait_ge(negM_turned, 1)
            dve.tensor_copy(negMT[:], ps[0:M_HEADS, 6, 0:T]).then_inc(negMT_ready, 1)
            dve.wait_ge(expm_ready, 1)
            dve.wait_ge(o_ready, 1)

            with steps.loop(0, M_HEADS, 9) as i:
                def ahead(q):
                    split_half(q, i * 8 + (2 * UNIT_GATES + q))

                def gate_sums(n):
                    dve.wait_ge(used, i * 8 + (2 * UNIT_GATES + 2 * n + 2))
                    sum_halves([gates[:, ds(i * 8 + (2 * n + b), 1)].rearrange("p a t -> p (a t)") for b in range(2)],
                               [ps[:, 2 * (n % 2) + b] for b in range(2)])

                ahead(2)
                dve.wait_ge(scores, i + 1)
                dve.scalar_tensor_tensor(decay[:, 0:P], ps[:, 7, 0:P], aa[:, 0, ds(i, 1)], mask_st[:], ALU.add, ALU.add)
                dve.tensor_scalar(decay[:, P:T], ps[:, 7, P:T], aa[:, 0, ds(i, 1)], None, ALU.add)
                dve.scalar_tensor_tensor(decay[:, T:REV], ps[:, 7, P:T], aa[:, 1, ds(i, 1)], mask_st[:],
                                         ALU.add, ALU.add).then_inc(decay_arg, 1)
                for a in range(2):
                    dve.wait_ge(logits, i * 2 + (a + 1))
                    dve.tensor_reduce(stat[:, 8 + 2 * a:9 + 2 * a], ps[:, 4 + a, 0:P], AX.X, ALU.max, negate=True)
                    dve.tensor_reduce(stat[:, 9 + 2 * a:10 + 2 * a], ps[:, 4 + a, P:REV], AX.X, ALU.max,
                                      negate=True).then_inc(negmax, 1)
                ahead(3)
                gate_sums(0)
                dve.wait_ge(decay_exp, i + 1)
                dve.scalar_tensor_tensor(scored[:], ps[:, 6, 0:REV], float(M_DIM) ** -0.5, decay[:],
                                         ALU.mult, ALU.mult).then_inc(scored_ready, 1)
                dve.wait_ge(prob_exp, i * 2 + 2)
                steps.done(dve.reciprocal(stat[:, 16:20], stat[:, 12:16]))
                for a in range(2):
                    dve.tensor_scalar(prob[:, a, 0:P], prob[:, a, 0:P], stat[:, 16 + 2 * a:17 + 2 * a], None, ALU.mult)
                    dve.tensor_scalar(prob[:, a, P:REV], prob[:, a, P:REV], stat[:, 17 + 2 * a:18 + 2 * a], None,
                                      ALU.mult).then_inc(prob_ready, 1)
                ahead(4)
                ahead(5)
                gate_sums(1)
                for a in range(2):
                    dve.wait_ge(prob_turned, i * 2 + (a + 1))
                    dve.tensor_copy(probT[:, a], ps[:, 4 + a, 0:REV]).then_inc(probT_ready, 1)
                dve.wait_ge(num_summed, i + 1)
                for t in range(TT):
                    last = dve.tensor_scalar(stat[:, 32 + t:33 + t], ps[:, 6 + t, M_DIM:M_DIM + 1], -1.0,
                                             expm[:, t, ds(i, 1)], ALU.mult, ALU.max)
                steps.done(last)
                for t in range(TT):
                    last = dve.tensor_tensor(stat[:, 32 + t:33 + t], stat[:, 32 + t:33 + t],
                                             ps[:, 6 + t, M_DIM:M_DIM + 1], ALU.max)
                steps.done(last)
                steps.done(dve.reciprocal(stat[:, 34:36], stat[:, 32:34]))
                for t in range(TT):
                    last = dve.tensor_scalar(hm[:, t], ps[:, 6 + t, 0:M_DIM], stat[:, 34 + t:35 + t], None, ALU.mult)
                steps.done(last)
                for t in range(TT):
                    last = dve.bn_stats(bn[:, t], hm[:, t])
                steps.done(last)
                dve.tensor_tensor(mean_var[:, :, 0], bn[:, :, 1], bn[:, :, 4], ALU.add)
                dve.tensor_tensor(stat[:, 52:54], bn[:, :, 1], bn[:, :, 4], ALU.subtract)
                steps.done(dve.tensor_tensor(mean_var[:, :, 1], bn[:, :, 2], bn[:, :, 5], ALU.add))
                dve.tensor_scalar(mean_var[:, :, 0], mean_var[:, :, 0], 0.5, None, ALU.mult)
                dve.tensor_scalar(mean_var[:, :, 1], mean_var[:, :, 1], 1.0 / M_DIM, LN_EPS, ALU.mult, ALU.add)
                steps.done(dve.tensor_tensor(stat[:, 52:54], stat[:, 52:54], stat[:, 52:54], ALU.mult))
                dve.scalar_tensor_tensor(stat[:, 36:38], stat[:, 52:54], 0.25, mean_var[:, :, 1], ALU.mult,
                                         ALU.add).then_inc(root_go, 1)
                dve.wait_ge(root_done, i + 2)
                for t in range(TT):
                    last = dve.tensor_scalar(hm[:, t], hm[:, t], mean_var[:, t, 0:1], stat[:, 36 + t:37 + t],
                                             ALU.subtract, ALU.mult)
                steps.done(last)
                dve.tensor_tensor(hm[:], hm[:], tok[:, 1, :, ds(i * M_DIM, M_DIM)], ALU.mult).then_inc(hm_ready, 1)
                ahead(6)
                ahead(7)
                gate_sums(2)
                for a in range(2):
                    dve.wait_ge(br_hi, i * 4 + (a + 1))
                    to = br_split[:, ds(i * 2 + (8 + a), 1)]
                    dve.tensor_tensor(to[:, 0, 1], ps[:, 4 + a, 0:T], to[:, 0, 0].bitcast(F32), ALU.subtract)
                for c in range(2):
                    dve.wait_ge(br_hi, i * 4 + 4)
                    to = br_split[:, ds(i * 2 + c, 1)]
                    last = dve.scalar_tensor_tensor(to[:, 0, 1], ps[:, 6, c * T:(c + 1) * T],
                                                    params[:, ds(i * 2 + (MN_ROW + c), 1)], to[:, 0, 0].bitcast(F32),
                                                    ALU.mult, ALU.subtract)
                last.then_inc(br_lo, 1)
                ahead(8)
                ahead(9)
                gate_sums(3)

            with steps.loop(0, UNITS_BRANCH // 2, 2) as i:
                for u in range(2):
                    split_ahead(u, UNIT_BRANCH, i)
                    dve.wait_ge(used, i * PAIR_HALVES + (2 * UNIT_BRANCH + 2 * u + 2))
                    dve.wait_ge(y_ready, i * 2 + (u + 1))
                    sum_halves([bsum[:, g, b] for g in range(2) for b in range(2)],
                               [ps[:, 4 * (1 - u) + 2 * g + b] for g in range(2) for b in range(2)])
                    dve.wait_ge(acc_free, i * 2 + (UNIT_BRANCH + u + 1))
                    dve.wait_ge(gate_sig, i * 2 + (u + 1))
                    steps.done(dve.tensor_tensor(bsum[:], bsum[:], sgm[:], ALU.mult))
                    dve.tensor_tensor(bsum[:, 0], bsum[:, 0], bsum[:, 1], ALU.add).then_inc(y_sum, 1)
                    dve.wait_ge(y_hi, i * 2 + (u + 1))
                    to = act_split[:, ds(i * 4 + 2 * u, 2)]
                    dve.tensor_tensor(to[:, :, 1], bsum[:, 0], to[:, :, 0].bitcast(F32), ALU.subtract).then_inc(y_ready, 1)

            dve.wait_ge(x2_loaded, 16)

            def out_sums(i, u):
                dve.wait_ge(used, i * PAIR_HALVES + (2 * UNIT_OUT + 2 * u + 2))
                dve.wait_ge(x2_ready, i * 2 + (u + 1))
                sum_halves([osum[:, t] for t in range(TT)], [ps[:, 2 * u + t] for t in range(TT)])
                dve.wait_ge(acc_free, i * 2 + (UNIT_OUT + u + 1))
                cols = x2[:, :, ds(i * (2 * UNIT) + u * UNIT, UNIT)]
                dve.tensor_tensor(cols, cols, osum[:], ALU.add).then_inc(x2_ready, 1)

            with dve.Fori(0, UNITS_OUT // 2 - 1) as i:
                for u in range(2):
                    split_ahead(u, UNIT_OUT, i)
                    out_sums(i, u)
            split_half(2, HALVES - 2)
            split_half(3, HALVES - 1)
            out_sums(UNITS_OUT // 2 - 1, 0)
            out_sums(UNITS_OUT // 2 - 1, 1)
            dve.wait_ge(x2_ready, UNITS_OUT + 1)

            dve.memset(xg[:, :, PAIRS:], 0.0)
            dve.wait_ge(squares2, TT)
            rms(20, 22, TT, M_HEADS + 2)
            for t in range(TT):
                dve.tensor_scalar(h2n[:, t], x2[:, t], stat[:, 22 + t:23 + t], None, ALU.mult).then_inc(h2n_ready, 1)
            for g in range(1, DC // 2, 2):
                dve.wait_ge(h2_turned, g + 1)
                for c in range(2):
                    dve.tensor_scalar(h2T[:, 2 * g + c], ps[:, g, c * T:(c + 1) * T], g2T[:, 2 * g + c:2 * g + c + 1],
                                      None, ALU.mult).then_inc(h2T_ready, 1)

            dve.wait_ge(routed, 1)
            dve.wait_ge(iotas, 1)
            n_r = GROUPS + EXPERTS
            steps.done(dve.tensor_tensor(lr[:], ps[:, 0, 0:TT * n_r].rearrange("p (t n) -> p t n", t=TT),
                                         brt[:].unsqueeze(1).to_broadcast([P, TT, n_r]), ALU.add))

            def first_of(chosen, values, top, n):
                steps.done(dve.tensor_scalar(rt[:, 6, 0:n], values, top, None, ALU.is_ge))
                steps.done(dve.tensor_tensor(rt[:, 6, 0:n], rt[:, 6, 0:n], iota_e[:, 0:n], ALU.mult))
                steps.done(dve.tensor_reduce(stat[:, 30:31], rt[:, 6, 0:n], AX.X, ALU.min))
                steps.done(dve.tensor_scalar(chosen, iota_e[:, 0:n], stat[:, 30:31], None, ALU.is_equal))

            for t in range(TT):
                g_log, e_log = lr[:, t, 0:GROUPS], lr[:, t, GROUPS:]
                steps.done(dve.tensor_reduce(stat[:, 29:30], g_log, AX.X, ALU.max))
                dve.tensor_scalar(stat[:, 24:25], stat[:, 29:30], -1.0, None, ALU.mult).then_inc(gexp_go, 1)
                first_of(rt[:, 7, 0:GROUPS], g_log, stat[:, 29:30], GROUPS)
                steps.done(dve.tensor_scalar(rt[:, 5, 0:GROUPS], rt[:, 7, 0:GROUPS], -MASKED, MASKED, ALU.mult, ALU.add))
                steps.done(dve.tensor_tensor(rt[:, 2].rearrange("p (g e) -> p g e", g=GROUPS),
                                             e_log.rearrange("p (g e) -> p g e", g=GROUPS),
                                             rt[:, 5, 0:GROUPS].unsqueeze(2).to_broadcast([P, GROUPS, PER_GROUP]), ALU.add))
                steps.done(dve.tensor_reduce(stat[:, 26:27], rt[:, 2], AX.X, ALU.max))
                first_of(oh[:, t, 0], rt[:, 2], stat[:, 26:27], EXPERTS)
                steps.done(dve.scalar_tensor_tensor(rt[:, 2], oh[:, t, 0], 2 * MASKED, rt[:, 2], ALU.mult, ALU.add))
                steps.done(dve.tensor_reduce(stat[:, 31:32], rt[:, 2], AX.X, ALU.max))
                dve.tensor_tensor(stat[:, 27:28], stat[:, 31:32], stat[:, 26:27], ALU.subtract).then_inc(gexp_go, 1)
                first_of(oh[:, t, 1], rt[:, 2], stat[:, 31:32], EXPERTS)
                dve.wait_ge(gexp_done, 2 * t + 2)
                steps.done(dve.tensor_scalar(stat[:, 32:33], stat[:, 28:29], 1.0, stat[:, 25:26], ALU.add, ALU.mult))
                steps.done(dve.reciprocal(stat[:, 33:34], stat[:, 32:33]))
                steps.done(dve.tensor_tensor(stat[:, 34:35], stat[:, 33:34], stat[:, 28:29], ALU.mult))
                steps.done(dve.tensor_scalar(wt[:, t], oh[:, t, 0], stat[:, 33:34], None, ALU.mult))
                steps.done(dve.scalar_tensor_tensor(wt[:, t], oh[:, t, 1], stat[:, 34:35], wt[:, t], ALU.mult, ALU.add))
                last = dve.tensor_tensor(mk[:, t], oh[:, t, 0], oh[:, t, 1], ALU.add)
            last.then_inc(mk_ready, 1)
            dve.wait_ge(rank_summed, 1)
            dve.tensor_copy(rank[:], ps[:, 1, 0:64].rearrange("p (t e) -> p t e", t=TT))
            steps.done(dve.tensor_copy(rt[:, 0], ps[:, 1, 64:96]))
            dve.tensor_reduce(stat[:, 35:36], rt[:, 0], AX.X, ALU.max)
            steps.done(dve.tensor_copy(rt[:, 1], rt[:, 0]))
            at, shift = 1, 1
            while shift < EXPERTS:
                to = 3 if at != 3 else 4
                dve.tensor_copy(rt[:, to, 0:shift], rt[:, at, 0:shift])
                steps.done(dve.tensor_tensor(rt[:, to, shift:], rt[:, at, shift:], rt[:, at, 0:EXPERTS - shift], ALU.add))
                at, shift = to, 2 * shift
            steps.done(dve.tensor_tensor(rt[:, 5], rt[:, at], rt[:, 0], ALU.subtract))
            for c in range(CHUNKS):
                last = dve.tensor_scalar(starts[:, :, c], rt[:, 5], float(c * SLOTS), float(PAIRS), ALU.add, ALU.min)
            steps.done(last)
            dve.tensor_copy(starts_i[:], starts[0:1])
            dve.tensor_copy(most_i[:], stat[0:1, 35:36]).then_inc(tab_ready, 1)
            steps.done(dve.tensor_tensor(pos[:], rank[:], rt[:, 5:6].to_broadcast([P, TT, EXPERTS]), ALU.add))
            for k in range(2):
                last = dve.tensor_tensor(rt[:, 2 * k:2 * k + 2], oh[:, :, k], pos[:], ALU.mult)
            steps.done(last)
            steps.done(dve.tensor_reduce(stat[:, 44:48], rt[:, 0:4], AX.X, ALU.add))
            for t in range(TT):
                last = dve.tensor_scalar(sel[:, t], iota_s[:], stat[:, 44 + t:45 + t], None, ALU.is_equal)
            steps.done(last)
            for t in range(TT):
                last = dve.scalar_tensor_tensor(sel[:, t], iota_s[:], stat[:, 46 + t:47 + t], sel[:, t],
                                                ALU.is_equal, ALU.add)
            last.then_inc(sel_ready, 1)
            for c in range(1, DC, 2):
                dve.wait_ge(xg_summed, c + 1)
                dve.tensor_scalar(xg[:, c, 0:PAIRS], ps[:, c % 8], g2T[:, c:c + 1], None, ALU.mult).then_inc(xg_dve, 1)
            dve.wait_ge(xg_act, DC // 2)
            dve.wait_ge(xg_dve, DC // 2)

            steps_x = Steps(dve, dve_x)

            def tokens_in(i, c, s):
                for b in range(2):
                    at = dve.value_load(starts_i[0:1, ds(i * 2 + b, 1), ds(c, 1)], min_val=0, max_val=PAIRS)
                    dve.wait_ge(h_summed, s * 2 + 1)
                    dve.tensor_copy(xe[:, b], xg[:, :, ds(at, SLOTS)]).then_inc(xe_ready, 1)
                dve.wait_ge(mix_turned, s + 1)
                for b in range(2):
                    for t in range(TT):
                        last = dve.tensor_scalar(mix[:, t, b * SLOTS:(b + 1) * SLOTS],
                                                 iota_c[:, ds(c, 1)].rearrange("p c s -> p (c s)"),
                                                 rank[:, t, ds(i * 2 + b, 1)], wt[:, t, ds(i * 2 + b, 1)],
                                                 ALU.is_equal, ALU.mult)
                last.then_inc(mix_ready, 1)

            def silu(s, b):
                dve.wait_ge(sg_ready, s * 2 + (b + 1))
                dve.wait_ge(hid_turned, s * 2 + (b + 1))
                steps_x.done(dve.tensor_tensor(hid[:], sg[:], ps[:, 0, 0:P], ALU.mult))
                dve.tensor_tensor(hid[:], hid[:], ps[:, 0, P:2 * P], ALU.mult).then_inc(hid_ready, 1)

            def add(s, groups):
                for g in groups:
                    dve.wait_ge(scattered, s * GROUPS_OUT + (g + 2))
                    dve.wait_ge(added, s * GROUPS_OUT + 1)
                    cols = x2[:, g // 4, g % 4 * 512:(g % 4 + 1) * 512]
                    dve.tensor_tensor(cols, cols, ps[:, 6 + g % 2], ALU.add).then_inc(added, 1)

            def experts(chunks):
                steps_x.n = 0
                if chunks > 1:
                    with steps_x.loop(0, EXPERTS // 2, 2 * chunks) as i:
                        with steps_x.loop(0, chunks, 2) as c:
                            s = i * chunks + c
                            tokens_in(i, c, s)
                            for b in range(2):
                                silu(s, b)
                            add(s, range(GROUPS_OUT))
                else:
                    tokens_in(0, 0, 0)
                    for b in range(2):
                        silu(0, b)
                    with steps_x.loop(1, EXPERTS // 2, 2) as i:
                        tokens_in(i, 0, i)
                        silu(i, 0)
                        add(i - 1, (0, 1, 2))
                        silu(i, 1)
                        add(i - 1, (3, 4, 5, 6, 7))
                    add(EXPERTS // 2 - 1, range(GROUPS_OUT))
                dve.wait_ge(added, EXPERTS // 2 * chunks * GROUPS_OUT + 1)

            by_most(dve, experts)
            dve.wait_ge(squares3, TT)
            rms(40, 42, TT, M_HEADS + 3)
            dve.wait_ge(fing_loaded, 16)
            for t in range(TT):
                dve.scalar_tensor_tensor(fin[:, t], x2[:, t], stat[:, 42 + t:43 + t], fin_g[:], ALU.mult,
                                         ALU.mult).then_inc(out_ready, 1)


_INS = ["x", "norm1_g", "w_in", "conv_w", "if_bias", "mnorm_g", "w_branch_m", "w_branch_a", "w_out", "rel_bias",
        "norm2_g", "w_grp", "b_grp", "w_exp", "b_exp", "w1", "w3", "w2", "final_g"]


def kernel(**inputs):
    import numpy as _np
    import concourse.bacc as _bacc
    from concourse import mybir as _mybir
    from concourse.bass_utils import run_bass_kernel_spmd as _run

    nc = _bacc.Bacc("TRN2", target_bir_lowering=False, num_devices=1, dynamic_dma_scratch_size=1024)
    arrays, args = {}, []
    for name in _INS + ["onehot"]:
        a = _np.ascontiguousarray(bucket_onehot() if name == "onehot" else inputs[name])
        if name not in ("rel_bias", "final_g", "onehot"):
            a = a.reshape(a.shape[1:])
        arrays[f"in_{name}_dram"] = a
        args.append(nc.dram_tensor(f"in_{name}_dram", a.shape, _mybir.dt.from_np(a.dtype), kind="ExternalInput").ap())
    args.append(nc.dram_tensor("out_0_dram", (T, D), F32, kind="ExternalOutput").ap())
    layer(nc, *args)
    r = _run(nc, [arrays], core_ids=[0])
    return r.results[0]["out_0_dram"].reshape(1, T, D)
```

```python
from contextlib import ExitStack, contextmanager

import numpy as np

import concourse.bass as bass
from concourse import mybir

F32 = mybir.dt.float32
F32R = mybir.dt.float32r
I32 = mybir.dt.int32
ALU = mybir.AluOpType
ACT = mybir.ActivationFunctionType
AX = mybir.AxisListType
ds = bass.ds

P = 128
T = 256
TT = T // P
D = 2048
DC = D // P
M_HEADS, M_DIM = 4, 256
M_WIDTH = M_HEADS * M_DIM
A_HEADS, A_DIM = 8, 128
A_WIDTH = A_HEADS * A_DIM
CONV = 4
BUCKETS, MAX_DIST = 32, 128
GROUPS, PER_GROUP = 4, 8
EXPERTS = GROUPS * PER_GROUP
FF = 256
FC = FF // P
RMS_EPS, LN_EPS = 1e-6, 1e-5
MASKED = -1e30

COL_QK, COL_V, COL_O = 0, 2 * M_WIDTH, 3 * M_WIDTH
COL_IF = 4 * M_WIDTH
COL_QA = COL_IF + 2 * M_HEADS
COL_KA, COL_VA = COL_QA + A_WIDTH, COL_QA + 2 * A_WIDTH
COL_GATES = COL_VA + A_WIDTH

UNIT = 256
HALF_K = DC // 2
RAW = 4
PAIR_HALVES = 4

UNITS_QK = 2 * M_WIDTH // UNIT
UNITS_QKA = 2 * A_WIDTH // UNIT
UNITS_VO = 2 * M_WIDTH // UNIT
UNITS_VA = A_WIDTH // UNIT
UNITS_GATES = 2 * D // UNIT
UNITS_BRANCH = D // UNIT
UNITS_OUT = D // UNIT
UNIT_QKA = UNITS_QK
UNIT_VO = UNIT_QKA + UNITS_QKA
UNIT_VA = UNIT_VO + UNITS_VO
UNIT_GATES = UNIT_VA + UNITS_VA
UNIT_BRANCH = UNIT_GATES + UNITS_GATES
UNIT_OUT = UNIT_BRANCH + UNITS_BRANCH
UNITS = UNIT_OUT + UNITS_OUT
HALVES = 2 * UNITS

SLOTS = 64
PAIRS = 2 * T
CHUNKS = T // SLOTS
GROUPS_OUT = TT * D // 512
REV = 384

G1_ROW, CONV_ROW, MN_ROW = 0, DC, DC + CONV * DC
G2_ROW = MN_ROW + M_WIDTH // P
PARAM_ROWS = G2_ROW + DC


def bucket_onehot():
    n = np.arange(T)
    half = BUCKETS // 2
    large = half + (np.log(np.maximum(n, 1).astype(np.float32) / half)
                    / np.log(MAX_DIST / half) * (BUCKETS - half)).astype(np.int32)
    bucket = np.where(n < half, n, np.minimum(large, BUCKETS - 1))[::-1]
    return (np.arange(BUCKETS)[:, None] == bucket[None, :]).astype(np.float32)


class Steps:

    def __init__(self, eng, sem):
        self.eng, self.sem, self.n, self.loops = eng, sem, 0, []

    def done(self, ins):
        ins.then_inc(self.sem, 1)
        self.n += 1
        value = self.n
        for i, per in self.loops:
            value = i * per + value
        self.eng.wait_ge(self.sem, value)

    @contextmanager
    def loop(self, start, end, per):
        entered = self.n
        with self.eng.Fori(start, end) as i:
            self.n -= start * per
            self.loops.append((i, per))
            yield i
            self.loops.pop()
            assert self.n == entered - start * per + per, (self.n - entered + start * per, per)
        self.n = entered + (end - start) * per


def layer(nc, x, norm1_g, w_in, conv_w, if_bias, mnorm_g, w_branch_m, w_branch_a, w_out, rel_bias,
          norm2_g, w_grp, b_grp, w_exp, b_exp, w1, w3, w2, final_g, onehot, out):
    ctx = ExitStack()
    with ctx:
        place = {"at": 2048, "end": 229 * 1000}

        def sb(name, shape, dt=F32, at=None):
            size = int(np.prod(shape[1:])) * 4
            where = place["at"] if at is None else at
            if at is None:
                place["at"] += (size + 31) // 32 * 32
            assert where + size <= place["end"], (name, where + size)
            return nc.alloc_sbuf_tensor_at(name, shape, dt, offset=where)

        def sem(name):
            return ctx.enter_context(nc.semaphore(name))

        KB = 1024
        AT_TOK = place["at"]
        AT_ACT = AT_TOK + 24 * KB
        AT_WRAW = AT_ACT + 32 * KB
        AT_WSPLIT = AT_WRAW + 32 * KB
        AT_GATES = AT_WSPLIT + 32 * KB
        AT_QK = AT_GATES + 32 * KB
        AT_SMALL = AT_QK + 32 * KB
        place["at"] = AT_SMALL
        tok = sb("tok", [P, 3, TT, M_WIDTH], at=AT_TOK)
        act_split = sb("act_split", [P, DC, 2, T], F32R, at=AT_ACT)
        wraw = sb("wraw", [P, RAW, HALF_K, UNIT], at=AT_WRAW)
        wsplit = sb("wsplit", [P, 2, HALF_K, 2, UNIT], F32R, at=AT_WSPLIT)
        gates = sb("gates", [P, 2 * DC, T], at=AT_GATES)
        xin = sb("xin", [P, TT, D], at=AT_GATES)
        qk = sb("qk", [P, 32, T], at=AT_QK)
        br_split = sb("br_split", [P, DC, 2, T], F32R, at=AT_QK)
        x2 = sb("x2", [P, TT, D], at=AT_TOK)
        xg = sb("xg", [P, DC, PAIRS + SLOTS], at=AT_TOK + 16 * KB)
        w13 = [sb("w13_a", [P, 2, DC, FF], at=AT_GATES), sb("w13_b", [P, 2, DC, FF], at=AT_WRAW)]
        w2s = [sb("w2_a", [P, 2, FC, D], at=AT_GATES + 32 * KB), sb("w2_b", [P, 2, FC, D], at=AT_WRAW + 32 * KB)]
        h2n = sb("h2n", [P, TT, D], at=AT_QK + 16 * KB)
        h2lo = sb("h2lo", [P, TT, D], F32R, at=AT_QK + 16 * KB)
        h2hi = sb("h2hi", [P, TT, D], F32R, at=AT_WSPLIT + 16 * KB)
        fin = sb("fin", [P, TT, D], at=AT_TOK + 16 * KB)
        fin_g = sb("fin_g", [P, D], at=AT_TOK + 32 * KB)
        x2g = sb("x2g", [P, TT, D], at=AT_GATES)

        ident = sb("ident", [P, P])
        flip = sb("flip", [P, P])
        ones = sb("ones", [P, P])
        upto = sb("upto", [P, P])
        before = sb("before", [P, P])
        mask_ts = sb("mask_ts", [P, P])
        mask_st = sb("mask_st", [P, P])
        params = sb("params", [P, PARAM_ROWS])
        g2T = sb("g2T", [P, DC])
        stat = sb("stat", [P, 64])
        power = sb("power", [P, TT])
        AT_PHASE = place["at"]

        pick = sb("pick", [M_HEADS, M_HEADS, P])
        ifb = sb("ifb", [P, 2 * M_HEADS])
        relb = sb("relb", [BUCKETS, A_HEADS])
        ifg = sb("ifg", [P, TT, 2 * M_HEADS])
        lsg = sb("lsg", [P, TT, M_HEADS])
        lst = sb("lst", [P, TT, M_HEADS])
        cum = sb("cum", [P, TT, M_HEADS])
        aa = sb("aa", [P, TT, M_HEADS])
        aaT = negMT = sb("row_by_head", [M_HEADS, T])
        negM = sb("negM", [P, TT, M_HEADS])
        pick_now = sb("pick_now", [M_HEADS, P])
        bn = sb("bn", [P, TT, 6])
        mean_var = sb("mean_var", [P, TT, 2])
        expm = sb("expm", [P, TT, M_HEADS])
        AT_CONV = place["at"]
        bias_flipped = sb("bias_flipped", [P, A_HEADS, T])
        qk_now = sb("qk_now", [P, 8, T])
        v_now = sb("v_now", [P, 2, TT, M_DIM])
        decay = scored = sb("decay", [P, REV])
        prob = probT = sb("prob", [P, 2, REV])
        hm = sb("hm", [P, TT, M_DIM])
        AT_EARLY = AT_CONV + 20 * KB
        param_rows = sb("param_rows", [PARAM_ROWS, P], at=AT_EARLY)
        wif_raw = sb("wif_raw", [P, DC, 2 * M_HEADS], at=AT_EARLY + 512)
        wif = sb("wif", [P, DC, 2, 2 * M_HEADS], F32R, at=AT_EARLY + 1024)
        onehot_s = sb("onehot_s", [BUCKETS, T], at=AT_EARLY + 2048)
        rev = sb("rev", [A_HEADS, REV], at=AT_EARLY + 3072)
        pre = sb("pre", [P, 2, T + CONV - 1], at=AT_CONV + 8 * KB)
        conv = sb("conv", [P, 2, 2, T], at=AT_CONV + 11 * KB)
        csig = sb("csig", [P, 2, T], at=AT_CONV + 16 * KB)
        bsum = sb("bsum", [P, 2, 2, T], at=AT_CONV + 4 * KB)
        osum = sb("osum", [P, TT, UNIT], at=AT_CONV + 8 * KB)
        sqs = sb("sqs", [P, TT, UNIT], at=AT_CONV + 10 * KB)
        x2u = sb("x2u", [P, 2, TT, UNIT], at=AT_CONV + 12 * KB)
        x2T = sb("x2T", [P, 2, 2, T], at=AT_CONV + 16 * KB)
        xsq = sb("xsq", [P, TT, D], at=AT_QK)

        place["at"] = AT_PHASE
        wrt = sb("wrt", [P, DC, GROUPS + EXPERTS])
        brt = sb("brt", [P, GROUPS + EXPERTS])
        sq2 = sb("sq2", [P, TT, UNITS_OUT])
        lr = sb("lr", [P, TT, GROUPS + EXPERTS])
        iota_e = sb("iota_e", [P, EXPERTS])
        iota_s = sb("iota_s", [P, PAIRS])
        iota_c = sb("iota_c", [P, CHUNKS, SLOTS])
        assert place["at"] - 3 * KB - 256 < AT_CONV, "what is written while w_out streams"
        rt = sb("rt", [P, 5, TT, EXPERTS])
        sc = sb("sc", [P, 12, TT])
        table = sb("table", [P, 6, EXPERTS])
        oh = sb("oh", [P, TT, 2, EXPERTS])
        mk = sb("mk", [P, TT, EXPERTS])
        wt = sb("wt", [P, TT, EXPERTS])
        rank = sb("rank", [P, TT, EXPERTS])
        pos = sb("pos", [P, TT, EXPERTS])
        starts = sb("starts", [P, EXPERTS, CHUNKS])
        starts_i = sb("starts_i", [1, EXPERTS, CHUNKS], I32)
        most_i = sb("most_i", [1, 1], I32)
        AT_SEL = place["at"]
        sel = sb("sel", [P, TT, PAIRS], F32R)
        place["at"] = AT_SEL
        xe = sb("xe", [P, 2, DC, SLOTS])
        mix = sb("mix", [P, TT, P])
        mixT = sb("mixT", [P, T])
        sg = sb("sg", [P, P])
        hid = sb("hid", [P, P])
        hidT = sb("hidT", [P, 2, P])
        ys = sb("ys", [P, D])

        ps = ctx.enter_context(nc.psum_tensor("ps", [P, 8, 512], F32))
        rev_dram = nc.dram_tensor("rev_dram", (A_HEADS, REV), F32, kind="Internal").ap()

        x_loaded = [sem("x_loaded_0"), sem("x_loaded_1")]
        par_loaded, consts = sem("par_loaded"), sem("consts_ready")
        raw_loaded = [sem(f"raw_loaded{i}") for i in range(RAW)]
        rounded, split, used, acc_free = sem("rounded"), sem("split"), sem("used"), sem("acc_free")
        dve_s, act_s, pool_s = sem("dve_step"), sem("act_step"), sem("pool_step")
        squares, normed, turned, hi_ready, bank_free = (sem(n) for n in (
            "squares", "normed", "turned", "hi_ready", "bank_free"))
        param_turned, param_ready, wif_hi, wif_ready = (sem(n) for n in (
            "param_turned", "param_ready", "wif_hi", "wif_ready"))
        rev_summed, rev_ready, rev_stored, flip_loaded = (sem(n) for n in (
            "rev_summed", "rev_ready", "rev_stored", "bias_flipped_loaded"))
        conv_ready, conv_sig, first_tap, silu_done = (sem(n) for n in (
            "conv_ready", "conv_sigmoid", "first_tap", "silu_done"))
        if_summed, absf_ready, expf_ready, onef_ready, lnf_ready, ls_ready, cum_summed, aa_ready = (
            sem(n) for n in ("if_summed", "absf_ready", "expf_ready", "onef_ready", "lnf_ready",
                             "ls_ready", "cum_summed", "aa_ready"))
        aa_turned, aaT_ready, aa_spread, negM_ready, negM_turned, negMT_ready, mt_ready, expm_ready = (
            sem(n) for n in ("aa_turned", "aaT_ready", "aa_spread", "negM_ready", "negM_turned",
                             "negMT_ready", "mt_ready", "expm_ready"))
        o_ready, staged = sem("o_sigmoid_ready"), sem("staged")
        logits, scores, decay_arg, decay_exp = (sem(n) for n in (
            "logits_summed", "scores_summed", "decay_arg", "decay_exp"))
        negmax, prob_exp, prob_ready, scored_ready = (sem(n) for n in (
            "negmax_ready", "prob_exp", "prob_ready", "scored_ready"))
        prob_turned, num_summed, probT_ready, hm_ready, ha_summed, hm_turned, br_hi, br_lo = (
            sem(n) for n in ("prob_turned", "num_summed", "probT_ready", "hm_ready", "ha_summed",
                             "hm_turned", "branch_hi", "branch_lo"))
        root_go, root_done, gate_sig, y_sum, y_hi, y_ready = (sem(n) for n in (
            "root_go", "root_done", "gate_sigmoid", "y_sum", "y_hi", "y_ready"))
        x2_loaded, x2_ready, moe_par, iotas = (sem(n) for n in (
            "x2_loaded", "x2_ready", "expert_params_loaded", "iotas_ready"))
        squares2, x2_turned, x2T_ready, routed, wrt_ready = (sem(n) for n in (
            "squares2", "x2_turned", "x2T_ready", "router_summed", "router_weights_ready"))
        h2hi_ready, h2lo_ready = sem("h2hi_ready"), sem("h2lo_ready")
        gexp_go, gexp_done, mk_ready, rank_summed, sel_ready, xg_summed, xg_act, xg_dve, tab_ready = (
            sem(n) for n in ("group_exp_go", "group_exp_done", "chosen_ready", "rank_summed",
                             "selection_ready", "gathered", "gathered_even", "gathered_odd",
                             "table_ready"))
        w13_loaded = [sem("w13a_loaded"), sem("w13b_loaded")]
        w2_loaded = [[sem(f"w2_loaded{slot}_{side}") for side in ("left", "right")] for slot in range(2)]
        xe_ready, h_summed, sg_ready, hid_ready, hid_turned, hidT_ready, y_summed, ys_ready = (
            sem(n) for n in ("xe_ready", "hidden_summed", "hidden_sigmoid", "hid_ready", "hid_turned",
                             "hidT_ready", "ye_summed", "ye_ready"))
        mix_ready, mix_turned, mixT_ready, scattered, added = (sem(n) for n in (
            "mix_ready", "mix_turned", "mixT_ready", "scattered", "added"))
        fing_loaded, squares3, final_root, out_stored, x2g_ready = (sem(n) for n in (
            "final_g_loaded", "squares3", "final_root", "out_stored", "x2g_ready"))
        out_ready = [sem("out_ready_0"), sem("out_ready_1")]
        dve_x = sem("dve_expert_step")

        win_v = w_in.rearrange("(h k p) n -> p h k n", h=2, p=P)
        wout_v = w_out.rearrange("(h k p) n -> p h k n", h=2, p=P)
        wbm_v = w_branch_m.rearrange("(k p) n -> p k n", p=P)
        wba_v = w_branch_a.rearrange("(k p) n -> p k n", p=P)
        x_v = x.rearrange("(t p) d -> p t d", p=P)
        out_v = out.rearrange("(t p) d -> p t d", p=P)
        w1_v = w1.rearrange("e (p c) f -> p e c f", c=DC)
        w3_v = w3.rearrange("e (p c) f -> p e c f", c=DC)
        w2_v = w2.rearrange("e (j p) n -> p e j n", p=P)

        def group_place(g):
            return g % 4 // 2, g // 4 * 2 + g % 2

        def halves_sum(bank):
            return bank.rearrange("p (a n) -> p n a", a=2)

        def by_most(eng, experts):
            eng.wait_ge(tab_ready, 1)
            most = eng.value_load(most_i[0:1, 0:1], min_val=0, max_val=T)
            with eng.If(most < SLOTS + 1):
                experts(1)
            with eng.Else():
                experts(CHUNKS)
            eng.end_ifs()

        @contextmanager
        def passes(eng, chunks, steps=None, per=0):
            if chunks == 1:
                yield 0
            elif steps is None:
                with eng.Fori(0, chunks) as c:
                    yield c
            else:
                with steps.loop(0, chunks, per) as c:
                    yield c

        block = ctx.enter_context(nc.Block())

        @block.sync
        def _(sp):
            for t in range(TT):
                sp.dma_start(xin[:, t], x_v[:, t]).then_inc(x_loaded[t], 16)
            sp.wait_ge(par_loaded, 16 * 9)

            def load(slot, src, half):
                if half is not None:
                    sp.wait_ge(split, half + (1 - RAW))
                sp.dma_start(wraw[:, slot], src).then_inc(raw_loaded[slot], 16)

            def pair(col, half):
                for q in range(PAIR_HALVES):
                    load(q, win_v[:, q % 2, :, ds(col + (q // 2) * UNIT, UNIT)],
                         None if half is None else half + q)

            def pairs(start, units, col, unit):
                with sp.Fori(start, units // 2) as i:
                    pair(i * (2 * UNIT) + col, i * PAIR_HALVES + 2 * unit)

            pair(COL_QK, None)
            pairs(1, UNITS_QK, COL_QK, 0)
            pairs(0, UNITS_QKA, COL_QA, UNIT_QKA)
            pairs(0, UNITS_VO, COL_V, UNIT_VO)
            pairs(0, UNITS_VA, COL_VA, UNIT_VA)
            pairs(0, UNITS_GATES, COL_GATES, UNIT_GATES)
            with sp.Fori(0, UNITS_BRANCH // 2) as i:
                for q in range(PAIR_HALVES):
                    load(q, (wbm_v, wba_v)[q % 2][:, :, ds(i * (2 * UNIT) + (q // 2) * UNIT, UNIT)],
                         i * PAIR_HALVES + 2 * UNIT_BRANCH + q)
            sp.wait_ge(br_lo, M_HEADS + 1)
            sp.dma_start(x2[:], x_v).then_inc(x2_loaded, 16)
            for q in range(PAIR_HALVES):
                load(q, wout_v[:, q // 2, :, (q % 2) * UNIT:(q % 2 + 1) * UNIT], 2 * UNIT_OUT + q)
            with sp.Fori(1, UNITS_OUT // 2) as i:
                for q in range(PAIR_HALVES):
                    load(q, wout_v[:, q % 2, :, ds(i * (2 * UNIT) + (q // 2) * UNIT, UNIT)],
                         i * PAIR_HALVES + 2 * UNIT_OUT + q)

            def load_hidden(b, e):
                sp.dma_start(w13[b][:, 0], w1_v[:, e]).then_inc(w13_loaded[b], 16)
                sp.dma_start(w13[b][:, 1], w3_v[:, e]).then_inc(w13_loaded[b], 16)

            def load_rows(slot, e_of):
                for h in range(2):
                    cols = slice(h * (D // 2), (h + 1) * (D // 2))
                    for b in range(2):
                        sp.dma_start(w2s[b][:, slot, :, cols],
                                     w2_v[:, e_of(b), :, cols]).then_inc(w2_loaded[slot][h], 16)

            sp.wait_ge(y_ready, UNITS_BRANCH + 1)
            load_hidden(0, 0)
            sp.wait_ge(used, HALVES)
            load_hidden(1, 1)
            load_rows(0, lambda b: b)
            sp.wait_ge(xg_summed, DC)
            load_rows(1, lambda b: b + 2)

            def experts(chunks):
                def next_hidden(i):
                    for b in range(2):
                        sp.wait_ge(h_summed, i * (2 * chunks) + (2 * chunks + b))
                        load_hidden(b, ds(i * 2 + (b + 2), 1))

                next_hidden(0)
                with sp.Fori(0, EXPERTS // 4 - 1) as j:
                    for slot in range(2):
                        i = j * 2 + (slot + 1)
                        next_hidden(i)
                        sp.wait_ge(y_summed, i * (2 * chunks) + 1)
                        load_rows(slot, lambda b: ds(i * 2 + (b + 2), 1))
                sp.wait_ge(xe_ready, EXPERTS * chunks)
                sp.dma_start(fin_g[:], final_g.partition_broadcast(P)).then_inc(fing_loaded, 16)

            by_most(sp, experts)
            for h in range(2):
                for t in range(TT):
                    cols = slice(h * (D // 2), (h + 1) * (D // 2))
                    sp.wait_ge(out_ready[t], h + 1)
                    sp.dma_start(out_v[:, t, cols], fin[:, t, cols]).then_inc(out_stored, 16)
            sp.wait_ge(out_stored, 16 * 2 * TT)

        @block.gpsimd
        def _(pool):
            steps = Steps(pool, pool_s)
            for primed in (silu_done, hm_turned, ha_summed, br_lo, y_sum, y_ready, x2_ready, h_summed, mix_turned, hid_turned,
                           hid_ready, hidT_ready, mixT_ready, y_summed, ys_ready, scattered, added):
                pool.sem_inc(primed, 1)
            for m in (ident, flip, before, mask_ts, mask_st, pick):
                last = pool.memset(m[:], 0.0)
            pool.memset(upto[:], 1.0)
            pool.memset(power[:], -0.5)
            steps.done(pool.memset(ones[:], 1.0))

            def choose(m, keep, fill, base, pattern, mult):
                return pool.affine_select(out=m[:], in_=m[:], compare_op=keep, fill=fill, base=base,
                                          pattern=pattern, channel_multiplier=mult)

            choose(ident, ALU.not_equal, 1.0, 0, [[-1, P]], 1)
            choose(flip, ALU.not_equal, 1.0, -(P - 1), [[1, P]], 1)
            choose(upto, ALU.is_ge, 0.0, 0, [[1, P]], -1)
            choose(before, ALU.is_ge, 1.0, 0, [[-1, P]], 1)
            choose(mask_ts, ALU.is_ge, MASKED, 0, [[-1, P]], 1)
            choose(mask_st, ALU.is_ge, MASKED, 0, [[1, P]], -1)
            choose(pick, ALU.not_equal, 1.0, 0, [[-1, M_HEADS], [0, P]], 1).then_inc(consts, 1)

            def root(col, n, turn):
                pool.wait_ge(root_go, turn)
                pool.tensor_tensor(stat[:, col:col + n], stat[:, col:col + n], power[:, 0:n], ALU.pow).then_inc(root_done, 1)

            root(2, TT, 1)
            pool.wait_ge(acc_free, UNIT_GATES)
            with steps.loop(0, M_HEADS, 1) as i:
                pool.wait_ge(hm_turned, i + 1)
                pool.wait_ge(ha_summed, i * 2 + 1)
                pool.tensor_copy(pick_now[:], pick[:, ds(i, 1)])
                pool.tensor_copy(qk_now[:, 0:4], qk[:, ds(i * 4, 4)])
                steps.done(pool.tensor_copy(qk_now[:, 4:8], qk[:, ds(i * 4 + 16, 4)]))
                q_now = qk_now[:, 4:8].rearrange("p (a k) t -> p a k t", k=2)[:, :, 0]
                pool.tensor_copy(v_now[:, 0], tok[:, 0, :, ds(i * M_DIM, M_DIM)])
                pool.tensor_scalar(q_now, q_now, float(A_DIM) ** -0.5, None, ALU.mult)
                pool.tensor_copy(v_now[:, 1], tok[:, 2, :, ds(i * M_DIM, M_DIM)]).then_inc(staged, 1)
                root(36, 2, i + 2)

            pool.wait_ge(x2_ready, UNITS_OUT + 1)
            pool.iota(iota_e[:], pattern=[[1, EXPERTS]], base=-SLOTS, channel_multiplier=0,
                      allow_small_or_imprecise_dtypes=True)
            pool.iota(iota_s[:], pattern=[[1, PAIRS]], base=0, channel_multiplier=0,
                      allow_small_or_imprecise_dtypes=True)
            pool.iota(iota_c[:], pattern=[[SLOTS, CHUNKS], [1, SLOTS]], base=0,
                      channel_multiplier=0, allow_small_or_imprecise_dtypes=True).then_inc(iotas, 1)
            root(22, TT, M_HEADS + 2)
            for t in range(TT):
                pool.wait_ge(h2hi_ready, t + 1)
                pool.tensor_tensor(h2lo[:, t], h2n[:, t], h2hi[:, t].bitcast(F32), ALU.subtract).then_inc(h2lo_ready, 1)
            root(42, TT, M_HEADS + 3)

        @block.scalar
        def _(act):
            steps = Steps(act, act_s)
            act.dma_start(param_rows[G1_ROW:CONV_ROW], norm1_g.rearrange("(r c) -> r c", c=P)).then_inc(par_loaded, 16)
            act.dma_start(param_rows[CONV_ROW:MN_ROW], conv_w.rearrange("j (r c) -> (j r) c", c=P)).then_inc(par_loaded, 16)
            act.dma_start(param_rows[MN_ROW:G2_ROW], mnorm_g.rearrange("(r c) -> r c", c=P)).then_inc(par_loaded, 16)
            act.dma_start(param_rows[G2_ROW:PARAM_ROWS], norm2_g.rearrange("(r c) -> r c", c=P)).then_inc(par_loaded, 16)
            act.dma_start(wif_raw[:], w_in[:, COL_IF:COL_QA].rearrange("(k p) n -> p k n", p=P)).then_inc(par_loaded, 16)
            act.dma_start(ifb[:], if_bias.partition_broadcast(P)).then_inc(par_loaded, 16)
            act.dma_start(relb[:], rel_bias).then_inc(par_loaded, 16)
            act.dma_start(onehot_s[:], onehot).then_inc(par_loaded, 16)
            act.dma_start(g2T[:], norm2_g.rearrange("(p c) -> p c", c=DC)).then_inc(par_loaded, 16)

            for t in range(TT):
                act.wait_ge(x_loaded[t], 16)
                act.activation(xsq[:, t], xin[:, t], ACT.Square, accum_out=stat[:, t:t + 1]).then_inc(squares, 1)
            act.wait_ge(par_loaded, 16 * 9)
            act.activation(wif[:, :, 0], wif_raw[:], ACT.Copy).then_inc(wif_hi, 1)

            def round_half(q, turn, half):
                act.wait_ge(raw_loaded[q % RAW], turn)
                if half is not None:
                    act.wait_ge(used, half - 1)
                act.activation(wsplit[:, q % 2, :, 0], wraw[:, q % RAW], ACT.Copy).then_inc(rounded, 1)

            def round_ahead(u, unit, i, last=False):
                for q in (2 * u + 2, 2 * u + 3):
                    round_half(q, i * 16 + (16 * (unit // 2 + q // RAW) + 16),
                               i * PAIR_HALVES + (2 * unit + q))

            for g in range(DC // 2):
                if g % (DC // 4) == 0:
                    round_half(g // (DC // 4), 16, None)
                    act.wait_ge(param_ready, 1)
                act.wait_ge(turned, g + 1)
                for c in range(2):
                    act.activation(act_split[:, 2 * g + c, 0], ps[:, g, c * T:(c + 1) * T], ACT.Copy,
                                   scale=params[:, G1_ROW + 2 * g + c:G1_ROW + 2 * g + c + 1]).then_inc(hi_ready, 1)
            act.wait_ge(rev_ready, 1)
            act.dma_start(rev_dram, rev[:]).then_inc(rev_stored, 16)
            act.wait_ge(rev_stored, 16)
            for h in range(A_HEADS):
                act.dma_start(bias_flipped[:, h], bass.AP(tensor=rev_dram.tensor, offset=h * REV, ap=[[1, P], [1, T]])).then_inc(flip_loaded, 16)

            def round_one(unit, q, i):
                round_half(q, i * 16 + (16 * (unit // 2 + q // RAW) + 16), i * PAIR_HALVES + (2 * unit + q))

            def conv_sigmoid(u, n):
                act.wait_ge(conv_ready, n + 1)
                act.wait_ge(silu_done, n + 1)
                act.activation(csig[:], conv[:, u], ACT.Sigmoid).then_inc(conv_sig, 1)

            def conv_pair(i):
                for u in range(2):
                    n = i * 2 + u
                    round_one(0, 2 * u + 3, i)
                    if u == 1 or not isinstance(i, int) or i > 0:
                        conv_sigmoid(1 - u, n - 1)
                    if not (isinstance(i, int) and i > 0 and u == 1):
                        round_one(0, 2 * u + 4, i)
                    act.wait_ge(acc_free, n + 1)
                    for b in range(2):
                        last = act.activation(conv[:, u, b], pre[:, b, 0:T], ACT.Copy,
                                              scale=params[:, ds(i * 4 + (CONV_ROW + 2 * u + b), 1)])
                    last.then_inc(first_tap, 1)

            round_one(0, 2, 0)
            conv_pair(0)
            with act.Fori(1, UNITS_QK // 2 - 1) as i:
                conv_pair(i)
            conv_pair(UNITS_QK // 2 - 1)
            conv_sigmoid(1, UNITS_QK - 1)
            act.wait_ge(absf_ready, 1)
            act.activation(lsg[:], lsg[:], ACT.Exp, scale=-1.0).then_inc(expf_ready, 1)
            act.wait_ge(onef_ready, 1)
            act.activation(lsg[:], lsg[:], ACT.Ln).then_inc(lnf_ready, 1)
            for unit, units in ((UNIT_QKA, UNITS_QKA), (UNIT_VO, UNITS_VO)):
                with act.Fori(0, units // 2) as i:
                    for u in range(2):
                        round_ahead(u, unit, i)
            act.wait_ge(acc_free, UNIT_VA)
            act.activation(tok[:, 1], tok[:, 1], ACT.Sigmoid).then_inc(o_ready, 1)
            with act.Fori(0, UNITS_VA // 2) as i:
                for u in range(2):
                    round_ahead(u, UNIT_VA, i)
            act.wait_ge(mt_ready, 1)
            act.activation(expm[:], expm[:], ACT.Exp, scale=-1.0).then_inc(expm_ready, 1)

            with act.Fori(0, M_HEADS) as i:
                def ahead(q):
                    round_half(q, i * 32 + (16 * (UNIT_GATES // 2 + q // RAW) + 16),
                               i * 8 + (2 * UNIT_GATES + q))

                ahead(2)
                act.wait_ge(decay_arg, i + 1)
                act.activation(decay[:], decay[:], ACT.Exp).then_inc(decay_exp, 1)
                for a in range(2):
                    act.wait_ge(negmax, i * 2 + (a + 1))
                    act.activation(prob[:, a, 0:P], ps[:, 4 + a, 0:P], ACT.Exp,
                                   bias=stat[:, 8 + 2 * a:9 + 2 * a], accum_out=stat[:, 12 + 2 * a:13 + 2 * a])
                    act.activation(prob[:, a, P:REV], ps[:, 4 + a, P:REV], ACT.Exp,
                                   bias=stat[:, 9 + 2 * a:10 + 2 * a],
                                   accum_out=stat[:, 13 + 2 * a:14 + 2 * a]).then_inc(prob_exp, 1)
                for q in range(3, 8):
                    ahead(q)
                for a in range(2):
                    act.wait_ge(ha_summed, i * 2 + (a + 2))
                    act.activation(br_split[:, ds(i * 2 + (8 + a), 1), 0], ps[:, 4 + a, 0:T], ACT.Copy).then_inc(br_hi, 1)
                act.wait_ge(hm_turned, i + 2)
                for c in range(2):
                    act.activation(br_split[:, ds(i * 2 + c, 1), 0], ps[:, 6, c * T:(c + 1) * T], ACT.Copy,
                                   scale=params[:, ds(i * 2 + (MN_ROW + c), 1)]).then_inc(br_hi, 1)
                ahead(8)
                ahead(9)
                act.wait_ge(acc_free, i * 4 + (UNIT_GATES + 4))
                act.activation(gates[:, ds(i * 8, 8)], gates[:, ds(i * 8, 8)], ACT.Sigmoid).then_inc(gate_sig, 1)

            round_one(UNIT_BRANCH, 2, 0)

            def y_round(n):
                act.wait_ge(y_sum, n + 2)
                act.activation(act_split[:, ds(n * 2, 2), 0], bsum[:, 0], ACT.Copy).then_inc(y_hi, 1)

            def branch_pair(i):
                for u in range(2):
                    round_one(UNIT_BRANCH, 2 * u + 3, i)
                    if u == 1 or not isinstance(i, int):
                        y_round(i * 2 + (u - 1))
                    round_one(UNIT_BRANCH, 2 * u + 4, i)

            branch_pair(0)
            with act.Fori(1, UNITS_BRANCH // 2) as i:
                branch_pair(i)
            y_round(UNITS_BRANCH - 1)
            act.dma_start(wrt[:, :, 0:GROUPS], w_grp.rearrange("(c p) n -> p c n", p=P)).then_inc(moe_par, 16)
            act.dma_start(wrt[:, :, GROUPS:], w_exp.rearrange("(c p) n -> p c n", p=P)).then_inc(moe_par, 16)
            act.dma_start(brt[:, 0:GROUPS], b_grp.partition_broadcast(P)).then_inc(moe_par, 16)
            act.dma_start(brt[:, GROUPS:], b_exp.partition_broadcast(P)).then_inc(moe_par, 16)

            def x2T_copy(u, n):
                act.wait_ge(x2_turned, n + 1)
                act.activation(x2T[:, u], ps[:, u], ACT.Copy).then_inc(x2T_ready, 1)

            def out_unit(i, u, end=False):
                n = i * 2 + u
                if not (end and u == 1):
                    round_one(UNIT_OUT, 2 * u + 3, i)
                if not (isinstance(i, int) and i == 0 and u == 0):
                    x2T_copy(1 - u, n - 1)
                if not end:
                    round_one(UNIT_OUT, 2 * u + 4, i)
                act.wait_ge(x2_ready, n + 2)
                act.activation(x2[:, :, ds(i * (2 * UNIT) + u * UNIT, UNIT)], x2u[:, u], ACT.Copy)
                if not (isinstance(i, int) and n == 0):
                    act.wait_ge(squares2, n)
                for t in range(TT):
                    last = act.activation(sqs[:, t], x2u[:, u, t], ACT.Square, accum_out=sq2[:, t, ds(n, 1)])
                last.then_inc(squares2, 1)

            for u in range(2):
                out_unit(0, u)
            with act.Fori(1, UNITS_OUT // 2 - 1) as i:
                for u in range(2):
                    out_unit(i, u)
            out_unit(UNITS_OUT // 2 - 1, 0, end=True)
            out_unit(UNITS_OUT // 2 - 1, 1, end=True)
            x2T_copy(1, UNITS_OUT - 1)

            act.wait_ge(root_done, M_HEADS + 2)
            for t in range(TT):
                act.activation(h2n[:, t], x2[:, t], ACT.Copy, scale=stat[:, 22 + t:23 + t])
            for t in range(TT):
                act.activation(h2hi[:, t], x2[:, t], ACT.Copy, scale=stat[:, 22 + t:23 + t]).then_inc(h2hi_ready, 1)
            act.wait_ge(gexp_go, 1)
            for t in range(TT):
                last = act.activation(rt[:, 4, t, 0:GROUPS], lr[:, t, 0:GROUPS], ACT.Exp, bias=sc[:, 1, t:t + 1],
                                      accum_out=sc[:, 2, t:t + 1])
            last.then_inc(gexp_done, 1)
            act.wait_ge(gexp_go, 2)
            act.activation(sc[:, 6], sc[:, 5], ACT.Exp).then_inc(gexp_done, 1)
            for c in range(DC):
                if c % 2 == 0:
                    act.wait_ge(xg_summed, c + 1)
                    act.activation(xg[:, c, 0:PAIRS], ps[:, c % 8], ACT.Copy, scale=g2T[:, c:c + 1]).then_inc(xg_act, 1)

            def experts(chunks):
                with act.Fori(0, EXPERTS // 2) as i:
                    with passes(act, chunks) as c:
                        s = i * chunks + c
                        for b in range(2):
                            n = s * 2 + b
                            act.wait_ge(h_summed, n + 2)
                            act.wait_ge(hid_ready, n + 1)
                            act.activation(sg[:], ps[:, 0, 0:P], ACT.Sigmoid).then_inc(sg_ready, 1)
                            act.wait_ge(hid_turned, n + 2)
                            act.wait_ge(y_summed, s * 2 + 1)
                            act.activation(hidT[:, b], ps[:, 1, 0:P], ACT.Copy).then_inc(hidT_ready, 1)
                        act.wait_ge(mix_turned, s + 2)
                        act.wait_ge(scattered, s * GROUPS_OUT + 1)
                        act.activation(mixT[:], ps[:, 1, P:3 * P], ACT.Copy).then_inc(mixT_ready, 1)
                        for h in range(2):
                            act.wait_ge(y_summed, s * 2 + (h + 2))
                            act.activation(ys[:, h * (D // 2):(h + 1) * (D // 2)],
                                           ps[:, 2 + 2 * h:4 + 2 * h].rearrange("p a n -> p (a n)"),
                                           ACT.Copy).then_inc(ys_ready, 1)
                for g in range(GROUPS_OUT):
                    t, n = group_place(g)
                    act.wait_ge(added, (EXPERTS // 2 * chunks - 1) * GROUPS_OUT + g + 2)
                    cols = slice(n * 512, (n + 1) * 512)
                    act.activation(fin[:, t, cols], x2[:, t, cols], ACT.Square,
                                   accum_out=sq2[:, t, n:n + 1]).then_inc(squares3, 1)

            by_most(act, experts)
            act.wait_ge(root_done, M_HEADS + 3)
            act.wait_ge(x2g_ready, GROUPS_OUT)
            act.wait_ge(squares3, GROUPS_OUT)
            for h in range(2):
                cols = slice(h * (D // 2), (h + 1) * (D // 2))
                act.activation(fin[:, 0, cols], x2g[:, 0, cols], ACT.Copy, scale=stat[:, 42:43]).then_inc(out_ready[0], 1)

        @block.tensor
        def _(pe):
            pe.wait_ge(consts, 1)
            pe.wait_ge(par_loaded, 16 * 9)
            pe.transpose(ps[:, 7, 0:PARAM_ROWS], param_rows[:], ident[0:PARAM_ROWS, 0:PARAM_ROWS]).then_inc(param_turned, 1)
            pe.matmul(ps[0:A_HEADS, 6, 0:T], relb[:], onehot_s[:], start=True, stop=True).then_inc(rev_summed, 1)
            pe.wait_ge(param_ready, 1)
            pe.wait_ge(rev_ready, 1)
            for t in range(TT):
                pe.wait_ge(normed, t + 1)
            for g in range(DC // 2):
                for c in range(2):
                    for t in range(TT):
                        last = pe.transpose(ps[:, g, c * T + t * P:c * T + (t + 1) * P],
                                            xin[:, t, (2 * g + c) * P:(2 * g + c + 1) * P], ident[:])
                last.then_inc(turned, 1)

            def channel_half(banks, q, first, last_half):
                w = wsplit[:, q % 2]
                for b in range(2):
                    for k in range(HALF_K):
                        a = act_of(q, k)
                        pe.matmul(banks[b], w[:, k, 0, b * P:(b + 1) * P], a, start=first and k == 0,
                                  stop=False)
                        last = pe.matmul(banks[b][:, 0:T], w[:, k, 1, b * P:(b + 1) * P], a[:, 0],
                                         start=False, stop=last_half and k == HALF_K - 1)
                last.then_inc(used, 1)

            def act_of(q, k):
                return act_split[:, (q % 2) * HALF_K + k]

            def token_half(banks, q, first, last_half, rows_half=None):
                rows_half = q % 2 if rows_half is None else rows_half
                w = wsplit[:, q % 2]
                for t in range(TT):
                    for k in range(HALF_K):
                        a = act_of(rows_half, k)
                        pe.matmul(banks[t], a[:, 0, t * P:(t + 1) * P], w[:, k], start=first and k == 0,
                                  stop=False)
                        last = pe.matmul(banks[t][:, 0:UNIT], a[:, 1, t * P:(t + 1) * P], w[:, k, 0],
                                         start=False, stop=last_half and k == HALF_K - 1)
                last.then_inc(used, 1)

            def half(kind, q, half_no, unit_no, bank=0):
                pe.wait_ge(split, half_no + 1)
                if q % 2 == 0 and unit_no is not None:
                    pe.wait_ge(acc_free, unit_no - 1)
                u = (q // 2) % 2
                kind([ps[:, bank + 2 * u], ps[:, bank + 2 * u + 1]], q, q % 2 == 0, q % 2 == 1)

            def stage_pair(kind, unit, i):
                for q in range(PAIR_HALVES):
                    half(kind, q, i * PAIR_HALVES + (2 * unit + q), i * 2 + (unit + q // 2))

            def stage(kind, unit, start, units):
                with pe.Fori(start, units // 2) as i:
                    stage_pair(kind, unit, i)

            for q in range(PAIR_HALVES):
                pe.wait_ge(bank_free, min(DC, (q + 1) * HALF_K))
                half(channel_half, q, q, None)
            stage(channel_half, 0, 1, UNITS_QK)

            pe.wait_ge(wif_ready, 1)
            for t in range(TT):
                out_if = ps[:, 4, t * 16:(t + 1) * 16]
                for k in range(DC):
                    pe.matmul(out_if, act_split[:, k, 0, t * P:(t + 1) * P], wif[:, k], start=k == 0, stop=False)
                    last = pe.matmul(out_if[:, 0:8], act_split[:, k, 1, t * P:(t + 1) * P], wif[:, k, 0],
                                     start=False, stop=k == DC - 1)
            last.then_inc(if_summed, 1)
            stage(channel_half, UNIT_QKA, 0, UNITS_QKA)

            pe.wait_ge(ls_ready, 1)
            pe.matmul(ps[:, 5, 0:4], upto[:], lst[:, 0], start=True, stop=True)
            pe.matmul(ps[:, 5, 4:8], ones[:], lst[:, 0], start=True, stop=False)
            pe.matmul(ps[:, 5, 4:8], upto[:], lst[:, 1], start=False, stop=True).then_inc(cum_summed, 1)
            stage(token_half, UNIT_VO, 0, UNITS_VO)
            pe.wait_ge(aa_ready, 1)
            for t in range(TT):
                last = pe.transpose(ps[0:M_HEADS, 6, t * P:(t + 1) * P], aa[:, t], ident[:])
            last.then_inc(aa_turned, 1)
            for i in range(UNITS_VA // 2):
                if i == 1:
                    pe.wait_ge(aaT_ready, 1)
                    for h in range(M_HEADS):
                        last = pe.matmul(ps[:, 4 + h // 2, (h % 2) * T:(h % 2 + 1) * T], pick[:, h], aaT[:],
                                         start=True, stop=True)
                    last.then_inc(aa_spread, 1)
                stage_pair(token_half, UNIT_VA, i)
            pe.wait_ge(negM_ready, 1)
            for t in range(TT):
                last = pe.transpose(ps[0:M_HEADS, 6, t * P:(t + 1) * P], negM[:, t], ident[:])
            last.then_inc(negM_turned, 1)
            pe.wait_ge(negMT_ready, 1)
            pe.wait_ge(flip_loaded, 16 * A_HEADS)

            with pe.Fori(0, M_HEADS) as i:
                def gate_half(q):
                    half(channel_half, q, i * 8 + (2 * UNIT_GATES + q), i * 4 + (UNIT_GATES + q // 2))

                gate_half(0)
                pe.wait_ge(staged, i + 1)
                pe.wait_ge(br_lo, i + 1)
                for a in range(2):
                    q_h, k_h, bias = qk_now[:, 4 + 2 * a], qk_now[:, 5 + 2 * a], bias_flipped[:, ds(i * 2 + a, 1)]
                    bank = ps[:, 4 + a]
                    pe.matmul(bank[:, 0:P], q_h[:, 0:P], k_h[:, 0:P], start=True, stop=False)
                    pe.matmul(bank[:, 0:P], flip[:], bias[:, 0, P:T], start=False, stop=True)
                    pe.matmul(bank[:, P:REV], q_h[:, P:T], k_h[:], start=True, stop=False)
                    pe.matmul(bank[:, P:REV], flip[:], bias[:, 0], start=False, stop=True).then_inc(logits, 1)
                for k in range(2):
                    pe.matmul(ps[:, 6, 0:T], qk_now[:, 2 + k, 0:P], qk_now[:, k], start=k == 0, stop=k == 1)
                for k in range(2):
                    pe.matmul(ps[:, 6, T:REV], qk_now[:, 2 + k, P:T], qk_now[:, k, P:T], start=k == 0, stop=k == 1)
                pe.matmul(ps[:, 7, 0:T], pick_now[:], negMT[:], start=True, stop=True).then_inc(scores, 1)
                for q in (1, 2, 3):
                    gate_half(q)
                for a in range(2):
                    pe.wait_ge(prob_ready, i * 2 + (a + 1))
                    for c in range(3):
                        last = pe.transpose(ps[:, 4 + a, c * P:(c + 1) * P], prob[:, a, c * P:(c + 1) * P], ident[:])
                    last.then_inc(prob_turned, 1)
                pe.wait_ge(scored_ready, i + 1)
                for t, parts in enumerate(([(0, 0)], [(1, 0), (2, 1)])):
                    for n, (c, s) in enumerate(parts):
                        s_t = scored[:, c * P:(c + 1) * P]
                        first, end = n == 0, n == len(parts) - 1
                        pe.matmul(ps[:, 6 + t, 0:M_DIM], s_t, v_now[:, 0, s], start=first, stop=end)
                    for n, (c, s) in enumerate(parts):
                        s_t = scored[:, c * P:(c + 1) * P]
                        first, end = n == 0, n == len(parts) - 1
                        last = pe.matmul(ps[:, 6 + t, M_DIM:M_DIM + 1], s_t, ones[:, 0:1], start=first, stop=end)
                last.then_inc(num_summed, 1)
                gate_half(4)
                gate_half(5)
                for a in range(2):
                    pe.wait_ge(probT_ready, i * 2 + (a + 1))
                    v_h = v_now[:, 1, :, a * P:(a + 1) * P]
                    pe.matmul(ps[:, 4 + a, 0:T], v_h[:, 0], probT[:, a, 0:T], start=True, stop=False)
                    pe.matmul(ps[:, 4 + a, P:T], v_h[:, 1], probT[:, a, T:REV], start=False, stop=True).then_inc(ha_summed, 1)
                pe.wait_ge(hm_ready, i + 1)
                for c in range(2):
                    for t in range(TT):
                        last = pe.transpose(ps[:, 6, c * T + t * P:c * T + (t + 1) * P], hm[:, t, c * P:(c + 1) * P], ident[:])
                last.then_inc(hm_turned, 1)
                gate_half(6)
                gate_half(7)

            pe.wait_ge(br_lo, M_HEADS + 1)
            with pe.Fori(0, UNITS_BRANCH // 2) as i:
                for q in range(PAIR_HALVES):
                    pe.wait_ge(split, i * PAIR_HALVES + (2 * UNIT_BRANCH + q + 1))
                    if q % 2 == 0:
                        pe.wait_ge(acc_free, i * 2 + (UNIT_BRANCH + q // 2 - 1))
                    w = wsplit[:, q % 2]
                    for b in range(2):
                        bank = ps[:, 4 * (1 - q // 2) + 2 * (q % 2) + b]
                        for k in range(HALF_K):
                            a = br_split[:, (q % 2) * HALF_K + k]
                            pe.matmul(bank, w[:, k, 0, b * P:(b + 1) * P], a, start=k == 0, stop=False)
                            last = pe.matmul(bank[:, 0:T], w[:, k, 1, b * P:(b + 1) * P], a[:, 0],
                                             start=False, stop=k == HALF_K - 1)
                    last.then_inc(used, 1)
            pe.wait_ge(y_ready, UNITS_BRANCH)
            n_r = GROUPS + EXPERTS

            def turn_x2(u, n):
                pe.wait_ge(x2_ready, n + 2)
                for c in range(2):
                    for t in range(TT):
                        last = pe.transpose(ps[:, u, c * T + t * P:c * T + (t + 1) * P],
                                            x2u[:, u, t, c * P:(c + 1) * P], ident[:])
                last.then_inc(x2_turned, 1)

            def route(i, u):
                pe.wait_ge(x2T_ready, i * 2 + (u + 1))
                for t in range(TT):
                    for c in range(2):
                        last = pe.matmul(ps[:, 2 + u, ds(i * (TT * n_r) + t * n_r, n_r)], x2T[:, u, c, t * P:(t + 1) * P],
                                         wrt[:, ds(i * 4 + (2 * u + c), 1)].rearrange("p c n -> p (c n)"),
                                         start=c == 0, stop=c == 1)
                return last

            def out_pair(i):
                for u in range(2):
                    half(token_half, 2 * u, i * PAIR_HALVES + (2 * UNIT_OUT + 2 * u), i * 2 + (UNIT_OUT + u), bank=4)
                    route(i - 1, u)
                    half(token_half, 2 * u + 1, i * PAIR_HALVES + (2 * UNIT_OUT + 2 * u + 1), None, bank=4)
                    turn_x2(1 - u, i * 2 + (u - 1))

            pe.wait_ge(acc_free, UNIT_OUT - 1)
            for q in range(PAIR_HALVES):
                if q == 2:
                    pe.wait_ge(y_ready, UNITS_BRANCH + 1)
                u, rows_half = q % 2, q // 2
                pe.wait_ge(split, 2 * UNIT_OUT + q + 1)
                token_half([ps[:, 4 + 2 * u], ps[:, 5 + 2 * u]], q, rows_half == 0, rows_half == 1, rows_half)
            turn_x2(0, 0)
            pe.wait_ge(wrt_ready, 1)
            with pe.Fori(1, UNITS_OUT // 2) as i:
                out_pair(i)
            turn_x2(1, UNITS_OUT - 1)
            for u in range(2):
                last = route(UNITS_OUT // 2 - 1, u)
            last.then_inc(routed, 1)

            pe.wait_ge(mk_ready, 1)
            pe.matmul(ps[:, 1, 0:32], before[:], mk[:, 0], start=True, stop=True)
            pe.matmul(ps[:, 1, 32:64], ones[:], mk[:, 0], start=True, stop=False)
            pe.matmul(ps[:, 1, 32:64], before[:], mk[:, 1], start=False, stop=True)
            pe.matmul(ps[:, 1, 64:96], ones[:], mk[:, 0], start=True, stop=False)
            pe.matmul(ps[:, 1, 64:96], ones[:], mk[:, 1], start=False, stop=True).then_inc(rank_summed, 1)
            pe.wait_ge(sel_ready, 1)
            pe.wait_ge(h2lo_ready, TT)
            parts = [part[:].rearrange("p t (q c) -> p t c q", c=DC) for part in (h2hi, h2lo)]
            for c in range(DC):
                if c >= 8:
                    pe.wait_ge((xg_act, xg_dve)[c % 2], (c - 8) // 2 + 1)
                for t in range(TT):
                    for n, part in enumerate(parts):
                        last = pe.matmul(ps[:, c % 8], part[:, t, c], sel[:, t], start=t == 0 and n == 0,
                                         stop=t == TT - 1 and n == 1)
                last.then_inc(xg_summed, 1)

            def hidden(i, s, b):
                pe.wait_ge(xe_ready, s * 2 + (b + 1))
                pe.wait_ge(w13_loaded[b], i * 32 + 32)
                pe.wait_ge(hid_ready, s * 2 + (b + 1))
                for k in range(DC):
                    for f in range(FC):
                        last = pe.matmul(
                            ps[f * SLOTS:(f + 1) * SLOTS, 0, 0:2 * P].rearrange("p (w f) -> p w f", w=2),
                            xe[:, b, k], w13[b][:, :, k, f * P:(f + 1) * P], start=k == 0, stop=k == DC - 1)
                last.then_inc(h_summed, 1)

            def turn(s, b):
                pe.wait_ge(hidT_ready, s * 2 + (b + 1))
                if b == 0:
                    pe.wait_ge(mixT_ready, s + 1)
                if b == 1:
                    pe.wait_ge(mix_ready, s + 1)
                    for t in range(TT):
                        last = pe.transpose(ps[:, 1, P + t * P:P + (t + 1) * P], mix[:, t], ident[:])
                    last.then_inc(mix_turned, 1)
                pe.wait_ge(hid_ready, s * 2 + (b + 2))
                pe.transpose(ps[:, 1, 0:P], hid[:], ident[:]).then_inc(hid_turned, 1)

            def rows(turn, s, slot):
                pe.wait_ge(hidT_ready, s * 2 + 3)
                pe.wait_ge(ys_ready, s * 2 + 1)
                for n in range(4):
                    if n % 2 == 0:
                        pe.wait_ge(w2_loaded[slot][n // 2], turn * 32 + 32)
                    for f in range(FC):
                        for b in range(2):
                            last = pe.matmul(ps[b * SLOTS:(b + 1) * SLOTS, 2 + n],
                                             hidT[:, b, f * SLOTS:(f + 1) * SLOTS],
                                             w2s[b][:, slot, f, n * 512:(n + 1) * 512],
                                             start=f == 0, stop=f == FC - 1)
                    if n % 2 == 1:
                        last.then_inc(y_summed, 1)

            def scatter(s, groups):
                for g in groups:
                    if g % 4 == 0:
                        pe.wait_ge(ys_ready, s * 2 + (g // 4 + 2))
                        pe.wait_ge(mixT_ready, s + 2)
                    pe.wait_ge(added, s * GROUPS_OUT + max(1, g))
                    t, n = group_place(g)
                    pe.matmul(ps[:, 6 + g % 2], mixT[:, t * P:(t + 1) * P],
                              ys[:, n * 512:(n + 1) * 512], start=True, stop=True).then_inc(scattered, 1)

            def experts(chunks):
                if chunks > 1:
                    with pe.Fori(0, EXPERTS // 4) as j:
                        for slot in range(2):
                            i = j * 2 + slot
                            with pe.Fori(0, chunks) as c:
                                s = i * chunks + c
                                for b in range(2):
                                    hidden(i, s, b)
                                    turn(s, b)
                                rows(j, s, slot)
                                scatter(s, range(GROUPS_OUT))
                    return
                for b in range(2):
                    hidden(0, 0, b)
                    turn(0, b)
                rows(0, 0, 0)

                def pair(i, turns, slot):
                    hidden(i, i, 0)
                    scatter(i - 1, (0, 1, 2))
                    turn(i, 0)
                    hidden(i, i, 1)
                    scatter(i - 1, (3, 4, 5))
                    turn(i, 1)
                    scatter(i - 1, (6, 7))
                    rows(turns, i, slot)

                with pe.Fori(0, EXPERTS // 4 - 1) as j:
                    pair(j * 2 + 1, j, 1)
                    pair(j * 2 + 2, j + 1, 0)
                pair(EXPERTS // 2 - 1, EXPERTS // 4 - 1, 1)
                scatter(EXPERTS // 2 - 1, range(GROUPS_OUT))

            by_most(pe, experts)

        @block.vector
        def _(dve):
            steps = Steps(dve, dve_s)

            def split_half(q, half_no):
                dve.wait_ge(rounded, half_no + 1)
                dve.tensor_tensor(wsplit[:, q % 2, :, 1], wraw[:, q % RAW], wsplit[:, q % 2, :, 0].bitcast(F32),
                                  ALU.subtract).then_inc(split, 1)

            def split_ahead(u, unit, i):
                for q in (2 * u + 2, 2 * u + 3):
                    split_half(q, i * PAIR_HALVES + (2 * unit + q))

            def sum_halves(outs, banks):
                for o, bank in zip(outs, banks):
                    last = dve.tensor_reduce(o, halves_sum(bank), AX.X, ALU.add)
                last.then_inc(acc_free, 1)

            def rms(col, out_col, n, turn):
                dve.tensor_scalar(stat[:, out_col:out_col + n], stat[:, col:col + n], 1.0 / D, RMS_EPS,
                                  ALU.mult, ALU.add).then_inc(root_go, 1)
                dve.wait_ge(root_done, turn)

            dve.memset(rev[:, T:REV], MASKED)
            dve.memset(pre[:, :, 0:CONV - 1], 0.0)
            dve.wait_ge(squares, TT)
            rms(0, 2, TT, 1)
            for t in range(TT):
                dve.tensor_scalar(xin[:, t], xin[:, t], stat[:, 2 + t:3 + t], None, ALU.mult).then_inc(normed, 1)
            dve.wait_ge(param_turned, 1)
            dve.tensor_copy(params[:], ps[:, 7, 0:PARAM_ROWS]).then_inc(param_ready, 1)
            dve.wait_ge(rev_summed, 1)
            dve.tensor_copy(rev[:, 0:T], ps[0:A_HEADS, 6, 0:T]).then_inc(rev_ready, 1)
            dve.wait_ge(wif_hi, 1)
            dve.tensor_tensor(wif[:, :, 1], wif_raw[:], wif[:, :, 0].bitcast(F32), ALU.subtract).then_inc(wif_ready, 1)
            for c in range(DC):
                if c % HALF_K == 0:
                    split_half(c // HALF_K, c // HALF_K)
                    dve.wait_ge(param_ready, 1)
                dve.wait_ge(hi_ready, c // 2 * 2 + 2)
                dve.scalar_tensor_tensor(act_split[:, c, 1], ps[:, c // 2, (c % 2) * T:(c % 2 + 1) * T],
                                         params[:, G1_ROW + c:G1_ROW + c + 1], act_split[:, c, 0].bitcast(F32),
                                         ALU.mult, ALU.subtract).then_inc(bank_free, 1)

            def split_one(unit, q, i):
                split_half(q, i * PAIR_HALVES + (2 * unit + q))

            def silu_conv(i, u):
                dve.wait_ge(conv_sig, i * 2 + (u + 1))
                to = (i % 2) * 8 + (i // 2) * 2 + 4 * u
                dve.tensor_tensor(qk[:, ds(to, 2)], conv[:, u], csig[:], ALU.mult).then_inc(silu_done, 1)

            def conv_pair(i, steps):
                for u in range(2):
                    n = i * 2 + u
                    split_one(0, 2 * u + 3, i)
                    dve.wait_ge(used, i * PAIR_HALVES + (2 * u + 2))
                    if not (isinstance(i, int) and n == 0):
                        dve.wait_ge(conv_ready, n)
                    sum_halves([pre[:, b, CONV - 1:] for b in range(2)], [ps[:, 2 * u + b] for b in range(2)])
                    if not (isinstance(i, int) and i > 0 and u == 1):
                        split_one(0, 2 * u + 4, i)
                    if u == 1 or not isinstance(i, int) or i > 0:
                        silu_conv(*((i, 0) if u == 1 else (i - 1, 1)))
                    dve.wait_ge(first_tap, n + 1)
                    dve.wait_ge(acc_free, n + 1)
                    for j in range(1, CONV):
                        for b in range(2):
                            tap = params[:, ds(i * 4 + (CONV_ROW + j * DC + 2 * u + b), 1)]
                            last = dve.scalar_tensor_tensor(conv[:, u, b], pre[:, b, j:j + T], tap, conv[:, u, b],
                                                            ALU.mult, ALU.add)
                        if j < CONV - 1:
                            steps.done(last)
                    last.then_inc(conv_ready, 1)

            split_one(0, 2, 0)
            conv_pair(0, steps)
            with steps.loop(1, UNITS_QK // 2 - 1, 2 * (CONV - 2)) as i:
                conv_pair(i, steps)
            conv_pair(UNITS_QK // 2 - 1, steps)
            silu_conv(UNITS_QK // 2 - 1, 1)

            dve.wait_ge(if_summed, 1)
            steps.done(dve.tensor_reduce(ifg[:], ps[:, 4, 0:32].rearrange("p (t a n) -> p t n a", t=TT, a=2), AX.X, ALU.add))
            steps.done(dve.tensor_tensor(ifg[:], ifg[:], ifb[:].unsqueeze(1).to_broadcast([P, TT, 2 * M_HEADS]), ALU.add))
            dve.scalar_tensor_tensor(lsg[:], ifg[:, :, M_HEADS:], -1.0, ifg[:, :, M_HEADS:], ALU.mult,
                                     ALU.max).then_inc(absf_ready, 1)
            dve.tensor_scalar(lst[:], ifg[:, :, M_HEADS:], 0.0, None, ALU.min)
            dve.wait_ge(expf_ready, 1)
            dve.tensor_scalar(lsg[:], lsg[:], 1.0, None, ALU.add).then_inc(onef_ready, 1)
            dve.wait_ge(lnf_ready, 1)
            dve.tensor_tensor(lst[:], lst[:], lsg[:], ALU.subtract).then_inc(ls_ready, 1)

            with dve.Fori(0, UNITS_QKA // 2) as i:
                for u in range(2):
                    split_ahead(u, UNIT_QKA, i)
                    dve.wait_ge(used, i * PAIR_HALVES + (2 * UNIT_QKA + 2 * u + 2))
                    sum_halves([qk[:, ds((i % 2) * 8 + i // 2 + (16 + 4 * u + 2 * b), 1)].rearrange("p a t -> p (a t)")
                                for b in range(2)],
                               [ps[:, 2 * u + b] for b in range(2)])

            dve.wait_ge(cum_summed, 1)
            steps.done(dve.tensor_copy(cum[:], ps[:, 5, 0:8].rearrange("p (t h) -> p t h", t=TT)))
            dve.tensor_tensor(aa[:], ifg[:, :, 0:M_HEADS], cum[:], ALU.subtract).then_inc(aa_ready, 1)

            tok_f = tok[:].rearrange("p k t n -> p (k t n)")

            def token_unit(unit, i, u, start):
                split_ahead(u, unit, i)
                dve.wait_ge(used, i * PAIR_HALVES + (2 * unit + 2 * u + 2))
                sum_halves([tok_f[:, ds(start + (t * M_WIDTH + u * UNIT), UNIT)] for t in range(TT)],
                           [ps[:, 2 * u + t] for t in range(TT)])

            with dve.Fori(0, UNITS_VO // 2) as i:
                for u in range(2):
                    token_unit(UNIT_VO, i, u, (i // 2) * (TT * M_WIDTH) + (i % 2) * (2 * UNIT))
            dve.wait_ge(aa_turned, 1)
            dve.tensor_copy(aaT[:], ps[0:M_HEADS, 6, 0:T]).then_inc(aaT_ready, 1)
            for u in range(2):
                token_unit(UNIT_VA, 0, u, 2 * TT * M_WIDTH)

            dve.wait_ge(aa_spread, 1)
            mask_2 = mask_ts[:].unsqueeze(1).to_broadcast([P, 2, P])
            for n in range(2):
                token_unit(UNIT_VA, 1, n, 2 * UNIT + 2 * TT * M_WIDTH)
                rows = ps[:, 4 + n].rearrange("p (h s) -> p h s", h=2)
                dve.tensor_tensor(prob[:, :, 0:P], rows[:, :, 0:P], mask_2, ALU.add)
                steps.done(dve.tensor_tensor(prob[:, :, P:T], rows[:, :, P:T], mask_2, ALU.add))
                dve.tensor_reduce(negM[:, 0, 2 * n:2 * n + 2], prob[:, :, 0:P], AX.X, ALU.max)
                dve.tensor_reduce(negM[:, 1, 2 * n:2 * n + 2], prob[:, :, P:T], AX.X, ALU.max)
                steps.done(dve.tensor_reduce(stat[:, 50:52], rows[:, :, 0:P], AX.X, ALU.max))
                steps.done(dve.tensor_tensor(negM[:, 1, 2 * n:2 * n + 2], negM[:, 1, 2 * n:2 * n + 2], stat[:, 50:52], ALU.max))
            dve.tensor_scalar(negM[:], negM[:], 0.0, -1.0, ALU.max, ALU.mult).then_inc(negM_ready, 1)
            dve.wait_ge(negM_ready, 1)
            dve.tensor_tensor(expm[:], cum[:], negM[:], ALU.subtract).then_inc(mt_ready, 1)
            dve.wait_ge(negM_turned, 1)
            dve.tensor_copy(negMT[:], ps[0:M_HEADS, 6, 0:T]).then_inc(negMT_ready, 1)
            dve.wait_ge(expm_ready, 1)
            dve.wait_ge(o_ready, 1)

            with steps.loop(0, M_HEADS, 9) as i:
                def ahead(q):
                    split_half(q, i * 8 + (2 * UNIT_GATES + q))

                def gate_sums(n):
                    dve.wait_ge(used, i * 8 + (2 * UNIT_GATES + 2 * n + 2))
                    sum_halves([gates[:, ds(i * 8 + (2 * n + b), 1)].rearrange("p a t -> p (a t)") for b in range(2)],
                               [ps[:, 2 * (n % 2) + b] for b in range(2)])

                ahead(2)
                dve.wait_ge(scores, i + 1)
                dve.scalar_tensor_tensor(decay[:, 0:P], ps[:, 7, 0:P], aa[:, 0, ds(i, 1)], mask_st[:], ALU.add, ALU.add)
                dve.tensor_scalar(decay[:, P:T], ps[:, 7, P:T], aa[:, 0, ds(i, 1)], None, ALU.add)
                dve.scalar_tensor_tensor(decay[:, T:REV], ps[:, 7, P:T], aa[:, 1, ds(i, 1)], mask_st[:],
                                         ALU.add, ALU.add).then_inc(decay_arg, 1)
                for a in range(2):
                    dve.wait_ge(logits, i * 2 + (a + 1))
                    dve.tensor_reduce(stat[:, 8 + 2 * a:9 + 2 * a], ps[:, 4 + a, 0:P], AX.X, ALU.max, negate=True)
                    dve.tensor_reduce(stat[:, 9 + 2 * a:10 + 2 * a], ps[:, 4 + a, P:REV], AX.X, ALU.max,
                                      negate=True).then_inc(negmax, 1)
                ahead(3)
                gate_sums(0)
                dve.wait_ge(decay_exp, i + 1)
                dve.scalar_tensor_tensor(scored[:], ps[:, 6, 0:REV], float(M_DIM) ** -0.5, decay[:],
                                         ALU.mult, ALU.mult).then_inc(scored_ready, 1)
                dve.wait_ge(prob_exp, i * 2 + 2)
                steps.done(dve.reciprocal(stat[:, 16:20], stat[:, 12:16]))
                for a in range(2):
                    dve.tensor_scalar(prob[:, a, 0:P], prob[:, a, 0:P], stat[:, 16 + 2 * a:17 + 2 * a], None, ALU.mult)
                    dve.tensor_scalar(prob[:, a, P:REV], prob[:, a, P:REV], stat[:, 17 + 2 * a:18 + 2 * a], None,
                                      ALU.mult).then_inc(prob_ready, 1)
                ahead(4)
                ahead(5)
                gate_sums(1)
                for a in range(2):
                    dve.wait_ge(prob_turned, i * 2 + (a + 1))
                    dve.tensor_copy(probT[:, a], ps[:, 4 + a, 0:REV]).then_inc(probT_ready, 1)
                dve.wait_ge(num_summed, i + 1)
                for t in range(TT):
                    last = dve.tensor_scalar(stat[:, 32 + t:33 + t], ps[:, 6 + t, M_DIM:M_DIM + 1], -1.0,
                                             expm[:, t, ds(i, 1)], ALU.mult, ALU.max)
                steps.done(last)
                for t in range(TT):
                    last = dve.tensor_tensor(stat[:, 32 + t:33 + t], stat[:, 32 + t:33 + t],
                                             ps[:, 6 + t, M_DIM:M_DIM + 1], ALU.max)
                steps.done(last)
                steps.done(dve.reciprocal(stat[:, 34:36], stat[:, 32:34]))
                for t in range(TT):
                    last = dve.tensor_scalar(hm[:, t], ps[:, 6 + t, 0:M_DIM], stat[:, 34 + t:35 + t], None, ALU.mult)
                steps.done(last)
                for t in range(TT):
                    last = dve.bn_stats(bn[:, t], hm[:, t])
                steps.done(last)
                dve.tensor_tensor(mean_var[:, :, 0], bn[:, :, 1], bn[:, :, 4], ALU.add)
                dve.tensor_tensor(stat[:, 52:54], bn[:, :, 1], bn[:, :, 4], ALU.subtract)
                steps.done(dve.tensor_tensor(mean_var[:, :, 1], bn[:, :, 2], bn[:, :, 5], ALU.add))
                dve.tensor_scalar(mean_var[:, :, 0], mean_var[:, :, 0], 0.5, None, ALU.mult)
                dve.tensor_scalar(mean_var[:, :, 1], mean_var[:, :, 1], 1.0 / M_DIM, LN_EPS, ALU.mult, ALU.add)
                steps.done(dve.tensor_tensor(stat[:, 52:54], stat[:, 52:54], stat[:, 52:54], ALU.mult))
                dve.scalar_tensor_tensor(stat[:, 36:38], stat[:, 52:54], 0.25, mean_var[:, :, 1], ALU.mult,
                                         ALU.add).then_inc(root_go, 1)
                dve.wait_ge(root_done, i + 2)
                for t in range(TT):
                    last = dve.tensor_scalar(hm[:, t], hm[:, t], mean_var[:, t, 0:1], stat[:, 36 + t:37 + t],
                                             ALU.subtract, ALU.mult)
                steps.done(last)
                dve.tensor_tensor(hm[:], hm[:], tok[:, 1, :, ds(i * M_DIM, M_DIM)], ALU.mult).then_inc(hm_ready, 1)
                ahead(6)
                ahead(7)
                gate_sums(2)
                for a in range(2):
                    dve.wait_ge(br_hi, i * 4 + (a + 1))
                    to = br_split[:, ds(i * 2 + (8 + a), 1)]
                    dve.tensor_tensor(to[:, 0, 1], ps[:, 4 + a, 0:T], to[:, 0, 0].bitcast(F32), ALU.subtract)
                for c in range(2):
                    dve.wait_ge(br_hi, i * 4 + 4)
                    to = br_split[:, ds(i * 2 + c, 1)]
                    last = dve.scalar_tensor_tensor(to[:, 0, 1], ps[:, 6, c * T:(c + 1) * T],
                                                    params[:, ds(i * 2 + (MN_ROW + c), 1)], to[:, 0, 0].bitcast(F32),
                                                    ALU.mult, ALU.subtract)
                last.then_inc(br_lo, 1)
                ahead(8)
                ahead(9)
                gate_sums(3)

            gates_v = gates[:].rearrange("p (g c) t -> p g c t", g=2)
            split_one(UNIT_BRANCH, 2, 0)

            def y_split(n):
                dve.wait_ge(y_hi, n + 1)
                to = act_split[:, ds(n * 2, 2)]
                dve.tensor_tensor(to[:, :, 1], bsum[:, 0], to[:, :, 0].bitcast(F32), ALU.subtract).then_inc(y_ready, 1)

            def branch_pair(i):
                for u in range(2):
                    split_one(UNIT_BRANCH, 2 * u + 3, i)
                    if u == 1 or not isinstance(i, int) or i > 0:
                        y_split(i * 2 + (u - 1))
                    dve.wait_ge(used, i * PAIR_HALVES + (2 * UNIT_BRANCH + 2 * u + 2))
                    dve.wait_ge(y_ready, i * 2 + (u + 1))
                    sum_halves([bsum[:, g, b] for g in range(2) for b in range(2)],
                               [ps[:, 4 * (1 - u) + 2 * g + b] for g in range(2) for b in range(2)])
                    dve.wait_ge(acc_free, i * 2 + (UNIT_BRANCH + u + 1))
                    if not (isinstance(i, int) and i > 0 and u == 1):
                        split_one(UNIT_BRANCH, 2 * u + 4, i)
                    dve.wait_ge(gate_sig, M_HEADS)
                    steps.done(dve.tensor_tensor(bsum[:], bsum[:], gates_v[:, :, ds(i * 4 + 2 * u, 2)], ALU.mult))
                    dve.tensor_tensor(bsum[:, 0], bsum[:, 0], bsum[:, 1], ALU.add).then_inc(y_sum, 1)

            branch_pair(0)
            with steps.loop(1, UNITS_BRANCH // 2 - 1, 2) as i:
                branch_pair(i)
            branch_pair(UNITS_BRANCH // 2 - 1)
            y_split(UNITS_BRANCH - 1)
            split_one(UNIT_OUT, 2, 0)

            dve.wait_ge(moe_par, 16 * 4)
            n_r = GROUPS + EXPERTS
            dve.tensor_tensor(wrt[:], wrt[:], params[:, G2_ROW:].unsqueeze(2).to_broadcast([P, DC, n_r]),
                              ALU.mult).then_inc(wrt_ready, 1)
            dve.wait_ge(x2_loaded, 16)

            def out_sums(i, u):
                n = i * 2 + u
                if isinstance(i, int) and i == 0:
                    dve.wait_ge(used, 2 * UNIT_OUT + u + 3)
                else:
                    dve.wait_ge(used, i * PAIR_HALVES + (2 * UNIT_OUT + 2 * u + 2))
                dve.wait_ge(x2_ready, n + 1)
                sum_halves([osum[:, t] for t in range(TT)], [ps[:, 4 + 2 * u + t] for t in range(TT)])
                dve.wait_ge(acc_free, n + (UNIT_OUT + 1))
                if not (isinstance(i, int) and i == 0):
                    dve.wait_ge(x2T_ready, n - 1)
                dve.tensor_tensor(x2u[:, u], x2[:, :, ds(i * (2 * UNIT) + u * UNIT, UNIT)], osum[:],
                                  ALU.add).then_inc(x2_ready, 1)

            def out_pair(i):
                for u in range(2):
                    split_one(UNIT_OUT, 2 * u + 3, i)
                    if isinstance(i, int):
                        split_one(UNIT_OUT, 2 * u + 4, i)
                        out_sums(i, u)
                    else:
                        out_sums(i, u)
                        split_one(UNIT_OUT, 2 * u + 4, i)

            out_pair(0)
            with dve.Fori(1, UNITS_OUT // 2 - 1) as i:
                out_pair(i)
            split_half(3, HALVES - 1)
            out_sums(UNITS_OUT // 2 - 1, 0)
            out_sums(UNITS_OUT // 2 - 1, 1)

            dve.wait_ge(squares2, UNITS_OUT)
            steps.done(dve.tensor_reduce(stat[:, 20:22], sq2[:], AX.X, ALU.add))
            rms(20, 22, TT, M_HEADS + 2)
            dve.memset(xg[:, :, PAIRS:], 0.0)

            GMAX, GNEG, GSUM, EMAX, E2MAX, E_DIFF, E_EXP, FIRST, W_1, W_2 = range(10)

            def by_token(row, n):
                return sc[:, row].unsqueeze(2).to_broadcast([P, TT, n])

            def first_of(chosen, values, top, n):
                iota_n = iota_e[:, 0:n].unsqueeze(1).to_broadcast([P, TT, n])
                steps.done(dve.tensor_tensor(rt[:, 1, :, 0:n], values, by_token(top, n), ALU.is_ge))
                steps.done(dve.tensor_tensor(rt[:, 1, :, 0:n], rt[:, 1, :, 0:n], iota_n, ALU.mult))
                steps.done(dve.tensor_reduce(sc[:, FIRST], rt[:, 1, :, 0:n], AX.X, ALU.min))
                steps.done(dve.tensor_tensor(chosen, iota_n, by_token(FIRST, n), ALU.is_equal))

            dve.wait_ge(routed, 1)
            dve.wait_ge(iotas, 1)
            unit_sums = rt[:].rearrange("p a t e -> p (a t e)")[:, 0:2 * TT * n_r].rearrange("p (u t n) -> p u t n", u=2, t=TT)
            for u in range(2):
                last = dve.tensor_reduce(
                    unit_sums[:, u].rearrange("p t n -> p (t n)"),
                    ps[:, 2 + u, 0:UNITS_OUT // 2 * TT * n_r].rearrange("p (i n) -> p n i", n=TT * n_r), AX.X, ALU.add)
            steps.done(last)
            for u in range(2):
                for t in range(TT):
                    last = dve.scalar_tensor_tensor(lr[:, t], unit_sums[:, u, t], stat[:, 22 + t:23 + t],
                                                    (brt[:], lr[:, t])[u], ALU.mult, ALU.add)
                steps.done(last)
            g_log, e_log = lr[:, :, 0:GROUPS], lr[:, :, GROUPS:]
            steps.done(dve.tensor_reduce(sc[:, GMAX], g_log, AX.X, ALU.max))
            dve.tensor_scalar(sc[:, GNEG], sc[:, GMAX], -1.0, None, ALU.mult).then_inc(gexp_go, 1)
            first_of(rt[:, 2, :, 0:GROUPS], g_log, GMAX, GROUPS)
            steps.done(dve.tensor_scalar(rt[:, 2, :, 0:GROUPS], rt[:, 2, :, 0:GROUPS], -MASKED, MASKED, ALU.mult, ALU.add))
            for t in range(TT):
                last = dve.tensor_tensor(rt[:, 0, t].rearrange("p (g e) -> p g e", g=GROUPS),
                                         e_log[:, t].rearrange("p (g e) -> p g e", g=GROUPS),
                                         rt[:, 2, t, 0:GROUPS].unsqueeze(2).to_broadcast([P, GROUPS, PER_GROUP]), ALU.add)
            steps.done(last)
            steps.done(dve.tensor_reduce(sc[:, EMAX], rt[:, 0], AX.X, ALU.max))
            first_of(oh[:, :, 0], rt[:, 0], EMAX, EXPERTS)
            steps.done(dve.scalar_tensor_tensor(rt[:, 0], oh[:, :, 0], 2 * MASKED, rt[:, 0], ALU.mult, ALU.add))
            steps.done(dve.tensor_reduce(sc[:, E2MAX], rt[:, 0], AX.X, ALU.max))
            dve.tensor_tensor(sc[:, E_DIFF], sc[:, E2MAX], sc[:, EMAX], ALU.subtract).then_inc(gexp_go, 1)
            first_of(oh[:, :, 1], rt[:, 0], E2MAX, EXPERTS)
            dve.tensor_tensor(mk[:], oh[:, :, 0], oh[:, :, 1], ALU.add).then_inc(mk_ready, 1)
            dve.wait_ge(rank_summed, 1)
            steps.done(dve.tensor_copy(table[:, 0], ps[:, 1, 64:96]))
            dve.tensor_copy(rank[:], ps[:, 1, 0:64].rearrange("p (t e) -> p t e", t=TT))
            at, shift = 0, 1
            while shift < EXPERTS:
                to = 1 if at != 1 else 2
                dve.tensor_copy(table[:, to, 0:shift], table[:, at, 0:shift])
                steps.done(dve.tensor_tensor(table[:, to, shift:], table[:, at, shift:],
                                             table[:, at, 0:EXPERTS - shift], ALU.add))
                at, shift = to, 2 * shift
            steps.done(dve.tensor_tensor(table[:, 3], table[:, at], table[:, 0], ALU.subtract))
            steps.done(dve.tensor_tensor(pos[:], rank[:], table[:, 3:4].to_broadcast([P, TT, EXPERTS]), ALU.add))
            for k in range(2):
                last = dve.tensor_tensor(rt[:, k], oh[:, :, k], pos[:], ALU.mult)
            steps.done(last)
            steps.done(dve.tensor_reduce(stat[:, 44:48], rt[:, 0:2].rearrange("p k t e -> p (k t) e"), AX.X, ALU.add))
            for t in range(TT):
                last = dve.tensor_scalar(sel[:, t], iota_s[:], stat[:, 44 + t:45 + t], None, ALU.is_equal)
            steps.done(last)
            for t in range(TT):
                last = dve.scalar_tensor_tensor(sel[:, t], iota_s[:], stat[:, 46 + t:47 + t], sel[:, t].bitcast(F32),
                                                ALU.is_equal, ALU.add)
            last.then_inc(sel_ready, 1)
            dve.wait_ge(gexp_done, 2)
            steps.done(dve.tensor_scalar(sc[:, W_1], sc[:, E_EXP], 1.0, None, ALU.add))
            steps.done(dve.tensor_tensor(sc[:, W_1], sc[:, W_1], sc[:, GSUM], ALU.mult))
            steps.done(dve.reciprocal(sc[:, W_1], sc[:, W_1]))
            steps.done(dve.tensor_tensor(sc[:, W_2], sc[:, W_1], sc[:, E_EXP], ALU.mult))
            steps.done(dve.tensor_tensor(wt[:], oh[:, :, 0], by_token(W_1, EXPERTS), ALU.mult))
            steps.done(dve.tensor_tensor(rt[:, 3], oh[:, :, 1], by_token(W_2, EXPERTS), ALU.mult))
            dve.tensor_tensor(wt[:], wt[:], rt[:, 3], ALU.add)
            dve.tensor_reduce(stat[:, 35:36], table[:, 0], AX.X, ALU.max)
            for c in range(CHUNKS):
                last = dve.tensor_scalar(starts[:, :, c], table[:, 3], float(c * SLOTS), float(PAIRS), ALU.add, ALU.min)
            steps.done(last)
            dve.tensor_copy(starts_i[:], starts[0:1])
            dve.tensor_copy(most_i[:], stat[0:1, 35:36]).then_inc(tab_ready, 1)
            for c in range(1, DC, 2):
                dve.wait_ge(xg_summed, c + 1)
                dve.tensor_scalar(xg[:, c, 0:PAIRS], ps[:, c % 8], g2T[:, c:c + 1], None, ALU.mult).then_inc(xg_dve, 1)
            dve.wait_ge(xg_act, DC // 2)
            dve.wait_ge(xg_dve, DC // 2)

            steps_x = Steps(dve, dve_x)

            def tokens_in(i, c, s):
                for b in range(2):
                    at = dve.value_load(starts_i[0:1, ds(i * 2 + b, 1), ds(c, 1)], min_val=0, max_val=PAIRS)
                    dve.wait_ge(h_summed, s * 2 + 1)
                    dve.tensor_copy(xe[:, b], xg[:, :, ds(at, SLOTS)]).then_inc(xe_ready, 1)
                dve.wait_ge(mix_turned, s + 1)
                for b in range(2):
                    for t in range(TT):
                        last = dve.tensor_scalar(mix[:, t, b * SLOTS:(b + 1) * SLOTS],
                                                 iota_c[:, ds(c, 1)].rearrange("p c s -> p (c s)"),
                                                 rank[:, t, ds(i * 2 + b, 1)], wt[:, t, ds(i * 2 + b, 1)],
                                                 ALU.is_equal, ALU.mult)
                last.then_inc(mix_ready, 1)

            def silu(s, b):
                dve.wait_ge(sg_ready, s * 2 + (b + 1))
                dve.wait_ge(hid_turned, s * 2 + (b + 1))
                steps_x.done(dve.tensor_tensor(hid[:], sg[:], ps[:, 0, 0:P], ALU.mult))
                dve.tensor_tensor(hid[:], hid[:], ps[:, 0, P:2 * P], ALU.mult).then_inc(hid_ready, 1)

            def add(s, groups):
                for g in groups:
                    dve.wait_ge(scattered, s * GROUPS_OUT + (g + 2))
                    dve.wait_ge(added, s * GROUPS_OUT + 1)
                    t, n = group_place(g)
                    cols = x2[:, t, n * 512:(n + 1) * 512]
                    dve.tensor_tensor(cols, cols, ps[:, 6 + g % 2], ALU.add).then_inc(added, 1)

            def experts(chunks):
                steps_x.n = 0
                if chunks > 1:
                    with steps_x.loop(0, EXPERTS // 2, 2 * chunks) as i:
                        with steps_x.loop(0, chunks, 2) as c:
                            s = i * chunks + c
                            tokens_in(i, c, s)
                            for b in range(2):
                                silu(s, b)
                            add(s, range(GROUPS_OUT))
                else:
                    tokens_in(0, 0, 0)
                    for b in range(2):
                        silu(0, b)
                    with steps_x.loop(1, EXPERTS // 2, 2) as i:
                        tokens_in(i, 0, i)
                        silu(i, 0)
                        add(i - 1, (0, 1, 2))
                        silu(i, 1)
                        add(i - 1, (3, 4, 5, 6, 7))
                    for g in range(GROUPS_OUT):
                        add(EXPERTS // 2 - 1, (g,))
                        if g > 0:
                            gained(chunks, g - 1)
                if chunks > 1:
                    for g in range(GROUPS_OUT - 1):
                        gained(chunks, g)
                gained(chunks, GROUPS_OUT - 1)

            def gained(chunks, g):
                if g == 0:
                    dve.wait_ge(fing_loaded, 16)
                dve.wait_ge(added, (EXPERTS // 2 * chunks - 1) * GROUPS_OUT + g + 2)
                t, n = group_place(g)
                cols = slice(n * 512, (n + 1) * 512)
                dve.tensor_tensor(x2g[:, t, cols], x2[:, t, cols], fin_g[:, cols], ALU.mult).then_inc(x2g_ready, 1)

            by_most(dve, experts)
            dve.wait_ge(squares3, GROUPS_OUT)
            steps_f = Steps(dve, final_root)
            steps_f.done(dve.tensor_reduce(stat[:, 40:42], sq2[:, :, 0:4], AX.X, ALU.add))
            rms(40, 42, TT, M_HEADS + 3)
            dve.wait_ge(x2g_ready, GROUPS_OUT)
            for h in range(2):
                cols = slice(h * (D // 2), (h + 1) * (D // 2))
                dve.tensor_scalar(fin[:, 1, cols], x2g[:, 1, cols], stat[:, 43:44], None, ALU.mult).then_inc(out_ready[1], 1)


_INS = ["x", "norm1_g", "w_in", "conv_w", "if_bias", "mnorm_g", "w_branch_m", "w_branch_a", "w_out", "rel_bias",
        "norm2_g", "w_grp", "b_grp", "w_exp", "b_exp", "w1", "w3", "w2", "final_g"]


def kernel(**inputs):
    import numpy as _np
    import concourse.bacc as _bacc
    from concourse import mybir as _mybir
    from concourse.bass_utils import run_bass_kernel_spmd as _run

    nc = _bacc.Bacc("TRN2", target_bir_lowering=False, num_devices=1, dynamic_dma_scratch_size=1024)
    arrays, args = {}, []
    for name in _INS + ["onehot"]:
        a = _np.ascontiguousarray(bucket_onehot() if name == "onehot" else inputs[name])
        if name not in ("rel_bias", "final_g", "onehot"):
            a = a.reshape(a.shape[1:])
        arrays[f"in_{name}_dram"] = a
        args.append(nc.dram_tensor(f"in_{name}_dram", a.shape, _mybir.dt.from_np(a.dtype), kind="ExternalInput").ap())
    args.append(nc.dram_tensor("out_0_dram", (T, D), F32, kind="ExternalOutput").ap())
    layer(nc, *args)
    r = _run(nc, [arrays], core_ids=[0])
    return r.results[0]["out_0_dram"].reshape(1, T, D)
```

```python
from contextlib import ExitStack, contextmanager

import numpy as np

import concourse.bass as bass
from concourse import mybir

F32 = mybir.dt.float32
F32R = mybir.dt.float32r
I32 = mybir.dt.int32
ALU = mybir.AluOpType
ACT = mybir.ActivationFunctionType
AX = mybir.AxisListType
ds = bass.ds

P = 128
T = 256
TT = T // P
D = 2048
DC = D // P
M_HEADS, M_DIM = 4, 256
M_WIDTH = M_HEADS * M_DIM
A_HEADS, A_DIM = 8, 128
A_WIDTH = A_HEADS * A_DIM
CONV = 4
BUCKETS, MAX_DIST = 32, 128
GROUPS, PER_GROUP = 4, 8
EXPERTS = GROUPS * PER_GROUP
FF = 256
FC = FF // P
RMS_EPS, LN_EPS = 1e-6, 1e-5
MASKED = -1e30

COL_QK, COL_V, COL_O = 0, 2 * M_WIDTH, 3 * M_WIDTH
COL_IF = 4 * M_WIDTH
COL_QA = COL_IF + 2 * M_HEADS
COL_KA, COL_VA = COL_QA + A_WIDTH, COL_QA + 2 * A_WIDTH
COL_GATES = COL_VA + A_WIDTH

UNIT = 256
HALF_K = DC // 2
RAW = 4
PAIR_HALVES = 4

UNITS_QK = 2 * M_WIDTH // UNIT
UNITS_QKA = 2 * A_WIDTH // UNIT
UNITS_VO = 2 * M_WIDTH // UNIT
UNITS_VA = A_WIDTH // UNIT
UNITS_GATES = 2 * D // UNIT
UNITS_BRANCH = D // UNIT
UNITS_OUT = D // UNIT
UNIT_QKA = UNITS_QK
UNIT_VO = UNIT_QKA + UNITS_QKA
UNIT_VA = UNIT_VO + UNITS_VO
UNIT_GATES = UNIT_VA + UNITS_VA
UNIT_BRANCH = UNIT_GATES + UNITS_GATES
UNIT_OUT = UNIT_BRANCH + UNITS_BRANCH
UNITS = UNIT_OUT + UNITS_OUT
HALVES = 2 * UNITS

SLOTS = 64
PAIRS = 2 * T
CHUNKS = T // SLOTS
GROUPS_OUT = TT * D // 512
REV = 384

G1_ROW, CONV_ROW, MN_ROW = 0, DC, DC + CONV * DC
G2_ROW = MN_ROW + M_WIDTH // P
PARAM_ROWS = G2_ROW + DC


def bucket_onehot():
    n = np.arange(T)
    half = BUCKETS // 2
    large = half + (np.log(np.maximum(n, 1).astype(np.float32) / half)
                    / np.log(MAX_DIST / half) * (BUCKETS - half)).astype(np.int32)
    bucket = np.where(n < half, n, np.minimum(large, BUCKETS - 1))[::-1]
    return (np.arange(BUCKETS)[:, None] == bucket[None, :]).astype(np.float32)


def first_unit(i, u):
    return isinstance(i, int) and i == 0 and u == 0


def last_unit(i, u):
    return isinstance(i, int) and i > 0 and u == 1


class Steps:

    def __init__(self, eng, sem):
        self.eng, self.sem, self.n, self.loops = eng, sem, 0, []

    def done(self, ins):
        ins.then_inc(self.sem, 1)
        self.n += 1
        value = self.n
        for i, per in self.loops:
            value = i * per + value
        self.eng.wait_ge(self.sem, value)

    @contextmanager
    def loop(self, start, end, per):
        entered = self.n
        with self.eng.Fori(start, end) as i:
            self.n -= start * per
            self.loops.append((i, per))
            yield i
            self.loops.pop()
            assert self.n == entered - start * per + per, (self.n - entered + start * per, per)
        self.n = entered + (end - start) * per


def layer(nc, x, norm1_g, w_in, conv_w, if_bias, mnorm_g, w_branch_m, w_branch_a, w_out, rel_bias,
          norm2_g, w_grp, b_grp, w_exp, b_exp, w1, w3, w2, final_g, onehot, out):
    ctx = ExitStack()
    with ctx:
        place = {"at": 2048, "end": 229 * 1000}

        def sb(name, shape, dt=F32, at=None):
            size = int(np.prod(shape[1:])) * 4
            where = place["at"] if at is None else at
            if at is None:
                place["at"] += (size + 31) // 32 * 32
            assert where + size <= place["end"], (name, where + size)
            return nc.alloc_sbuf_tensor_at(name, shape, dt, offset=where)

        def sem(name):
            return ctx.enter_context(nc.semaphore(name))

        KB = 1024
        AT_TOK = place["at"]
        AT_ACT = AT_TOK + 24 * KB
        AT_WRAW = AT_ACT + 32 * KB
        AT_WSPLIT = AT_WRAW + 32 * KB
        AT_GATES = AT_WSPLIT + 32 * KB
        AT_QK = AT_GATES + 32 * KB
        AT_SMALL = AT_QK + 32 * KB
        place["at"] = AT_SMALL
        tok = sb("tok", [P, 3, TT, M_WIDTH], at=AT_TOK)
        act_split = sb("act_split", [P, DC, 2, T], F32R, at=AT_ACT)
        wraw = sb("wraw", [P, RAW, HALF_K, UNIT], at=AT_WRAW)
        wsplit = sb("wsplit", [P, 2, HALF_K, 2, UNIT], F32R, at=AT_WSPLIT)
        gates = sb("gates", [P, 2 * DC, T], at=AT_GATES)
        xin = sb("xin", [P, TT, D], at=AT_GATES)
        qk = sb("qk", [P, 32, T], at=AT_QK)
        br_split = sb("br_split", [P, DC, 2, T], F32R, at=AT_QK)
        x2 = sb("x2", [P, TT, D], at=AT_TOK)
        xg = sb("xg", [P, DC, PAIRS + SLOTS], at=AT_TOK + 16 * KB)
        w13 = [sb("w13_a", [P, 2, DC, FF], at=AT_GATES), sb("w13_b", [P, 2, DC, FF], at=AT_WRAW)]
        AT_W2 = (place["end"] - 16 * KB) // 32 * 32
        w2s = [[sb("w2_a0", [P, FC, D], at=AT_GATES + 32 * KB), sb("w2_b0", [P, FC, D], at=AT_WRAW + 32 * KB)],
               [sb("w2_a1", [P, FC, D], at=AT_W2), sb("w2_b1", [P, FC, D], at=AT_WRAW + 48 * KB)]]
        h2n = sb("h2n", [P, TT, D], at=AT_QK + 16 * KB)
        h2lo = sb("h2lo", [P, TT, D], F32R, at=AT_QK + 16 * KB)
        h2hi = sb("h2hi", [P, TT, D], F32R, at=AT_WSPLIT + 16 * KB)
        fin = sb("fin", [P, TT, D], at=AT_TOK + 16 * KB)
        fin_g = sb("fin_g", [P, D], at=AT_TOK + 32 * KB)
        x2g = sb("x2g", [P, TT, D], at=AT_GATES)

        ident = sb("ident", [P, P])
        flip = sb("flip", [P, P])
        ones = sb("ones", [P, P])
        upto = sb("upto", [P, P])
        before = sb("before", [P, P])
        mask_ts = sb("mask_ts", [P, P])
        mask_st = sb("mask_st", [P, P])
        params = sb("params", [P, PARAM_ROWS])
        g2T = sb("g2T", [P, DC])
        stat = sb("stat", [P, 64])
        power = sb("power", [P, TT])
        AT_PHASE = place["at"]

        pick = sb("pick", [M_HEADS, M_HEADS, P])
        ifb = sb("ifb", [P, 2 * M_HEADS])
        relb = sb("relb", [BUCKETS, A_HEADS])
        ifg = sb("ifg", [P, TT, 2 * M_HEADS])
        lsg = sb("lsg", [P, TT, M_HEADS])
        lst = sb("lst", [P, TT, M_HEADS])
        cum = sb("cum", [P, TT, M_HEADS])
        aa = sb("aa", [P, TT, M_HEADS])
        aaT = negMT = sb("row_by_head", [M_HEADS, T])
        negM = sb("negM", [P, TT, M_HEADS])
        pick_now = sb("pick_now", [M_HEADS, P])
        bn = sb("bn", [P, TT, 6])
        mean_var = sb("mean_var", [P, TT, 2])
        expm = sb("expm", [P, TT, M_HEADS])
        AT_CONV = place["at"]
        bias_flipped = sb("bias_flipped", [P, A_HEADS, T])
        qk_now = sb("qk_now", [P, 8, T])
        va_now = sb("va_now", [P, TT, 2 * A_DIM])
        vm_now = sb("vm_now", [P, TT, M_DIM + 1])
        decay = scored = sb("decay", [P, REV])
        prob = probT = sb("prob", [P, 2, REV])
        hm = sb("hm", [P, TT, M_DIM])
        AT_EARLY = AT_CONV + 20 * KB
        param_rows = sb("param_rows", [PARAM_ROWS, P], at=AT_EARLY)
        wif_raw = sb("wif_raw", [P, DC, 2 * M_HEADS], at=AT_EARLY + 512)
        wif = sb("wif", [P, DC, 2, 2 * M_HEADS], F32R, at=AT_EARLY + 1024)
        onehot_s = sb("onehot_s", [BUCKETS, T], at=AT_EARLY + 2048)
        rev = sb("rev", [A_HEADS, REV], at=AT_EARLY + 3072)
        if_parts = sb("if_parts", [4 * M_HEADS, 2 * T], at=AT_EARLY + 4608)
        fold = sb("fold", [4 * M_HEADS, 2 * M_HEADS])
        pre = sb("pre", [P, 2, T + CONV - 1], at=AT_CONV + 8 * KB)
        conv = sb("conv", [P, 2, 2, T], at=AT_CONV + 11 * KB)
        csig = sb("csig", [P, 2, T], at=AT_CONV + 16 * KB)
        diag = sb("diag", [P, TT, P], at=AT_CONV + 18 * KB)
        bsum = sb("bsum", [P, 2, 2, T], at=AT_CONV + 4 * KB)
        osum = sb("osum", [P, TT, UNIT], at=AT_CONV + 8 * KB)
        sqs = sb("sqs", [P, TT, UNIT], at=AT_CONV + 10 * KB)
        x2u = sb("x2u", [P, 2, TT, UNIT], at=AT_CONV + 12 * KB)
        x2T = sb("x2T", [P, 2, 2, T], at=AT_CONV + 16 * KB)
        xsq = sb("xsq", [P, TT, D], at=AT_QK)

        place["at"] = AT_PHASE
        wrt = sb("wrt", [P, DC, GROUPS + EXPERTS])
        brt = sb("brt", [P, GROUPS + EXPERTS])
        sq2 = sb("sq2", [P, TT, UNITS_OUT])
        lr = sb("lr", [P, TT, GROUPS + EXPERTS])
        iota_e = sb("iota_e", [P, EXPERTS])
        iota_s = sb("iota_s", [P, PAIRS])
        iota_c = sb("iota_c", [P, CHUNKS, SLOTS])
        assert place["at"] - 3 * KB - 256 < AT_CONV, "what is written while w_out streams"
        rt = sb("rt", [P, 5, TT, EXPERTS])
        sc = sb("sc", [P, 12, TT])
        table = sb("table", [P, 2, EXPERTS])
        oh = sb("oh", [P, TT, 2, EXPERTS])
        mk = sb("mk", [P, TT, 2, EXPERTS], F32R)
        wt = sb("wt", [P, TT, EXPERTS])
        rank = sb("rank", [P, TT, EXPERTS])
        ones_r = sb("ones_r", [P, P], F32R)
        before_r = sb("before_r", [P, P], F32R)
        pos = sb("pos", [P, TT, EXPERTS])
        starts = sb("starts", [P, EXPERTS, CHUNKS])
        starts_i = sb("starts_i", [1, EXPERTS, CHUNKS], I32)
        most_i = sb("most_i", [1, 1], I32)
        AT_SEL = place["at"]
        sel = sb("sel", [P, TT, PAIRS], F32R)
        assert place["at"] <= AT_W2
        xe = sb("xe", [P, 2, DC, SLOTS], at=AT_QK + 16 * KB)
        ys = sb("ys", [P, D], at=AT_QK + 24 * KB)
        place["at"] = AT_SEL
        mix = sb("mix", [P, TT, P])
        mixT = sb("mixT", [P, T])
        sg = sb("sg", [P, P])
        hid = sb("hid", [P, P])
        hidT = sb("hidT", [P, 2, P])
        spare = sb("spare", [P, 1])
        assert place["at"] <= AT_W2

        ps = ctx.enter_context(nc.psum_tensor("ps", [P, 8, 512], F32))
        rev_dram = nc.dram_tensor("rev_dram", (A_HEADS, REV), F32, kind="Internal").ap()

        x_loaded = [sem("x_loaded_0"), sem("x_loaded_1")]
        par_loaded, consts = sem("par_loaded"), sem("consts_ready")
        raw_loaded = [sem(f"raw_loaded{i}") for i in range(RAW)]
        rounded, split, used, acc_free = sem("rounded"), sem("split"), sem("used"), sem("acc_free")
        dve_s, pool_s = sem("dve_step"), sem("pool_step")
        squares, normed, turned, hi_ready, bank_free = (sem(n) for n in (
            "squares", "normed", "turned", "hi_ready", "bank_free"))
        param_turned, param_ready, wif_hi, wif_ready = (sem(n) for n in (
            "param_turned", "param_ready", "wif_hi", "wif_ready"))
        rev_summed, rev_ready, rev_stored, flip_loaded = (sem(n) for n in (
            "rev_summed", "rev_ready", "rev_stored", "bias_flipped_loaded"))
        conv_ready, conv_sig, first_tap, silu_done = (sem(n) for n in (
            "conv_ready", "conv_sigmoid", "first_tap", "silu_done"))
        if_products, if_copied, if_summed, absf_ready, expf_ready, onef_ready, lnf_ready, ls_ready, cum_summed, aa_ready = (
 sem(n) for n in ("if_products", "if_copied", "if_summed", "absf_ready", "expf_ready", "onef_ready", "lnf_ready",
                             "ls_ready", "cum_summed", "aa_ready"))
        aa_turned, aaT_ready, aa_spread, negM_ready, negM_turned, negMT_ready, mt_ready, expm_ready = (
            sem(n) for n in ("aa_turned", "aaT_ready", "aa_spread", "negM_ready", "negM_turned",
                             "negMT_ready", "mt_ready", "expm_ready"))
        o_ready, staged = sem("o_sigmoid_ready"), sem("staged")
        logits, scores, decay_arg, decay_exp = (sem(n) for n in (
            "logits_summed", "scores_summed", "decay_arg", "decay_exp"))
        negmax, prob_exp, prob_ready, scored_ready = (sem(n) for n in (
            "negmax_ready", "prob_exp", "prob_ready", "scored_ready"))
        prob_turned, num_summed, probT_ready, hm_ready, ha_summed, hm_turned, br_hi, br_lo = (
            sem(n) for n in ("prob_turned", "num_summed", "probT_ready", "hm_ready", "ha_summed",
                             "hm_turned", "branch_hi", "branch_lo"))
        root_go, root_done, gate_sig, y_sum, y_hi, y_ready = (sem(n) for n in (
            "root_go", "root_done", "gate_sigmoid", "y_sum", "y_hi", "y_ready"))
        x2_loaded, x2_ready, moe_par, iotas = (sem(n) for n in (
            "x2_loaded", "x2_ready", "expert_params_loaded", "iotas_ready"))
        squares2, x2_turned, x2T_ready, routed, wrt_ready = (sem(n) for n in (
            "squares2", "x2_turned", "x2T_ready", "router_summed", "router_weights_ready"))
        h2hi_ready, h2lo_ready = sem("h2hi_ready"), sem("h2lo_ready")
        gexp_go, gexp_done, mk_ready, rank_summed, sel_ready, xg_summed, xg_act, xg_dve, tab_ready = (
            sem(n) for n in ("group_exp_go", "group_exp_done", "chosen_ready", "rank_summed",
                             "selection_ready", "gathered", "gathered_even", "gathered_odd",
                             "table_ready"))
        w13_loaded = [[sem(f"w13{b}_{kh}_loaded") for kh in ("upper", "lower")] for b in "ab"]
        w2_loaded = [[sem(f"w2_loaded{slot}_{side}") for side in ("left", "right")] for slot in range(2)]
        xe_ready, h_summed, sg_ready, hid_ready, hid_turned, hidT_ready, y_summed, ys_ready = (
            sem(n) for n in ("xe_ready", "hidden_summed", "hidden_sigmoid", "hid_ready", "hid_turned",
                             "hidT_ready", "ye_summed", "ye_ready"))
        upper_used = sem("upper_chunks_used")
        mix_ready, mix_turned, mixT_ready, scattered, added = (sem(n) for n in (
            "mix_ready", "mix_turned", "mixT_ready", "scattered", "added"))
        fing_loaded, squares3, squares_total, out_stored, x2g_ready = (sem(n) for n in (
            "final_g_loaded", "squares3", "squares_total", "out_stored", "x2g_ready"))
        out_ready = [sem("out_ready_0"), sem("out_ready_1")]
        dve_x = sem("dve_expert_step")

        win_v = w_in.rearrange("(h k p) n -> p h k n", h=2, p=P)
        wout_v = w_out.rearrange("(h k p) n -> p h k n", h=2, p=P)
        wbm_v = w_branch_m.rearrange("(k p) n -> p k n", p=P)
        wba_v = w_branch_a.rearrange("(k p) n -> p k n", p=P)
        x_v = x.rearrange("(t p) d -> p t d", p=P)
        out_v = out.rearrange("(t p) d -> p t d", p=P)
        w1_v = w1.rearrange("e (p c) f -> p e c f", c=DC)
        w3_v = w3.rearrange("e (p c) f -> p e c f", c=DC)
        w2_v = w2.rearrange("e (j p) n -> p e j n", p=P)

        def group_place(g):
            return g % 4 // 2, g // 4 * 2 + g % 2

        def halves_sum(bank):
            return bank.rearrange("p (a n) -> p n a", a=2)

        def by_most(eng, experts):
            eng.wait_ge(tab_ready, 1)
            most = eng.value_load(most_i[0:1, 0:1], min_val=0, max_val=T)
            with eng.If(most < SLOTS + 1):
                experts(1)
            with eng.Else():
                experts(CHUNKS)
            eng.end_ifs()

        @contextmanager
        def passes(eng, chunks, steps=None, per=0):
            if chunks == 1:
                yield 0
            elif steps is None:
                with eng.Fori(0, chunks) as c:
                    yield c
            else:
                with steps.loop(0, chunks, per) as c:
                    yield c

        block = ctx.enter_context(nc.Block())

        @block.sync
        def _(sp):
            for t in range(TT):
                sp.dma_start(xin[:, t], x_v[:, t]).then_inc(x_loaded[t], 16)
            sp.wait_ge(par_loaded, 16 * 9)

            def load(slot, src, half):
                if half is not None:
                    sp.wait_ge(split, half + (1 - RAW))
                sp.dma_start(wraw[:, slot], src).then_inc(raw_loaded[slot], 16)

            def pair(col, half):
                for q in range(PAIR_HALVES):
                    load(q, win_v[:, q % 2, :, ds(col + (q // 2) * UNIT, UNIT)],
                         None if half is None else half + q)

            def pairs(start, units, col, unit):
                with sp.Fori(start, units // 2) as i:
                    pair(i * (2 * UNIT) + col, i * PAIR_HALVES + 2 * unit)

            pair(COL_QK, None)
            sp.wait_ge(rev_ready, 1)
            sp.dma_start(rev_dram, rev[:]).then_inc(rev_stored, 16)
            sp.wait_ge(rev_stored, 16)
            for h in range(A_HEADS):
                sp.dma_start(bias_flipped[:, h], bass.AP(tensor=rev_dram.tensor, offset=h * REV,
                                                         ap=[[1, P], [1, T]])).then_inc(flip_loaded, 16)
            pairs(1, UNITS_QK, COL_QK, 0)
            pairs(0, UNITS_QKA, COL_QA, UNIT_QKA)
            pairs(0, UNITS_VO, COL_V, UNIT_VO)
            pairs(0, UNITS_VA, COL_VA, UNIT_VA)
            pairs(0, UNITS_GATES, COL_GATES, UNIT_GATES)
            with sp.Fori(0, UNITS_BRANCH // 2) as i:
                for q in range(PAIR_HALVES):
                    load(q, (wbm_v, wba_v)[q % 2][:, :, ds(i * (2 * UNIT) + (q // 2) * UNIT, UNIT)],
                         i * PAIR_HALVES + 2 * UNIT_BRANCH + q)
            sp.wait_ge(br_lo, M_HEADS + 1)
            sp.dma_start(x2[:], x_v).then_inc(x2_loaded, 16)
            for q in range(PAIR_HALVES):
                load(q, wout_v[:, q // 2, :, (q % 2) * UNIT:(q % 2 + 1) * UNIT], 2 * UNIT_OUT + q)
            with sp.Fori(1, UNITS_OUT // 2) as i:
                for q in range(PAIR_HALVES):
                    load(q, wout_v[:, q % 2, :, ds(i * (2 * UNIT) + (q // 2) * UNIT, UNIT)],
                         i * PAIR_HALVES + 2 * UNIT_OUT + q)

            def load_hidden(b, e, kh):
                ks = slice(kh * HALF_K, (kh + 1) * HALF_K)
                for w, w_v in enumerate((w1_v, w3_v)):
                    sp.dma_start(w13[b][:, w, ks], w_v[:, e, ks]).then_inc(w13_loaded[b][kh], 16)

            def load_rows(slot, e_of, experts=(0, 1)):
                for h in range(2):
                    cols = slice(h * (D // 2), (h + 1) * (D // 2))
                    for b in experts:
                        sp.dma_start(w2s[slot][b][:, :, cols],
                                     w2_v[:, e_of(b), :, cols]).then_inc(w2_loaded[slot][h], 16)

            sp.wait_ge(y_ready, UNITS_BRANCH + 1)
            for kh in range(2):
                load_hidden(0, 0, kh)
            sp.wait_ge(used, HALVES)
            for kh in range(2):
                load_hidden(1, 1, kh)
            load_rows(0, lambda b: b)
            sp.wait_ge(routed, 1)
            load_rows(1, lambda b: b + 2, (0,))
            sp.wait_ge(xg_summed, DC)
            load_rows(1, lambda b: b + 2, (1,))

            def experts(chunks):
                def next_hidden(i):
                    for b in range(2):
                        sp.wait_ge(upper_used, i * (2 * chunks) + (2 * chunks - 1 + b))
                        load_hidden(b, ds(i * 2 + (b + 2), 1), 0)
                        sp.wait_ge(h_summed, i * (2 * chunks) + (2 * chunks + b))
                        load_hidden(b, ds(i * 2 + (b + 2), 1), 1)

                next_hidden(0)
                with sp.Fori(0, EXPERTS // 4 - 1) as j:
                    for slot in range(2):
                        i = j * 2 + (slot + 1)
                        next_hidden(i)
                        sp.wait_ge(y_summed, i * (2 * chunks) + 1)
                        load_rows(slot, lambda b: ds(i * 2 + (b + 2), 1))
                sp.wait_ge(xe_ready, EXPERTS * chunks)
                sp.dma_start(fin_g[:], final_g.partition_broadcast(P)).then_inc(fing_loaded, 16)

            by_most(sp, experts)
            for h in range(2):
                for t in range(TT):
                    cols = slice(h * (D // 2), (h + 1) * (D // 2))
                    sp.wait_ge(out_ready[t], h + 1)
                    sp.dma_start(out_v[:, t, cols], fin[:, t, cols]).then_inc(out_stored, 16)
            sp.wait_ge(out_stored, 16 * 2 * TT)

        @block.gpsimd
        def _(pool):
            steps = Steps(pool, pool_s)
            for primed in (silu_done, hm_turned, ha_summed, br_lo, y_sum, y_ready, x2_ready, h_summed,
                           mix_turned, hid_turned, hid_ready, hidT_ready, mixT_ready, y_summed, ys_ready, scattered, added):
                pool.sem_inc(primed, 1)
            for m in (ident, flip, before, mask_ts, mask_st, pick):
                last = pool.memset(m[:], 0.0)
            pool.memset(upto[:], 1.0)
            pool.memset(power[:], -0.5)
            steps.done(pool.memset(ones[:], 1.0))

            def choose(m, keep, fill, base, pattern, mult):
                return pool.affine_select(out=m[:], in_=m[:], compare_op=keep, fill=fill, base=base,
                                          pattern=pattern, channel_multiplier=mult)

            choose(ident, ALU.not_equal, 1.0, 0, [[-1, P]], 1)
            choose(flip, ALU.not_equal, 1.0, -(P - 1), [[1, P]], 1)
            choose(upto, ALU.is_ge, 0.0, 0, [[1, P]], -1)
            choose(before, ALU.is_ge, 1.0, 0, [[-1, P]], 1)
            choose(mask_ts, ALU.is_ge, MASKED, 0, [[-1, P]], 1)
            choose(mask_st, ALU.is_ge, MASKED, 0, [[1, P]], -1)
            choose(pick, ALU.not_equal, 1.0, 0, [[-1, M_HEADS], [0, P]], 1).then_inc(consts, 1)

            def root(col, n, turn):
                pool.wait_ge(root_go, turn)
                pool.tensor_tensor(stat[:, col:col + n], stat[:, col:col + n], power[:, 0:n], ALU.pow).then_inc(root_done, 1)

            root(2, TT, 1)
            pool.wait_ge(acc_free, UNIT_VO)
            pool.memset(vm_now[:, :, M_DIM:], 1.0)
            with steps.loop(0, M_HEADS, 1) as i:
                pool.wait_ge(hm_turned, i + 1)
                pool.wait_ge(ha_summed, i * 2 + 1)
                pool.tensor_copy(pick_now[:], pick[:, ds(i, 1)])
                pool.tensor_copy(qk_now[:, 0:4], qk[:, ds(i * 4, 4)])
                steps.done(pool.tensor_copy(qk_now[:, 4:8], qk[:, ds(i * 4 + 16, 4)]))
                q_now = qk_now[:, 4:8].rearrange("p (a k) t -> p a k t", k=2)[:, :, 0]
                pool.wait_ge(acc_free, UNIT_VA)
                pool.tensor_copy(vm_now[:, :, 0:M_DIM], tok[:, 0, :, ds(i * M_DIM, M_DIM)])
                pool.tensor_scalar(q_now, q_now, float(A_DIM) ** -0.5, None, ALU.mult)
                pool.wait_ge(acc_free, UNIT_GATES)
                pool.tensor_copy(va_now[:], tok[:, 2, :, ds(i * 2 * A_DIM, 2 * A_DIM)]).then_inc(staged, 1)
                root(36, 2, i + 2)

            pool.wait_ge(x2_ready, UNITS_OUT + 1)
            pool.iota(iota_e[:], pattern=[[1, EXPERTS]], base=-SLOTS, channel_multiplier=0,
                      allow_small_or_imprecise_dtypes=True)
            pool.iota(iota_s[:], pattern=[[1, PAIRS]], base=0, channel_multiplier=0,
                      allow_small_or_imprecise_dtypes=True)
            pool.iota(iota_c[:], pattern=[[SLOTS, CHUNKS], [1, SLOTS]], base=0,
                      channel_multiplier=0, allow_small_or_imprecise_dtypes=True).then_inc(iotas, 1)
            root(22, TT, M_HEADS + 2)
            for t, cols in ((0, slice(0, D)), (1, slice(0, D // 2))):
                pool.wait_ge(h2hi_ready, t + 1)
                pool.tensor_tensor(h2lo[:, t, cols], h2n[:, t, cols], h2hi[:, t, cols].bitcast(F32),
                                   ALU.subtract).then_inc(h2lo_ready, 1)
            root(42, TT, M_HEADS + 3)

        @block.scalar
        def _(act):
            act.dma_start(param_rows[G1_ROW:CONV_ROW], norm1_g.rearrange("(r c) -> r c", c=P)).then_inc(par_loaded, 16)
            act.dma_start(param_rows[CONV_ROW:MN_ROW], conv_w.rearrange("j (r c) -> (j r) c", c=P)).then_inc(par_loaded, 16)
            act.dma_start(param_rows[MN_ROW:G2_ROW], mnorm_g.rearrange("(r c) -> r c", c=P)).then_inc(par_loaded, 16)
            act.dma_start(param_rows[G2_ROW:PARAM_ROWS], norm2_g.rearrange("(r c) -> r c", c=P)).then_inc(par_loaded, 16)
            act.dma_start(wif_raw[:], w_in[:, COL_IF:COL_QA].rearrange("(k p) n -> p k n", p=P)).then_inc(par_loaded, 16)
            act.dma_start(ifb[:], if_bias.partition_broadcast(P)).then_inc(par_loaded, 16)
            act.dma_start(relb[:], rel_bias).then_inc(par_loaded, 16)
            act.dma_start(onehot_s[:], onehot).then_inc(par_loaded, 16)
            act.dma_start(g2T[:], norm2_g.rearrange("(p c) -> p c", c=DC)).then_inc(par_loaded, 16)

            for t in range(TT):
                act.wait_ge(x_loaded[t], 16)
                act.activation(xsq[:, t], xin[:, t], ACT.Square, accum_out=stat[:, t:t + 1]).then_inc(squares, 1)
            act.wait_ge(par_loaded, 16 * 9)
            act.activation(wif[:, :, 0], wif_raw[:], ACT.Copy).then_inc(wif_hi, 1)

            def round_half(q, turn, half):
                act.wait_ge(raw_loaded[q % RAW], turn)
                if half is not None:
                    act.wait_ge(used, half - 1)
                act.activation(wsplit[:, q % 2, :, 0], wraw[:, q % RAW], ACT.Copy).then_inc(rounded, 1)

            def round_ahead(u, unit, i):
                for q in (2 * u + 2, 2 * u + 3):
                    round_half(q, i * 16 + (16 * (unit // 2 + q // RAW) + 16),
                               i * PAIR_HALVES + (2 * unit + q))

            for g in range(DC // 2):
                if g % (DC // 4) == 0:
                    round_half(g // (DC // 4), 16, None)
                    act.wait_ge(param_ready, 1)
                act.wait_ge(turned, g + 1)
                for c in range(2):
                    act.activation(act_split[:, 2 * g + c, 0], ps[:, g, c * T:(c + 1) * T], ACT.Copy,
                                   scale=params[:, G1_ROW + 2 * g + c:G1_ROW + 2 * g + c + 1]).then_inc(hi_ready, 1)
            def round_one(unit, q, i):
                round_half(q, i * 16 + (16 * (unit // 2 + q // RAW) + 16), i * PAIR_HALVES + (2 * unit + q))

            def conv_sigmoid(u, n):
                act.wait_ge(conv_ready, n + 1)
                act.wait_ge(silu_done, n + 1)
                act.activation(csig[:], conv[:, u], ACT.Sigmoid).then_inc(conv_sig, 1)

            def conv_pair(i):
                for u in range(2):
                    n = i * 2 + u
                    round_one(0, 2 * u + 3, i)
                    if not first_unit(i, u):
                        conv_sigmoid(1 - u, n - 1)
                    if not last_unit(i, u):
                        round_one(0, 2 * u + 4, i)
                    act.wait_ge(acc_free, n + 1)
                    for b in range(2):
                        last = act.activation(conv[:, u, b], pre[:, b, 0:T], ACT.Copy,
                                              scale=params[:, ds(i * 4 + (CONV_ROW + 2 * u + b), 1)])
                    last.then_inc(first_tap, 1)

            round_one(0, 2, 0)
            conv_pair(0)
            with act.Fori(1, UNITS_QK // 2 - 1) as i:
                conv_pair(i)
            conv_pair(UNITS_QK // 2 - 1)
            conv_sigmoid(1, UNITS_QK - 1)
            for u in range(2):
                round_ahead(u, UNIT_QKA, 0)
            act.wait_ge(absf_ready, 1)
            act.activation(lsg[:], lsg[:], ACT.Exp, scale=-1.0).then_inc(expf_ready, 1)
            act.wait_ge(onef_ready, 1)
            act.activation(lsg[:], lsg[:], ACT.Ln).then_inc(lnf_ready, 1)
            for unit, start, units in ((UNIT_QKA, 1, UNITS_QKA), (UNIT_VO, 0, UNITS_VO)):
                with act.Fori(start, units // 2) as i:
                    for u in range(2):
                        round_ahead(u, unit, i)
            act.wait_ge(acc_free, UNIT_VA)
            act.activation(tok[:, 1], tok[:, 1], ACT.Sigmoid).then_inc(o_ready, 1)
            for u in range(UNITS_VA - 1):
                round_ahead(u % 2, UNIT_VA, u // 2)
            round_one(UNIT_VA, 4, UNITS_VA // 2 - 1)
            act.wait_ge(mt_ready, 1)
            act.activation(expm[:], expm[:], ACT.Exp, scale=-1.0).then_inc(expm_ready, 1)
            round_one(UNIT_VA, 5, UNITS_VA // 2 - 1)

            with act.Fori(0, M_HEADS) as i:
                def ahead(q):
                    round_half(q, i * 32 + (16 * (UNIT_GATES // 2 + q // RAW) + 16),
                               i * 8 + (2 * UNIT_GATES + q))

                ahead(2)
                act.wait_ge(decay_arg, i + 1)
                act.activation(decay[:], decay[:], ACT.Exp).then_inc(decay_exp, 1)
                ahead(3)
                for a in range(2):
                    act.wait_ge(negmax, i * 2 + (a + 1))
                    act.activation(prob[:, a, 0:P], ps[:, 4 + a, 0:P], ACT.Exp,
                                   bias=stat[:, 8 + 2 * a:9 + 2 * a], accum_out=stat[:, 12 + 2 * a:13 + 2 * a])
                    act.activation(prob[:, a, P:REV], ps[:, 4 + a, P:REV], ACT.Exp,
                                   bias=stat[:, 9 + 2 * a:10 + 2 * a],
                                   accum_out=stat[:, 13 + 2 * a:14 + 2 * a]).then_inc(prob_exp, 1)
                for q in range(4, 8):
                    ahead(q)
                for a in range(2):
                    act.wait_ge(ha_summed, i * 2 + (a + 2))
                    act.activation(br_split[:, ds(i * 2 + (8 + a), 1), 0], ps[:, 4 + a, 0:T], ACT.Copy).then_inc(br_hi, 1)
                act.wait_ge(hm_turned, i + 2)
                for c in range(2):
                    act.activation(br_split[:, ds(i * 2 + c, 1), 0], ps[:, 6, c * T:(c + 1) * T], ACT.Copy,
                                   scale=params[:, ds(i * 2 + (MN_ROW + c), 1)]).then_inc(br_hi, 1)
                ahead(8)
                act.wait_ge(acc_free, i * 4 + (UNIT_GATES + 2))
                act.activation(gates[:, ds(i * 8, 4)], gates[:, ds(i * 8, 4)], ACT.Sigmoid)
                ahead(9)
                act.wait_ge(acc_free, i * 4 + (UNIT_GATES + 4))
                act.activation(gates[:, ds(i * 8 + 4, 4)], gates[:, ds(i * 8 + 4, 4)], ACT.Sigmoid).then_inc(gate_sig, 1)

            round_one(UNIT_BRANCH, 2, 0)

            def y_round(n):
                act.wait_ge(y_sum, n + 2)
                act.activation(act_split[:, ds(n * 2, 2), 0], bsum[:, 0], ACT.Copy).then_inc(y_hi, 1)

            def branch_pair(i):
                for u in range(2):
                    round_one(UNIT_BRANCH, 2 * u + 3, i)
                    if not first_unit(i, u):
                        y_round(i * 2 + (u - 1))
                    round_one(UNIT_BRANCH, 2 * u + 4, i)

            branch_pair(0)
            with act.Fori(1, UNITS_BRANCH // 2) as i:
                branch_pair(i)
            y_round(UNITS_BRANCH - 1)
            act.dma_start(wrt[:, :, 0:GROUPS], w_grp.rearrange("(c p) n -> p c n", p=P)).then_inc(moe_par, 16)
            act.dma_start(wrt[:, :, GROUPS:], w_exp.rearrange("(c p) n -> p c n", p=P)).then_inc(moe_par, 16)
            act.dma_start(brt[:, 0:GROUPS], b_grp.partition_broadcast(P)).then_inc(moe_par, 16)
            act.dma_start(brt[:, GROUPS:], b_exp.partition_broadcast(P)).then_inc(moe_par, 16)

            def x2T_copy(u, n):
                act.wait_ge(x2_turned, n + 1)
                act.activation(x2T[:, u], ps[:, u], ACT.Copy).then_inc(x2T_ready, 1)

            def out_unit(i, u, end=False):
                n = i * 2 + u
                if not (end and u == 1):
                    round_one(UNIT_OUT, 2 * u + 3, i)
                if not first_unit(i, u):
                    x2T_copy(1 - u, n - 1)
                if not end:
                    round_one(UNIT_OUT, 2 * u + 4, i)
                act.wait_ge(x2_ready, n + 2)
                act.activation(x2[:, :, ds(i * (2 * UNIT) + u * UNIT, UNIT)], x2u[:, u], ACT.Copy)
                if not first_unit(i, u):
                    act.wait_ge(squares2, n)
                for t in range(TT):
                    last = act.activation(sqs[:, t], x2u[:, u, t], ACT.Square, accum_out=sq2[:, t, ds(n, 1)])
                last.then_inc(squares2, 1)

            for u in range(2):
                out_unit(0, u)
            with act.Fori(1, UNITS_OUT // 2 - 1) as i:
                for u in range(2):
                    out_unit(i, u)
            out_unit(UNITS_OUT // 2 - 1, 0, end=True)
            out_unit(UNITS_OUT // 2 - 1, 1, end=True)
            x2T_copy(1, UNITS_OUT - 1)

            act.wait_ge(root_done, M_HEADS + 2)
            for t in range(TT):
                act.activation(h2n[:, t], x2[:, t], ACT.Copy, scale=stat[:, 22 + t:23 + t])
            for t in range(TT):
                act.activation(h2hi[:, t], x2[:, t], ACT.Copy, scale=stat[:, 22 + t:23 + t]).then_inc(h2hi_ready, 1)
            act.wait_ge(gexp_go, 1)
            for t in range(TT):
                last = act.activation(rt[:, 4, t, 0:GROUPS], lr[:, t, 0:GROUPS], ACT.Exp, bias=sc[:, 1, t:t + 1],
                                      accum_out=sc[:, 2, t:t + 1])
            last.then_inc(gexp_done, 1)
            act.wait_ge(gexp_go, 2)
            act.activation(sc[:, 6], sc[:, 5], ACT.Exp).then_inc(gexp_done, 1)
            for c in range(DC):
                if c % 2 == 0:
                    act.wait_ge(xg_summed, c + 1)
                    act.activation(xg[:, c, 0:PAIRS], ps[:, c % 8], ACT.Copy, scale=g2T[:, c:c + 1]).then_inc(xg_act, 1)

            def experts(chunks):
                with act.Fori(0, EXPERTS // 2) as i:
                    with passes(act, chunks) as c:
                        s = i * chunks + c
                        act.activation(spare[:], ident[:, 0:1], ACT.Sigmoid)
                        for b in range(2):
                            n = s * 2 + b
                            act.wait_ge(h_summed, n + 2)
                            act.wait_ge(hid_ready, n + 1)
                            act.activation(sg[:], ps[:, 0, 0:P], ACT.Sigmoid).then_inc(sg_ready, 1)
                            act.wait_ge(hid_turned, n + 2)
                            act.wait_ge(y_summed, s * 2 + 1)
                            act.activation(hidT[:, b], ps[:, 1, 0:P], ACT.Copy).then_inc(hidT_ready, 1)
                        act.wait_ge(mix_turned, s + 2)
                        act.wait_ge(scattered, s * GROUPS_OUT + 1)
                        act.activation(mixT[:], ps[:, 1, P:3 * P], ACT.Copy).then_inc(mixT_ready, 1)
                        for h in range(2):
                            act.wait_ge(y_summed, s * 2 + (h + 2))
                            act.activation(ys[:, h * (D // 2):(h + 1) * (D // 2)],
                                           ps[:, 2 + 2 * h:4 + 2 * h].rearrange("p a n -> p (a n)"),
                                           ACT.Copy).then_inc(ys_ready, 1)
                for g in range(GROUPS_OUT):
                    t, n = group_place(g)
                    act.wait_ge(added, (EXPERTS // 2 * chunks - 1) * GROUPS_OUT + g + 2)
                    cols = slice(n * 512, (n + 1) * 512)
                    act.activation(fin[:, t, cols], x2[:, t, cols], ACT.Square,
                                   accum_out=sq2[:, t, n:n + 1]).then_inc(squares3, 1)

            by_most(act, experts)
            act.wait_ge(root_done, M_HEADS + 3)
            act.wait_ge(x2g_ready, GROUPS_OUT)
            act.wait_ge(squares3, GROUPS_OUT)
            for h in range(2):
                cols = slice(h * (D // 2), (h + 1) * (D // 2))
                act.activation(fin[:, 0, cols], x2g[:, 0, cols], ACT.Copy, scale=stat[:, 42:43]).then_inc(out_ready[0], 1)

        @block.tensor
        def _(pe):
            pe.wait_ge(consts, 1)
            pe.wait_ge(par_loaded, 16 * 9)
            pe.transpose(ps[:, 7, 0:PARAM_ROWS], param_rows[:], ident[0:PARAM_ROWS, 0:PARAM_ROWS]).then_inc(param_turned, 1)
            pe.matmul(ps[0:A_HEADS, 6, 0:T], relb[:], onehot_s[:], start=True, stop=True).then_inc(rev_summed, 1)
            pe.wait_ge(param_ready, 1)
            pe.wait_ge(rev_ready, 1)
            for t in range(TT):
                pe.wait_ge(x_loaded[t], 16)
                pe.wait_ge(normed, t + 1)
            for g in range(DC // 2):
                for c in range(2):
                    for t in range(TT):
                        last = pe.matmul(ps[:, g, c * T + t * P:c * T + (t + 1) * P],
                                         xin[:, t, (2 * g + c) * P:(2 * g + c + 1) * P], diag[:, t],
                                         start=True, stop=True)
                last.then_inc(turned, 1)

            def channel_half(banks, q, first, last_half):
                w = wsplit[:, q % 2]
                for b in range(2):
                    for k in range(HALF_K):
                        a = act_of(q, k)
                        pe.matmul(banks[b], w[:, k, 0, b * P:(b + 1) * P], a, start=first and k == 0,
                                  stop=False)
                        last = pe.matmul(banks[b][:, 0:T], w[:, k, 1, b * P:(b + 1) * P], a[:, 0],
                                         start=False, stop=last_half and k == HALF_K - 1)
                last.then_inc(used, 1)

            def act_of(q, k):
                return act_split[:, (q % 2) * HALF_K + k]

            def token_half(banks, q, first, last_half, rows_half=None):
                rows_half = q % 2 if rows_half is None else rows_half
                w = wsplit[:, q % 2]
                for t in range(TT):
                    for k in range(HALF_K):
                        a = act_of(rows_half, k)
                        pe.matmul(banks[t], a[:, 0, t * P:(t + 1) * P], w[:, k], start=first and k == 0,
                                  stop=False)
                        last = pe.matmul(banks[t][:, 0:UNIT], a[:, 1, t * P:(t + 1) * P], w[:, k, 0],
                                         start=False, stop=last_half and k == HALF_K - 1)
                last.then_inc(used, 1)

            def half(kind, q, half_no, unit_no, bank=0):
                pe.wait_ge(split, half_no + 1)
                if q % 2 == 0 and unit_no is not None:
                    pe.wait_ge(acc_free, unit_no - 1)
                u = (q // 2) % 2
                kind([ps[:, bank + 2 * u], ps[:, bank + 2 * u + 1]], q, q % 2 == 0, q % 2 == 1)

            def stage_pair(kind, unit, i):
                for q in range(PAIR_HALVES):
                    half(kind, q, i * PAIR_HALVES + (2 * unit + q), i * 2 + (unit + q // 2))

            def stage(kind, unit, start, units):
                with pe.Fori(start, units // 2) as i:
                    stage_pair(kind, unit, i)

            for q in range(PAIR_HALVES):
                pe.wait_ge(bank_free, min(DC, (q + 1) * HALF_K))
                half(channel_half, q, q, None)
            stage(channel_half, 0, 1, UNITS_QK)

            pe.wait_ge(wif_ready, 1)
            for k in range(DC):
                last = pe.matmul(ps[0:4 * M_HEADS, 4], wif[:, k].rearrange("p a n -> p (a n)"),
                                 act_split[:, k].rearrange("p a t -> p (a t)"), start=k == 0, stop=k == DC - 1)
            last.then_inc(if_products, 1)
            stage_pair(channel_half, UNIT_QKA, 0)
            pe.wait_ge(if_copied, 1)
            for t in range(TT):
                for a in range(2):
                    last = pe.matmul(ps[:, 5, t * 2 * M_HEADS:(t + 1) * 2 * M_HEADS],
                                     if_parts[:, a * T + t * P:a * T + (t + 1) * P], fold[:], start=a == 0, stop=a == 1)
            last.then_inc(if_summed, 1)
            stage(channel_half, UNIT_QKA, 1, UNITS_QKA)

            pe.wait_ge(ls_ready, 1)
            pe.matmul(ps[:, 5, 0:4], upto[:], lst[:, 0], start=True, stop=True)
            pe.matmul(ps[:, 5, 4:8], ones[:], lst[:, 0], start=True, stop=False)
            pe.matmul(ps[:, 5, 4:8], upto[:], lst[:, 1], start=False, stop=True).then_inc(cum_summed, 1)
            stage(token_half, UNIT_VO, 0, UNITS_VO - 2)
            pe.wait_ge(aa_ready, 1)
            for t in range(TT):
                last = pe.transpose(ps[0:M_HEADS, 6, t * P:(t + 1) * P], aa[:, t], ident[:])
            last.then_inc(aa_turned, 1)
            stage_pair(token_half, UNIT_VO, UNITS_VO // 2 - 1)
            pe.wait_ge(aaT_ready, 1)
            for h in range(M_HEADS):
                last = pe.matmul(ps[:, 4 + h // 2, (h % 2) * T:(h % 2 + 1) * T], pick[:, h], aaT[:],
                                 start=True, stop=True)
            last.then_inc(aa_spread, 1)
            stage(token_half, UNIT_VA, 0, UNITS_VA)
            pe.wait_ge(negM_ready, 1)
            for t in range(TT):
                last = pe.transpose(ps[0:M_HEADS, 7, t * P:(t + 1) * P], negM[:, t], ident[:])
            last.then_inc(negM_turned, 1)
            pe.wait_ge(flip_loaded, 16 * A_HEADS)

            with pe.Fori(0, M_HEADS) as i:
                def gate_half(q):
                    half(channel_half, q, i * 8 + (2 * UNIT_GATES + q), i * 4 + (UNIT_GATES + q // 2))

                gate_half(0)
                pe.wait_ge(staged, i + 1)
                pe.wait_ge(br_lo, i + 1)
                for a in range(2):
                    q_h, k_h, bias = qk_now[:, 4 + 2 * a], qk_now[:, 5 + 2 * a], bias_flipped[:, ds(i * 2 + a, 1)]
                    bank = ps[:, 4 + a]
                    pe.matmul(bank[:, 0:P], q_h[:, 0:P], k_h[:, 0:P], start=True, stop=False)
                    pe.matmul(bank[:, 0:P], flip[:], bias[:, 0, P:T], start=False, stop=True)
                    pe.matmul(bank[:, P:REV], q_h[:, P:T], k_h[:], start=True, stop=False)
                    pe.matmul(bank[:, P:REV], flip[:], bias[:, 0], start=False, stop=True).then_inc(logits, 1)
                for k in range(2):
                    pe.matmul(ps[:, 6, 0:T], qk_now[:, 2 + k, 0:P], qk_now[:, k], start=k == 0, stop=k == 1)
                for k in range(2):
                    pe.matmul(ps[:, 6, T:REV], qk_now[:, 2 + k, P:T], qk_now[:, k, P:T], start=k == 0, stop=k == 1)
                pe.wait_ge(negMT_ready, 1)
                pe.matmul(ps[:, 7, 0:T], pick_now[:], negMT[:], start=True, stop=True).then_inc(scores, 1)
                for q in (1, 2, 3):
                    gate_half(q)
                for a in range(2):
                    pe.wait_ge(prob_ready, i * 2 + (a + 1))
                    for c in range(3):
                        last = pe.transpose(ps[:, 4 + a, c * P:(c + 1) * P], prob[:, a, c * P:(c + 1) * P], ident[:])
                    last.then_inc(prob_turned, 1)
                pe.wait_ge(scored_ready, i + 1)
                for t, parts in enumerate(([(0, 0)], [(1, 0), (2, 1)])):
                    for n, (c, s) in enumerate(parts):
                        last = pe.matmul(ps[:, 6 + t, 0:M_DIM + 1], scored[:, c * P:(c + 1) * P], vm_now[:, s],
                                         start=n == 0, stop=n == len(parts) - 1)
                last.then_inc(num_summed, 1)
                gate_half(4)
                gate_half(5)
                for a in range(2):
                    pe.wait_ge(probT_ready, i * 2 + (a + 1))
                    v_h = va_now[:, :, a * P:(a + 1) * P]
                    pe.matmul(ps[:, 4 + a, 0:T], v_h[:, 0], probT[:, a, 0:T], start=True, stop=False)
                    pe.matmul(ps[:, 4 + a, P:T], v_h[:, 1], probT[:, a, T:REV], start=False, stop=True).then_inc(ha_summed, 1)
                pe.wait_ge(hm_ready, i + 1)
                for c in range(2):
                    for t in range(TT):
                        last = pe.transpose(ps[:, 6, c * T + t * P:c * T + (t + 1) * P], hm[:, t, c * P:(c + 1) * P], ident[:])
                last.then_inc(hm_turned, 1)
                gate_half(6)
                gate_half(7)

            pe.wait_ge(br_lo, M_HEADS + 1)
            with pe.Fori(0, UNITS_BRANCH // 2) as i:
                for q in range(PAIR_HALVES):
                    pe.wait_ge(split, i * PAIR_HALVES + (2 * UNIT_BRANCH + q + 1))
                    if q % 2 == 0:
                        pe.wait_ge(acc_free, i * 2 + (UNIT_BRANCH + q // 2 - 1))
                    w = wsplit[:, q % 2]
                    for b in range(2):
                        bank = ps[:, 4 * (1 - q // 2) + 2 * (q % 2) + b]
                        for k in range(HALF_K):
                            a = br_split[:, (q % 2) * HALF_K + k]
                            pe.matmul(bank, w[:, k, 0, b * P:(b + 1) * P], a, start=k == 0, stop=False)
                            last = pe.matmul(bank[:, 0:T], w[:, k, 1, b * P:(b + 1) * P], a[:, 0],
                                             start=False, stop=k == HALF_K - 1)
                    last.then_inc(used, 1)
            n_r = GROUPS + EXPERTS

            def turn_x2(u, n):
                pe.wait_ge(x2_ready, n + 2)
                for c in range(2):
                    for t in range(TT):
                        last = pe.transpose(ps[:, u, c * T + t * P:c * T + (t + 1) * P],
                                            x2u[:, u, t, c * P:(c + 1) * P], ident[:])
                last.then_inc(x2_turned, 1)

            def route(i, u):
                pe.wait_ge(x2T_ready, i * 2 + (u + 1))
                for t in range(TT):
                    for c in range(2):
                        last = pe.matmul(ps[:, 2 + u, ds(i * (TT * n_r) + t * n_r, n_r)], x2T[:, u, c, t * P:(t + 1) * P],
                                         wrt[:, ds(i * 4 + (2 * u + c), 1)].rearrange("p c n -> p (c n)"),
                                         start=c == 0, stop=c == 1)
                return last

            def out_pair(i):
                for u in range(2):
                    half(token_half, 2 * u, i * PAIR_HALVES + (2 * UNIT_OUT + 2 * u), i * 2 + (UNIT_OUT + u), bank=4)
                    route(i - 1, u)
                    half(token_half, 2 * u + 1, i * PAIR_HALVES + (2 * UNIT_OUT + 2 * u + 1), None, bank=4)
                    turn_x2(1 - u, i * 2 + (u - 1))

            pe.wait_ge(acc_free, UNIT_OUT - 1)
            pe.wait_ge(y_ready, UNITS_BRANCH // 2 + 1)
            for q in range(PAIR_HALVES):
                if q == 2:
                    pe.wait_ge(y_ready, UNITS_BRANCH + 1)
                u, rows_half = q % 2, q // 2
                pe.wait_ge(split, 2 * UNIT_OUT + q + 1)
                token_half([ps[:, 4 + 2 * u], ps[:, 5 + 2 * u]], q, rows_half == 0, rows_half == 1, rows_half)
            turn_x2(0, 0)
            pe.wait_ge(wrt_ready, 1)
            with pe.Fori(1, UNITS_OUT // 2) as i:
                out_pair(i)
            turn_x2(1, UNITS_OUT - 1)
            for u in range(2):
                last = route(UNITS_OUT // 2 - 1, u)
            last.then_inc(routed, 1)

            pe.wait_ge(mk_ready, 1)
            pe.matmul(ps[:, 1, 0:EXPERTS], before_r[:], mk[:, 0, 0], start=True, stop=True)
            pe.matmul(ps[:, 1, EXPERTS:2 * EXPERTS], ones_r[:], mk[:, 0, 0], start=True, stop=False)
            pe.matmul(ps[:, 1, EXPERTS:2 * EXPERTS], before_r[:], mk[:, 1, 0], start=False, stop=True)
            for t in range(TT):
                last = pe.matmul(ps[:, 1, 2 * EXPERTS:4 * EXPERTS], ones_r[:], mk[:, t].rearrange("p k e -> p (k e)"),
                                 start=t == 0, stop=t == TT - 1)
            last.then_inc(rank_summed, 1)
            pe.wait_ge(sel_ready, 1)
            pe.wait_ge(h2lo_ready, TT)
            parts = [part[:].rearrange("p t (q c) -> p t c q", c=DC) for part in (h2hi, h2lo)]
            for c in range(DC):
                if c >= 8:
                    pe.wait_ge((xg_act, xg_dve)[c % 2], (c - 8) // 2 + 1)
                for t in range(TT):
                    for n, part in enumerate(parts):
                        last = pe.matmul(ps[:, c % 8], part[:, t, c], sel[:, t], start=t == 0 and n == 0,
                                         stop=t == TT - 1 and n == 1)
                last.then_inc(xg_summed, 1)

            def hidden(i, s, b):
                pe.wait_ge(xe_ready, s * 2 + (b + 1))
                pe.wait_ge(hid_ready, s * 2 + (b + 1))
                for k in range(DC):
                    if k % HALF_K == 0:
                        pe.wait_ge(w13_loaded[b][k // HALF_K], i * 32 + 32)
                    for f in range(FC):
                        last = pe.matmul(
                            ps[f * SLOTS:(f + 1) * SLOTS, 0, 0:2 * P].rearrange("p (w f) -> p w f", w=2),
                            xe[:, b, k], w13[b][:, :, k, f * P:(f + 1) * P], start=k == 0, stop=k == DC - 1)
                    if k == HALF_K - 1:
                        last.then_inc(upper_used, 1)
                last.then_inc(h_summed, 1)

            def turn(s, b):
                pe.wait_ge(hidT_ready, s * 2 + (b + 1))
                if b == 0:
                    pe.wait_ge(mixT_ready, s + 1)
                if b == 1:
                    pe.wait_ge(mix_ready, s + 1)
                    for t in range(TT):
                        last = pe.transpose(ps[:, 1, P + t * P:P + (t + 1) * P], mix[:, t], ident[:])
                    last.then_inc(mix_turned, 1)
                pe.wait_ge(hid_ready, s * 2 + (b + 2))
                pe.transpose(ps[:, 1, 0:P], hid[:], ident[:]).then_inc(hid_turned, 1)

            def rows(load_no, s, slot):
                pe.wait_ge(hidT_ready, s * 2 + 3)
                pe.wait_ge(ys_ready, s * 2 + 1)
                for n in range(4):
                    if n % 2 == 0:
                        pe.wait_ge(w2_loaded[slot][n // 2], load_no * 32 + 32)
                    for f in range(FC):
                        for b in range(2):
                            last = pe.matmul(ps[b * SLOTS:(b + 1) * SLOTS, 2 + n],
                                             hidT[:, b, f * SLOTS:(f + 1) * SLOTS],
                                             w2s[slot][b][:, f, n * 512:(n + 1) * 512],
                                             start=f == 0, stop=f == FC - 1)
                    if n % 2 == 1:
                        last.then_inc(y_summed, 1)

            def scatter(s, groups):
                for g in groups:
                    if g % 4 == 0:
                        pe.wait_ge(ys_ready, s * 2 + (g // 4 + 2))
                        pe.wait_ge(mixT_ready, s + 2)
                    pe.wait_ge(added, s * GROUPS_OUT + max(1, g))
                    t, n = group_place(g)
                    pe.matmul(ps[:, 6 + g % 2], mixT[:, t * P:(t + 1) * P],
                              ys[:, n * 512:(n + 1) * 512], start=True, stop=True).then_inc(scattered, 1)

            def experts(chunks):
                if chunks > 1:
                    with pe.Fori(0, EXPERTS // 4) as j:
                        for slot in range(2):
                            i = j * 2 + slot
                            with pe.Fori(0, chunks) as c:
                                s = i * chunks + c
                                for b in range(2):
                                    hidden(i, s, b)
                                    turn(s, b)
                                rows(j, s, slot)
                                scatter(s, range(GROUPS_OUT))
                    return
                for b in range(2):
                    hidden(0, 0, b)
                    turn(0, b)
                rows(0, 0, 0)

                def pair(i, load_no, slot):
                    hidden(i, i, 0)
                    scatter(i - 1, (0, 1, 2))
                    turn(i, 0)
                    hidden(i, i, 1)
                    scatter(i - 1, (3, 4, 5))
                    turn(i, 1)
                    scatter(i - 1, (6, 7))
                    rows(load_no, i, slot)

                with pe.Fori(0, EXPERTS // 4 - 1) as j:
                    pair(j * 2 + 1, j, 1)
                    pair(j * 2 + 2, j + 1, 0)
                pair(EXPERTS // 2 - 1, EXPERTS // 4 - 1, 1)
                scatter(EXPERTS // 2 - 1, range(GROUPS_OUT))

            by_most(pe, experts)

        @block.vector
        def _(dve):
            steps = Steps(dve, dve_s)

            def split_half(q, half_no):
                dve.wait_ge(rounded, half_no + 1)
                dve.tensor_tensor(wsplit[:, q % 2, :, 1], wraw[:, q % RAW], wsplit[:, q % 2, :, 0].bitcast(F32),
                                  ALU.subtract).then_inc(split, 1)

            def split_one(unit, q, i):
                split_half(q, i * PAIR_HALVES + (2 * unit + q))

            def sum_halves(outs, banks):
                for o, bank in zip(outs, banks):
                    last = dve.tensor_reduce(o, halves_sum(bank), AX.X, ALU.add)
                last.then_inc(acc_free, 1)

            def rms(col, out_col, n, turn):
                dve.tensor_scalar(stat[:, out_col:out_col + n], stat[:, col:col + n], 1.0 / D, RMS_EPS,
                                  ALU.mult, ALU.add).then_inc(root_go, 1)
                dve.wait_ge(root_done, turn)

            dve.wait_ge(consts, 1)
            dve.memset(rev[:, T:REV], MASKED)
            dve.memset(pre[:, :, 0:CONV - 1], 0.0)
            dve.wait_ge(squares, TT)
            rms(0, 2, TT, 1)
            for t in range(TT):
                dve.tensor_scalar(diag[:, t], ident[:], stat[:, 2 + t:3 + t], None, ALU.mult).then_inc(normed, 1)
            dve.wait_ge(param_turned, 1)
            dve.tensor_copy(params[:], ps[:, 7, 0:PARAM_ROWS]).then_inc(param_ready, 1)
            dve.wait_ge(rev_summed, 1)
            dve.tensor_copy(rev[:, 0:T], ps[0:A_HEADS, 6, 0:T]).then_inc(rev_ready, 1)
            dve.wait_ge(wif_hi, 1)
            dve.tensor_tensor(wif[:, :, 1], wif_raw[:], wif[:, :, 0].bitcast(F32), ALU.subtract).then_inc(wif_ready, 1)
            dve.wait_ge(param_ready, 1)
            for c in range(DC):
                if c % HALF_K == 0:
                    split_half(c // HALF_K, c // HALF_K)
                dve.wait_ge(hi_ready, c // 2 * 2 + 2)
                dve.scalar_tensor_tensor(act_split[:, c, 1], ps[:, c // 2, (c % 2) * T:(c % 2 + 1) * T],
                                         params[:, G1_ROW + c:G1_ROW + c + 1], act_split[:, c, 0].bitcast(F32),
                                         ALU.mult, ALU.subtract).then_inc(bank_free, 1)

            def silu_conv(i, u):
                dve.wait_ge(conv_sig, i * 2 + (u + 1))
                to = (i % 2) * 8 + (i // 2) * 2 + 4 * u
                dve.tensor_tensor(qk[:, ds(to, 2)], conv[:, u], csig[:], ALU.mult).then_inc(silu_done, 1)

            def conv_pair(i, steps):
                for u in range(2):
                    n = i * 2 + u
                    split_one(0, 2 * u + 3, i)
                    dve.wait_ge(used, i * PAIR_HALVES + (2 * u + 2))
                    if not first_unit(i, u):
                        dve.wait_ge(conv_ready, n)
                    sum_halves([pre[:, b, CONV - 1:] for b in range(2)], [ps[:, 2 * u + b] for b in range(2)])
                    if not last_unit(i, u):
                        split_one(0, 2 * u + 4, i)
                    if not first_unit(i, u):
                        silu_conv(*((i, 0) if u == 1 else (i - 1, 1)))
                    dve.wait_ge(first_tap, n + 1)
                    dve.wait_ge(acc_free, n + 1)
                    for j in range(1, CONV):
                        for b in range(2):
                            tap = params[:, ds(i * 4 + (CONV_ROW + j * DC + 2 * u + b), 1)]
                            last = dve.scalar_tensor_tensor(conv[:, u, b], pre[:, b, j:j + T], tap, conv[:, u, b],
                                                            ALU.mult, ALU.add)
                        if j < CONV - 1:
                            steps.done(last)
                    last.then_inc(conv_ready, 1)

            split_one(0, 2, 0)
            conv_pair(0, steps)
            with steps.loop(1, UNITS_QK // 2 - 1, 2 * (CONV - 2)) as i:
                conv_pair(i, steps)
            conv_pair(UNITS_QK // 2 - 1, steps)
            silu_conv(UNITS_QK // 2 - 1, 1)

            def qka_pair(i):
                for u in range(2):
                    split_one(UNIT_QKA, 2 * u + 2, i)
                    dve.wait_ge(used, i * PAIR_HALVES + (2 * UNIT_QKA + 2 * u + 2))
                    sum_halves([qk[:, ds((i % 2) * 8 + i // 2 + (16 + 4 * u + 2 * b), 1)].rearrange("p a t -> p (a t)")
                                for b in range(2)],
                               [ps[:, 2 * u + b] for b in range(2)])
                    split_one(UNIT_QKA, 2 * u + 3, i)

            dve.wait_ge(if_products, 1)
            dve.tensor_copy(if_parts[:], ps[0:4 * M_HEADS, 4])
            dve.tensor_tensor(fold[:], ident[0:4 * M_HEADS, 0:2 * M_HEADS], ident[0:4 * M_HEADS, 2 * M_HEADS:4 * M_HEADS],
                              ALU.add).then_inc(if_copied, 1)
            qka_pair(0)
            dve.wait_ge(if_summed, 1)
            steps.done(dve.tensor_tensor(ifg[:], ps[:, 5, 0:TT * 2 * M_HEADS].rearrange("p (t n) -> p t n", t=TT),
                                         ifb[:].unsqueeze(1).to_broadcast([P, TT, 2 * M_HEADS]), ALU.add))
            dve.scalar_tensor_tensor(lsg[:], ifg[:, :, M_HEADS:], -1.0, ifg[:, :, M_HEADS:], ALU.mult,
                                     ALU.max).then_inc(absf_ready, 1)
            dve.tensor_scalar(lst[:], ifg[:, :, M_HEADS:], 0.0, None, ALU.min)
            dve.wait_ge(expf_ready, 1)
            dve.tensor_scalar(lsg[:], lsg[:], 1.0, None, ALU.add).then_inc(onef_ready, 1)
            dve.wait_ge(lnf_ready, 1)
            dve.tensor_tensor(lst[:], lst[:], lsg[:], ALU.subtract).then_inc(ls_ready, 1)

            with dve.Fori(1, UNITS_QKA // 2) as i:
                qka_pair(i)

            dve.wait_ge(cum_summed, 1)
            steps.done(dve.tensor_copy(cum[:], ps[:, 5, 0:8].rearrange("p (t h) -> p t h", t=TT)))
            dve.tensor_tensor(aa[:], ifg[:, :, 0:M_HEADS], cum[:], ALU.subtract).then_inc(aa_ready, 1)

            tok_f = tok[:].rearrange("p k t n -> p (k t n)")

            def token_unit(unit, i, u, start):
                split_one(unit, 2 * u + 2, i)
                dve.wait_ge(used, i * PAIR_HALVES + (2 * unit + 2 * u + 2))
                sum_halves([tok_f[:, ds(start + (t * M_WIDTH + u * UNIT), UNIT)] for t in range(TT)],
                           [ps[:, 2 * u + t] for t in range(TT)])
                split_one(unit, 2 * u + 3, i)

            def vo_pair(i):
                for u in range(2):
                    token_unit(UNIT_VO, i, u, (i // 2) * (TT * M_WIDTH) + (i % 2) * (2 * UNIT))

            with dve.Fori(0, UNITS_VO // 2 - 1) as i:
                vo_pair(i)
            dve.wait_ge(aa_turned, 1)
            dve.tensor_copy(aaT[:], ps[0:M_HEADS, 6, 0:T]).then_inc(aaT_ready, 1)
            vo_pair(UNITS_VO // 2 - 1)
            token_unit(UNIT_VA, 0, 0, 2 * TT * M_WIDTH)

            dve.wait_ge(aa_spread, 1)
            mask_2 = mask_ts[:].unsqueeze(1).to_broadcast([P, 2, P])
            for n in range(2):
                token_unit(UNIT_VA, n, 1 - n, n * 2 * UNIT + 2 * TT * M_WIDTH)
                rows = ps[:, 4 + n].rearrange("p (h s) -> p h s", h=2)
                dve.tensor_tensor(prob[:, :, 0:P], rows[:, :, 0:P], mask_2, ALU.add)
                steps.done(dve.tensor_tensor(prob[:, :, P:T], rows[:, :, P:T], mask_2, ALU.add))
                dve.tensor_reduce(negM[:, 0, 2 * n:2 * n + 2], prob[:, :, 0:P], AX.X, ALU.max)
                dve.tensor_reduce(negM[:, 1, 2 * n:2 * n + 2], prob[:, :, P:T], AX.X, ALU.max)
                steps.done(dve.tensor_reduce(stat[:, 50:52], rows[:, :, 0:P], AX.X, ALU.max))
                steps.done(dve.tensor_tensor(negM[:, 1, 2 * n:2 * n + 2], negM[:, 1, 2 * n:2 * n + 2], stat[:, 50:52], ALU.max))
            dve.tensor_scalar(negM[:], negM[:], 0.0, -1.0, ALU.max, ALU.mult).then_inc(negM_ready, 1)
            dve.wait_ge(negM_ready, 1)
            dve.tensor_tensor(expm[:], cum[:], negM[:], ALU.subtract).then_inc(mt_ready, 1)
            token_unit(UNIT_VA, 1, 1, 2 * UNIT + 2 * TT * M_WIDTH)
            dve.wait_ge(negM_turned, 1)
            dve.tensor_copy(negMT[:], ps[0:M_HEADS, 7, 0:T]).then_inc(negMT_ready, 1)
            dve.wait_ge(expm_ready, 1)
            dve.wait_ge(o_ready, 1)

            with steps.loop(0, M_HEADS, 9) as i:
                def ahead(q):
                    split_half(q, i * 8 + (2 * UNIT_GATES + q))

                def gate_sums(n):
                    dve.wait_ge(used, i * 8 + (2 * UNIT_GATES + 2 * n + 2))
                    sum_halves([gates[:, ds(i * 8 + (2 * n + b), 1)].rearrange("p a t -> p (a t)") for b in range(2)],
                               [ps[:, 2 * (n % 2) + b] for b in range(2)])

                ahead(2)
                dve.wait_ge(scores, i + 1)
                dve.scalar_tensor_tensor(decay[:, 0:P], ps[:, 7, 0:P], aa[:, 0, ds(i, 1)], mask_st[:], ALU.add, ALU.add)
                dve.tensor_scalar(decay[:, P:T], ps[:, 7, P:T], aa[:, 0, ds(i, 1)], None, ALU.add)
                dve.scalar_tensor_tensor(decay[:, T:REV], ps[:, 7, P:T], aa[:, 1, ds(i, 1)], mask_st[:],
                                         ALU.add, ALU.add).then_inc(decay_arg, 1)
                for a in range(2):
                    dve.wait_ge(logits, i * 2 + (a + 1))
                    dve.tensor_reduce(stat[:, 8 + 2 * a:9 + 2 * a], ps[:, 4 + a, 0:P], AX.X, ALU.max, negate=True)
                    dve.tensor_reduce(stat[:, 9 + 2 * a:10 + 2 * a], ps[:, 4 + a, P:REV], AX.X, ALU.max,
                                      negate=True).then_inc(negmax, 1)
                gate_sums(0)
                ahead(3)
                dve.wait_ge(decay_exp, i + 1)
                dve.scalar_tensor_tensor(scored[:], ps[:, 6, 0:REV], float(M_DIM) ** -0.5, decay[:],
                                         ALU.mult, ALU.mult).then_inc(scored_ready, 1)
                dve.wait_ge(prob_exp, i * 2 + 2)
                steps.done(dve.reciprocal(stat[:, 16:20], stat[:, 12:16]))
                for a in range(2):
                    dve.tensor_scalar(prob[:, a, 0:P], prob[:, a, 0:P], stat[:, 16 + 2 * a:17 + 2 * a], None, ALU.mult)
                    dve.tensor_scalar(prob[:, a, P:REV], prob[:, a, P:REV], stat[:, 17 + 2 * a:18 + 2 * a], None,
                                      ALU.mult).then_inc(prob_ready, 1)
                ahead(4)
                gate_sums(1)
                ahead(5)
                for a in range(2):
                    dve.wait_ge(prob_turned, i * 2 + (a + 1))
                    dve.tensor_copy(probT[:, a], ps[:, 4 + a, 0:REV]).then_inc(probT_ready, 1)
                dve.wait_ge(num_summed, i + 1)
                for t in range(TT):
                    last = dve.tensor_scalar(stat[:, 32 + t:33 + t], ps[:, 6 + t, M_DIM:M_DIM + 1], -1.0,
                                             expm[:, t, ds(i, 1)], ALU.mult, ALU.max)
                steps.done(last)
                for t in range(TT):
                    last = dve.tensor_tensor(stat[:, 32 + t:33 + t], stat[:, 32 + t:33 + t],
                                             ps[:, 6 + t, M_DIM:M_DIM + 1], ALU.max)
                steps.done(last)
                steps.done(dve.reciprocal(stat[:, 34:36], stat[:, 32:34]))
                for t in range(TT):
                    last = dve.tensor_scalar(hm[:, t], ps[:, 6 + t, 0:M_DIM], stat[:, 34 + t:35 + t], None, ALU.mult)
                steps.done(last)
                for t in range(TT):
                    last = dve.bn_stats(bn[:, t], hm[:, t])
                steps.done(last)
                dve.tensor_tensor(mean_var[:, :, 0], bn[:, :, 1], bn[:, :, 4], ALU.add)
                dve.tensor_tensor(stat[:, 52:54], bn[:, :, 1], bn[:, :, 4], ALU.subtract)
                steps.done(dve.tensor_tensor(mean_var[:, :, 1], bn[:, :, 2], bn[:, :, 5], ALU.add))
                dve.tensor_scalar(mean_var[:, :, 0], mean_var[:, :, 0], 0.5, None, ALU.mult)
                dve.tensor_scalar(mean_var[:, :, 1], mean_var[:, :, 1], 1.0 / M_DIM, LN_EPS, ALU.mult, ALU.add)
                steps.done(dve.tensor_tensor(stat[:, 52:54], stat[:, 52:54], stat[:, 52:54], ALU.mult))
                dve.scalar_tensor_tensor(stat[:, 36:38], stat[:, 52:54], 0.25, mean_var[:, :, 1], ALU.mult,
                                         ALU.add).then_inc(root_go, 1)
                dve.wait_ge(root_done, i + 2)
                for t in range(TT):
                    last = dve.tensor_scalar(hm[:, t], hm[:, t], mean_var[:, t, 0:1], stat[:, 36 + t:37 + t],
                                             ALU.subtract, ALU.mult)
                steps.done(last)
                dve.tensor_tensor(hm[:], hm[:], tok[:, 1, :, ds(i * M_DIM, M_DIM)], ALU.mult).then_inc(hm_ready, 1)
                ahead(6)
                gate_sums(2)
                ahead(7)
                for a in range(2):
                    dve.wait_ge(br_hi, i * 4 + (a + 1))
                    to = br_split[:, ds(i * 2 + (8 + a), 1)]
                    dve.tensor_tensor(to[:, 0, 1], ps[:, 4 + a, 0:T], to[:, 0, 0].bitcast(F32), ALU.subtract)
                for c in range(2):
                    dve.wait_ge(br_hi, i * 4 + 4)
                    to = br_split[:, ds(i * 2 + c, 1)]
                    last = dve.scalar_tensor_tensor(to[:, 0, 1], ps[:, 6, c * T:(c + 1) * T],
                                                    params[:, ds(i * 2 + (MN_ROW + c), 1)], to[:, 0, 0].bitcast(F32),
                                                    ALU.mult, ALU.subtract)
                last.then_inc(br_lo, 1)
                ahead(8)
                gate_sums(3)
                ahead(9)

            gates_v = gates[:].rearrange("p (g c) t -> p g c t", g=2)
            split_one(UNIT_BRANCH, 2, 0)

            def y_split(n):
                dve.wait_ge(y_hi, n + 1)
                to = act_split[:, ds(n * 2, 2)]
                dve.tensor_tensor(to[:, :, 1], bsum[:, 0], to[:, :, 0].bitcast(F32), ALU.subtract).then_inc(y_ready, 1)

            def branch_pair(i):
                for u in range(2):
                    split_one(UNIT_BRANCH, 2 * u + 3, i)
                    if not first_unit(i, u):
                        y_split(i * 2 + (u - 1))
                    dve.wait_ge(used, i * PAIR_HALVES + (2 * UNIT_BRANCH + 2 * u + 2))
                    dve.wait_ge(y_ready, i * 2 + (u + 1))
                    sum_halves([bsum[:, g, b] for g in range(2) for b in range(2)],
                               [ps[:, 4 * (1 - u) + 2 * g + b] for g in range(2) for b in range(2)])
                    dve.wait_ge(acc_free, i * 2 + (UNIT_BRANCH + u + 1))
                    if not last_unit(i, u):
                        split_one(UNIT_BRANCH, 2 * u + 4, i)
                    dve.wait_ge(gate_sig, M_HEADS)
                    steps.done(dve.tensor_tensor(bsum[:], bsum[:], gates_v[:, :, ds(i * 4 + 2 * u, 2)], ALU.mult))
                    dve.tensor_tensor(bsum[:, 0], bsum[:, 0], bsum[:, 1], ALU.add).then_inc(y_sum, 1)

            branch_pair(0)
            with steps.loop(1, UNITS_BRANCH // 2 - 1, 2) as i:
                branch_pair(i)
            branch_pair(UNITS_BRANCH // 2 - 1)
            y_split(UNITS_BRANCH - 1)
            split_one(UNIT_OUT, 2, 0)

            dve.wait_ge(moe_par, 16 * 4)
            n_r = GROUPS + EXPERTS
            dve.tensor_tensor(wrt[:], wrt[:], params[:, G2_ROW:].unsqueeze(2).to_broadcast([P, DC, n_r]),
                              ALU.mult).then_inc(wrt_ready, 1)
            dve.wait_ge(x2_loaded, 16)

            def out_sums(i, u, then_split=None):
                n = i * 2 + u
                if isinstance(i, int) and i == 0:
                    dve.wait_ge(used, 2 * UNIT_OUT + u + 3)
                else:
                    dve.wait_ge(used, i * PAIR_HALVES + (2 * UNIT_OUT + 2 * u + 2))
                dve.wait_ge(x2_ready, n + 1)
                sum_halves([osum[:, t] for t in range(TT)], [ps[:, 4 + 2 * u + t] for t in range(TT)])
                if then_split:
                    split_one(UNIT_OUT, then_split, i)
                dve.wait_ge(acc_free, n + (UNIT_OUT + 1))
                if not (isinstance(i, int) and i == 0):
                    dve.wait_ge(x2T_ready, n - 1)
                dve.tensor_tensor(x2u[:, u], x2[:, :, ds(i * (2 * UNIT) + u * UNIT, UNIT)], osum[:],
                                  ALU.add).then_inc(x2_ready, 1)

            def out_pair(i):
                for u in range(2):
                    if isinstance(i, int):
                        split_one(UNIT_OUT, 2 * u + 3, i)
                        split_one(UNIT_OUT, 2 * u + 4, i)
                        out_sums(i, u)
                    else:
                        out_sums(i, u, 2 * u + 3)
                        split_one(UNIT_OUT, 2 * u + 4, i)

            out_pair(0)
            with dve.Fori(1, UNITS_OUT // 2 - 1) as i:
                out_pair(i)
            split_half(3, HALVES - 1)
            out_sums(UNITS_OUT // 2 - 1, 0)
            out_sums(UNITS_OUT // 2 - 1, 1)

            dve.wait_ge(squares2, UNITS_OUT)
            steps.done(dve.tensor_reduce(stat[:, 20:22], sq2[:], AX.X, ALU.add))
            dve.tensor_copy(ones_r[:], ones[:])
            dve.tensor_copy(before_r[:], before[:])
            rms(20, 22, TT, M_HEADS + 2)

            GMAX, GNEG, GSUM, EMAX, E2MAX, E_DIFF, E_EXP, FIRST, W_1, W_2 = range(10)

            def by_token(row, n):
                return sc[:, row].unsqueeze(2).to_broadcast([P, TT, n])

            def first_of(chosen, values, top, n):
                iota_n = iota_e[:, 0:n].unsqueeze(1).to_broadcast([P, TT, n])
                for t in range(TT):
                    last = dve.scalar_tensor_tensor(rt[:, 1, t, 0:n], values[:, t], sc[:, top, t:t + 1], iota_e[:, 0:n],
                                                    ALU.is_ge, ALU.mult)
                steps.done(last)
                steps.done(dve.tensor_reduce(sc[:, FIRST], rt[:, 1, :, 0:n], AX.X, ALU.min))
                steps.done(dve.tensor_tensor(chosen, iota_n, by_token(FIRST, n), ALU.is_equal))

            dve.wait_ge(routed, 1)
            dve.wait_ge(iotas, 1)
            unit_sums = rt[:].rearrange("p a t e -> p (a t e)")[:, 0:2 * TT * n_r].rearrange("p (u t n) -> p u t n", u=2, t=TT)
            for u in range(2):
                last = dve.tensor_reduce(
                    unit_sums[:, u].rearrange("p t n -> p (t n)"),
                    ps[:, 2 + u, 0:UNITS_OUT // 2 * TT * n_r].rearrange("p (i n) -> p n i", n=TT * n_r), AX.X, ALU.add)
            steps.done(last)
            for u in range(2):
                for t in range(TT):
                    last = dve.scalar_tensor_tensor(lr[:, t], unit_sums[:, u, t], stat[:, 22 + t:23 + t],
                                                    (brt[:], lr[:, t])[u], ALU.mult, ALU.add)
                steps.done(last)
            g_log, e_log = lr[:, :, 0:GROUPS], lr[:, :, GROUPS:]
            steps.done(dve.tensor_reduce(sc[:, GMAX], g_log, AX.X, ALU.max))
            dve.tensor_scalar(sc[:, GNEG], sc[:, GMAX], -1.0, None, ALU.mult).then_inc(gexp_go, 1)
            first_of(rt[:, 2, :, 0:GROUPS], g_log, GMAX, GROUPS)
            steps.done(dve.tensor_scalar(rt[:, 2, :, 0:GROUPS], rt[:, 2, :, 0:GROUPS], -MASKED, MASKED, ALU.mult, ALU.add))
            for t in range(TT):
                last = dve.tensor_tensor(rt[:, 0, t].rearrange("p (g e) -> p g e", g=GROUPS),
                                         e_log[:, t].rearrange("p (g e) -> p g e", g=GROUPS),
                                         rt[:, 2, t, 0:GROUPS].unsqueeze(2).to_broadcast([P, GROUPS, PER_GROUP]), ALU.add)
            steps.done(last)
            steps.done(dve.tensor_reduce(sc[:, EMAX], rt[:, 0], AX.X, ALU.max))
            first_of(oh[:, :, 0], rt[:, 0], EMAX, EXPERTS)
            iota_t = iota_e[:].unsqueeze(1).to_broadcast([P, TT, EXPERTS])
            dve.tensor_tensor(rt[:, 3], iota_t, by_token(FIRST, EXPERTS), ALU.is_gt)
            steps.done(dve.scalar_tensor_tensor(rt[:, 0], oh[:, :, 0], 2 * MASKED, rt[:, 0], ALU.mult, ALU.add))
            steps.done(dve.tensor_reduce(sc[:, E2MAX], rt[:, 0], AX.X, ALU.max))
            dve.tensor_tensor(sc[:, E_DIFF], sc[:, E2MAX], sc[:, EMAX], ALU.subtract).then_inc(gexp_go, 1)
            first_of(oh[:, :, 1], rt[:, 0], E2MAX, EXPERTS)
            dve.tensor_tensor(mk[:, :, 0], oh[:, :, 0], oh[:, :, 1], ALU.add)
            steps.done(dve.tensor_tensor(rt[:, 1], iota_t, by_token(FIRST, EXPERTS), ALU.is_gt))
            dve.tensor_tensor(mk[:, :, 1], rt[:, 3], rt[:, 1], ALU.add).then_inc(mk_ready, 1)
            dve.wait_ge(h2hi_ready, TT)
            cols = slice(D // 2, D)
            dve.tensor_tensor(h2lo[:, 1, cols], h2n[:, 1, cols], h2hi[:, 1, cols].bitcast(F32), ALU.subtract)
            dve.wait_ge(rank_summed, 1)
            dve.tensor_copy(table[:], ps[:, 1, 64:128].rearrange("p (k e) -> p k e", k=2))
            steps.done(dve.tensor_copy(rank[:], ps[:, 1, 0:64].rearrange("p (t e) -> p t e", t=TT)))
            steps.done(dve.tensor_tensor(pos[:], rank[:], table[:, 1:2].to_broadcast([P, TT, EXPERTS]), ALU.add))
            for k in range(2):
                last = dve.tensor_tensor(rt[:, k], oh[:, :, k], pos[:], ALU.mult)
            steps.done(last)
            steps.done(dve.tensor_reduce(stat[:, 44:48], rt[:, 0:2].rearrange("p k t e -> p (k t) e"), AX.X, ALU.add))
            for t in range(TT):
                last = dve.tensor_scalar(sel[:, t], iota_s[:], stat[:, 44 + t:45 + t], None, ALU.is_equal)
            steps.done(last)
            for t in range(TT):
                last = dve.scalar_tensor_tensor(sel[:, t], iota_s[:], stat[:, 46 + t:47 + t], sel[:, t].bitcast(F32),
                                                ALU.is_equal, ALU.add)
            last.then_inc(sel_ready, 1)
            dve.wait_ge(gexp_done, 2)
            steps.done(dve.tensor_scalar(sc[:, W_1], sc[:, E_EXP], 1.0, None, ALU.add))
            steps.done(dve.tensor_tensor(sc[:, W_1], sc[:, W_1], sc[:, GSUM], ALU.mult))
            steps.done(dve.reciprocal(sc[:, W_1], sc[:, W_1]))
            steps.done(dve.tensor_tensor(sc[:, W_2], sc[:, W_1], sc[:, E_EXP], ALU.mult))
            steps.done(dve.tensor_tensor(wt[:], oh[:, :, 0], by_token(W_1, EXPERTS), ALU.mult))
            steps.done(dve.tensor_tensor(rt[:, 3], oh[:, :, 1], by_token(W_2, EXPERTS), ALU.mult))
            dve.tensor_tensor(wt[:], wt[:], rt[:, 3], ALU.add)
            dve.tensor_reduce(stat[:, 35:36], table[:, 0], AX.X, ALU.max)
            for c in range(CHUNKS):
                last = dve.tensor_scalar(starts[:, :, c], table[:, 1], float(c * SLOTS), float(PAIRS), ALU.add, ALU.min)
            steps.done(last)
            dve.tensor_copy(starts_i[:], starts[0:1])
            dve.tensor_copy(most_i[:], stat[0:1, 35:36]).then_inc(tab_ready, 1)
            dve.memset(xg[:, :, PAIRS:], 0.0)

            def gathered():
                for c in range(1, DC, 2):
                    dve.wait_ge(xg_summed, c + 1)
                    dve.tensor_scalar(xg[:, c, 0:PAIRS], ps[:, c % 8], g2T[:, c:c + 1], None, ALU.mult).then_inc(xg_dve, 1)
                dve.wait_ge(xg_act, DC // 2)
                dve.wait_ge(xg_dve, DC // 2)

            steps_x = Steps(dve, dve_x)

            def tokens_in(i, c, s, before_copies=None):
                starts_at = [dve.value_load(starts_i[0:1, ds(i * 2 + b, 1), ds(c, 1)], min_val=0, max_val=PAIRS)
                             for b in range(2)]
                if before_copies:
                    before_copies()
                dve.wait_ge(h_summed, s * 2 + 1)
                for b, at in enumerate(starts_at):
                    dve.tensor_copy(xe[:, b], xg[:, :, ds(at, SLOTS)]).then_inc(xe_ready, 1)
                dve.wait_ge(mix_turned, s + 1)
                for b in range(2):
                    for t in range(TT):
                        last = dve.tensor_scalar(mix[:, t, b * SLOTS:(b + 1) * SLOTS],
                                                 iota_c[:, ds(c, 1)].rearrange("p c s -> p (c s)"),
                                                 rank[:, t, ds(i * 2 + b, 1)], wt[:, t, ds(i * 2 + b, 1)],
                                                 ALU.is_equal, ALU.mult)
                last.then_inc(mix_ready, 1)

            def silu(s, b):
                dve.wait_ge(sg_ready, s * 2 + (b + 1))
                dve.wait_ge(hid_turned, s * 2 + (b + 1))
                steps_x.done(dve.tensor_tensor(hid[:], sg[:], ps[:, 0, 0:P], ALU.mult))
                dve.tensor_tensor(hid[:], hid[:], ps[:, 0, P:2 * P], ALU.mult).then_inc(hid_ready, 1)

            def add(s, groups):
                for g in groups:
                    dve.wait_ge(scattered, s * GROUPS_OUT + (g + 2))
                    dve.wait_ge(added, s * GROUPS_OUT + 1)
                    t, n = group_place(g)
                    cols = x2[:, t, n * 512:(n + 1) * 512]
                    dve.tensor_tensor(cols, cols, ps[:, 6 + g % 2], ALU.add).then_inc(added, 1)

            def experts(chunks):
                steps_x.n = 0
                if chunks > 1:
                    gathered()
                    with steps_x.loop(0, EXPERTS // 2, 2 * chunks) as i:
                        with steps_x.loop(0, chunks, 2) as c:
                            s = i * chunks + c
                            tokens_in(i, c, s)
                            for b in range(2):
                                silu(s, b)
                            add(s, range(GROUPS_OUT))
                else:
                    tokens_in(0, 0, 0, before_copies=gathered)
                    for b in range(2):
                        silu(0, b)
                    with steps_x.loop(1, EXPERTS // 2, 2) as i:
                        tokens_in(i, 0, i)
                        silu(i, 0)
                        add(i - 1, (0, 1, 2))
                        silu(i, 1)
                        add(i - 1, (3, 4, 5, 6, 7))
                    for g in range(GROUPS_OUT):
                        add(EXPERTS // 2 - 1, (g,))
                        if g > 0:
                            gained(chunks, g - 1)
                if chunks > 1:
                    for g in range(GROUPS_OUT - 1):
                        gained(chunks, g)
                gained(chunks, GROUPS_OUT - 1)

            def gained(chunks, g):
                if g == 0:
                    dve.wait_ge(fing_loaded, 16)
                dve.wait_ge(added, (EXPERTS // 2 * chunks - 1) * GROUPS_OUT + g + 2)
                t, n = group_place(g)
                cols = slice(n * 512, (n + 1) * 512)
                dve.tensor_tensor(x2g[:, t, cols], x2[:, t, cols], fin_g[:, cols], ALU.mult).then_inc(x2g_ready, 1)

            by_most(dve, experts)
            dve.wait_ge(squares3, GROUPS_OUT)
            steps_f = Steps(dve, squares_total)
            steps_f.done(dve.tensor_reduce(stat[:, 40:42], sq2[:, :, 0:4], AX.X, ALU.add))
            rms(40, 42, TT, M_HEADS + 3)
            dve.wait_ge(x2g_ready, GROUPS_OUT)
            for h in range(2):
                cols = slice(h * (D // 2), (h + 1) * (D // 2))
                dve.tensor_scalar(fin[:, 1, cols], x2g[:, 1, cols], stat[:, 43:44], None, ALU.mult).then_inc(out_ready[1], 1)


_INS = ["x", "norm1_g", "w_in", "conv_w", "if_bias", "mnorm_g", "w_branch_m", "w_branch_a", "w_out", "rel_bias",
        "norm2_g", "w_grp", "b_grp", "w_exp", "b_exp", "w1", "w3", "w2", "final_g"]


def kernel(**inputs):
    import numpy as _np
    import concourse.bacc as _bacc
    from concourse import mybir as _mybir
    from concourse.bass_utils import run_bass_kernel_spmd as _run

    nc = _bacc.Bacc("TRN2", target_bir_lowering=False, num_devices=1, dynamic_dma_scratch_size=1024)
    arrays, args = {}, []
    for name in _INS + ["onehot"]:
        a = _np.ascontiguousarray(bucket_onehot() if name == "onehot" else inputs[name])
        if name not in ("rel_bias", "final_g", "onehot"):
            a = a.reshape(a.shape[1:])
        arrays[f"in_{name}_dram"] = a
        args.append(nc.dram_tensor(f"in_{name}_dram", a.shape, _mybir.dt.from_np(a.dtype), kind="ExternalInput").ap())
    args.append(nc.dram_tensor("out_0_dram", (T, D), F32, kind="ExternalOutput").ap())
    layer(nc, *args)
    r = _run(nc, [arrays], core_ids=[0])
    return r.results[0]["out_0_dram"].reshape(1, T, D)
```
